# Optimizing a Trainium2 kernel written in Bass

```python
import jax, jax.numpy as jnp
from jax import lax
import numpy as np

D_MODEL = 1024
BATCH = 1
SEQ = 256
DEPTH = 1

D_POOL = D_MODEL // 2
POOL_WINDOWS = (2, 4, 8, 16)
N_POOL_GROUPS = len(POOL_WINDOWS)
POOL_GROUP_DIM = D_POOL // N_POOL_GROUPS
V_HEAD_DIM = 64
N_HEADS = (D_MODEL // 2) // V_HEAD_DIM
D_ATTN = N_HEADS * V_HEAD_DIM
D_MIX = D_POOL + D_ATTN
QK_NOPE_DIM = 64
QK_ROPE_DIM = 32
QK_DIM = QK_NOPE_DIM + QK_ROPE_DIM
Q_LORA_RANK = D_MODEL // 4
KV_LORA_RANK = D_MODEL // 8
ROPE_THETA = 10000.0
Q_BLOCK = 128
D_IN_PROJ = D_POOL + Q_LORA_RANK + KV_LORA_RANK + QK_ROPE_DIM
N_EXPERTS = 32
TOP_K = 4
D_EXPERT = D_MODEL
SWIGLU_ALPHA = 1.702
SWIGLU_LIMIT = 7.0
MOE_BLOCK = 128
RMS_EPS = 1e-6


def rmsnorm(x, g):
    xf = x.astype(jnp.float32)
    y = xf * lax.rsqrt(jnp.mean(xf * xf, axis=-1, keepdims=True) + RMS_EPS)
    return (y * g.astype(jnp.float32)).astype(x.dtype)

def rope_tables(positions):
    half = QK_ROPE_DIM // 2
    inv = ROPE_THETA ** (-jnp.arange(half, dtype=jnp.float32) / half)
    ang = positions.astype(jnp.float32)[..., None] * inv
    return jnp.cos(ang), jnp.sin(ang)

def apply_rope(x, cos, sin):
    half = QK_ROPE_DIM // 2
    xf = x.astype(jnp.float32)
    x1, x2 = xf[..., :half], xf[..., half:]
    out = jnp.concatenate([x1 * cos - x2 * sin, x2 * cos + x1 * sin], axis=-1)
    return out.astype(x.dtype)

def pool_mixer(u, w_pool, b_pool, pool_scale):
    B, S, _ = u.shape
    uf = u.reshape(B, S, N_POOL_GROUPS, POOL_GROUP_DIM).astype(jnp.float32)
    csum = jnp.pad(jnp.cumsum(uf, axis=1), ((0, 0), (1, 0), (0, 0), (0, 0)))
    t = jnp.arange(S)
    pooled = []
    for g, w in enumerate(POOL_WINDOWS):
        c = csum[:, :, g]
        lo = jnp.pad(c[:, :S + 1 - w], ((0, 0), (w - 1, 0), (0, 0)))
        cnt = jnp.minimum(t + 1, w).astype(jnp.float32)[None, :, None]
        pooled.append((c[:, 1:] - lo) / cnt)
    pooled = jnp.stack(pooled, axis=2)
    diff = (pooled - uf).astype(u.dtype)
    mixed = jnp.einsum('bsgc,gcd->bsgd', diff, w_pool) + b_pool
    return mixed.reshape(B, S, D_POOL) * pool_scale

def mla_attention(q_lat, kv_lat, k_rope_raw, cos, sin, g_q_a, w_q_b, g_kv_a, w_kv_b):
    B, S, _ = q_lat.shape
    q = (rmsnorm(q_lat, g_q_a) @ w_q_b).reshape(B, S, N_HEADS, QK_DIM)
    q_nope = q[..., :QK_NOPE_DIM]
    q_rope = apply_rope(q[..., QK_NOPE_DIM:], cos[:, :, None, :], sin[:, :, None, :])
    kv = (rmsnorm(kv_lat, g_kv_a) @ w_kv_b).reshape(B, S, N_HEADS, QK_NOPE_DIM + V_HEAD_DIM)
    k_nope, v = kv[..., :QK_NOPE_DIM], kv[..., QK_NOPE_DIM:]
    k_rope = apply_rope(k_rope_raw, cos, sin)
    scale = QK_DIM ** -0.5
    nb = S // Q_BLOCK
    qn_b = q_nope.reshape(B, nb, Q_BLOCK, N_HEADS, QK_NOPE_DIM).transpose(1, 0, 2, 3, 4)
    qr_b = q_rope.reshape(B, nb, Q_BLOCK, N_HEADS, QK_ROPE_DIM).transpose(1, 0, 2, 3, 4)
    k_idx = jnp.arange(S)

    def attend(args):
        qn, qr, blk = args
        s = (jnp.einsum('bqhd,bkhd->bhqk', qn, k_nope, preferred_element_type=jnp.float32)
             + jnp.einsum('bqhr,bkr->bhqk', qr, k_rope, preferred_element_type=jnp.float32)) * scale
        q_idx = blk * Q_BLOCK + jnp.arange(Q_BLOCK)
        s = jnp.where(k_idx[None, :] <= q_idx[:, None], s, -jnp.inf)
        p = jax.nn.softmax(s, axis=-1).astype(v.dtype)
        return jnp.einsum('bhqk,bkhd->bqhd', p, v)

    out = lax.map(attend, (qn_b, qr_b, jnp.arange(nb)))
    return out.transpose(1, 0, 2, 3, 4).reshape(B, S, D_ATTN)

def moe(h, w_router, b_router, w_gate_up, b_gate_up, w_down, b_down):
    B, S, D = h.shape
    T = B * S
    ht = h.reshape(T, D)
    logits = (ht @ w_router + b_router).astype(jnp.float32)
    top_vals, top_idx = lax.top_k(logits, TOP_K)
    gates = jax.nn.softmax(top_vals, axis=-1)
    n_assign = T * TOP_K
    e_flat = top_idx.reshape(-1).astype(jnp.int32)
    tok_flat = jnp.repeat(jnp.arange(T, dtype=jnp.int32), TOP_K)
    g_flat = gates.reshape(-1)
    order = jnp.argsort(e_flat)
    e_sorted = e_flat[order]
    counts = jnp.zeros((N_EXPERTS,), jnp.int32).at[e_flat].add(1)
    padded = ((counts + MOE_BLOCK - 1) // MOE_BLOCK) * MOE_BLOCK
    start = jnp.cumsum(counts) - counts
    pad_end = jnp.cumsum(padded)
    pad_start = pad_end - padded
    dest = pad_start[e_sorted] + (jnp.arange(n_assign, dtype=jnp.int32) - start[e_sorted])
    n_blocks = n_assign // MOE_BLOCK + N_EXPERTS
    n_rows = n_blocks * MOE_BLOCK
    row_tok = jnp.full((n_rows,), T, jnp.int32).at[dest].set(tok_flat[order])
    row_gate = jnp.zeros((n_rows,), jnp.float32).at[dest].set(g_flat[order])
    block_expert = jnp.minimum(
        jnp.searchsorted(pad_end, jnp.arange(n_blocks, dtype=jnp.int32) * MOE_BLOCK, side='right'),
        N_EXPERTS - 1)
    h_pad = jnp.concatenate([ht, jnp.zeros((1, D), ht.dtype)], axis=0)
    xb = h_pad[row_tok].reshape(n_blocks, MOE_BLOCK, D)

    def expert_block(args):
        xblk, e = args
        gu = xblk @ w_gate_up[e] + b_gate_up[e]
        gate = jnp.minimum(gu[:, :D_EXPERT], SWIGLU_LIMIT)
        up = jnp.clip(gu[:, D_EXPERT:], -SWIGLU_LIMIT, SWIGLU_LIMIT)
        act = gate * jax.nn.sigmoid(SWIGLU_ALPHA * gate) * (up + 1)
        return act @ w_down[e] + b_down[e]

    yb = lax.map(expert_block, (xb, block_expert)).reshape(n_rows, D)
    y = jnp.zeros((T + 1, D), h.dtype).at[row_tok].add(row_gate[:, None].astype(h.dtype) * yb)
    return y[:T].reshape(B, S, D)

def first_inputs(seed: int = 0) -> dict:
    key = jax.random.key(seed)
    ks = jax.random.split(key, 24)
    L, D, E, F = DEPTH, D_MODEL, N_EXPERTS, D_EXPERT
    nrm = lambda k, shape, fan_in: jax.random.normal(k, shape, jnp.float32) * (fan_in ** -0.5)
    gain = lambda k, shape: 1.0 + 0.05 * jax.random.normal(k, shape, jnp.float32)
    small = lambda k, shape: 0.01 * jax.random.normal(k, shape, jnp.float32)
    x = jax.random.normal(ks[0], (BATCH, SEQ, D), jnp.float32)
    positions = jnp.broadcast_to(jnp.arange(SEQ, dtype=jnp.int32), (BATCH, SEQ))
    return {
        'x': x,
        'positions': positions,
        'g_attn_norm': gain(ks[1], (L, D)),
        'w_in': nrm(ks[2], (L, D, D_IN_PROJ), D),
        'w_pool': nrm(ks[3], (L, N_POOL_GROUPS, POOL_GROUP_DIM, POOL_GROUP_DIM), POOL_GROUP_DIM),
        'b_pool': small(ks[4], (L, N_POOL_GROUPS, POOL_GROUP_DIM)),
        'pool_scale': gain(ks[5], (L, D_POOL)),
        'g_q_a': gain(ks[6], (L, Q_LORA_RANK)),
        'w_q_b': nrm(ks[7], (L, Q_LORA_RANK, N_HEADS * QK_DIM), Q_LORA_RANK),
        'g_kv_a': gain(ks[8], (L, KV_LORA_RANK)),
        'w_kv_b': nrm(ks[9], (L, KV_LORA_RANK, N_HEADS * (QK_NOPE_DIM + V_HEAD_DIM)), KV_LORA_RANK),
        'g_out_pool': gain(ks[10], (L, D_POOL)),
        'g_out_attn': gain(ks[11], (L, D_ATTN)),
        'w_out': nrm(ks[12], (L, D_MIX, D), D_MIX),
        'g_ffn_norm': gain(ks[13], (L, D)),
        'w_router': nrm(ks[14], (L, D, E), D),
        'b_router': small(ks[15], (L, E)),
        'w_gate_up': nrm(ks[16], (L, E, D, 2 * F), D),
        'b_gate_up': small(ks[17], (L, E, 2 * F)),
        'w_down': nrm(ks[18], (L, E, F, D), F),
        'b_down': small(ks[19], (L, E, D)),
        'g_final': gain(ks[20], (D,)),
    }

def first_block(x, positions, g_attn_norm, w_in, w_pool, b_pool, pool_scale, g_q_a, w_q_b,
              g_kv_a, w_kv_b, g_out_pool, g_out_attn, w_out, g_ffn_norm, w_router, b_router,
              w_gate_up, b_gate_up, w_down, b_down, g_final):
    cos, sin = rope_tables(positions)
    o1 = D_POOL
    o2 = o1 + Q_LORA_RANK
    o3 = o2 + KV_LORA_RANK
    for l in range(DEPTH):
        h = rmsnorm(x, g_attn_norm[l])
        proj = h @ w_in[l]
        u, q_lat, kv_lat, k_r = proj[..., :o1], proj[..., o1:o2], proj[..., o2:o3], proj[..., o3:]
        y_pool = pool_mixer(u, w_pool[l], b_pool[l], pool_scale[l])
        y_attn = mla_attention(q_lat, kv_lat, k_r, cos, sin, g_q_a[l], w_q_b[l], g_kv_a[l], w_kv_b[l])
        mix = jnp.concatenate([rmsnorm(y_pool, g_out_pool[l]), rmsnorm(y_attn, g_out_attn[l])], axis=-1)
        x = x + mix @ w_out[l]
        h = rmsnorm(x, g_ffn_norm[l])
        x = x + moe(h, w_router[l], b_router[l], w_gate_up[l], b_gate_up[l], w_down[l], b_down[l])
    return rmsnorm(x, g_final)


HEAD_DIM = 64
N_HEADS_2 = D_MODEL // HEAD_DIM
ML_HEADS = N_HEADS_2 // 4
FOX_HEADS = (N_HEADS_2 - ML_HEADS) // 2
MOBA_HEADS = N_HEADS_2 - ML_HEADS - FOX_HEADS
FOX_W = FOX_HEADS * HEAD_DIM
ML_W = ML_HEADS * HEAD_DIM
MOBA_W = MOBA_HEADS * HEAD_DIM
ML_CHUNK = 64
ML_CONV = 4
MOBA_BLOCK = 256
MOBA_TOPK = 3
ALIBI_MAX = 8.0
D_FF = ((8 * D_MODEL // 3 + 255) // 256) * 256
EPS = 1e-6
SPLIT_SIZES = (FOX_W, FOX_W, FOX_W, FOX_HEADS,
               ML_W, ML_W, ML_W, ML_HEADS, ML_HEADS, ML_W,
               MOBA_W, MOBA_W, MOBA_W)
IN_COLS = sum(SPLIT_SIZES)


def _rms(x, g=None):
    xf = x.astype(jnp.float32)
    y = xf * lax.rsqrt(jnp.mean(xf * xf, axis=-1, keepdims=True) + EPS)
    return y if g is None else y * g.astype(jnp.float32)

def _to_heads(x, h):
    b, t, _ = x.shape
    return x.reshape(b, t, h, HEAD_DIM).transpose(0, 2, 1, 3)

def _from_heads(x):
    b, h, t, d = x.shape
    return x.transpose(0, 2, 1, 3).reshape(b, t, h * d)

def _alibi_slopes(h):
    return jnp.exp2(-ALIBI_MAX * jnp.arange(1, h + 1, dtype=jnp.float32) / h)

def _causal_conv(x, w, bias):
    ch = x.shape[-1]
    y = lax.conv_general_dilated(x, w.astype(x.dtype)[:, None, :], window_strides=(1,),
                                 padding=((ML_CONV - 1, 0),),
                                 dimension_numbers=('NWC', 'WIO', 'NWC'),
                                 feature_group_count=ch)
    return y + bias.astype(x.dtype)

def _fox_attention(q, k, v, f_pre):
    b, h, t, d = q.shape
    nq = t // Q_BLOCK
    logf = jax.nn.log_sigmoid(f_pre).transpose(0, 2, 1)
    cum = jnp.cumsum(logf, axis=-1)
    kpos = jnp.arange(t)
    qb = q.reshape(b, h, nq, Q_BLOCK, d).transpose(2, 0, 1, 3, 4)
    cq = cum.reshape(b, h, nq, Q_BLOCK).transpose(2, 0, 1, 3)
    starts = jnp.arange(nq) * Q_BLOCK
    scale = HEAD_DIM ** -0.5

    def block(args):
        qc, cqc, st = args
        qpos = st + jnp.arange(Q_BLOCK)
        s = jnp.einsum('bhqd,bhkd->bhqk', qc, k) * scale
        s = s + (cqc[..., None] - cum[:, :, None, :])
        s = jnp.where(kpos[None, :] <= qpos[:, None], s, -jnp.inf)
        p = jax.nn.softmax(s, axis=-1)
        return jnp.einsum('bhqk,bhkd->bhqd', p, v)

    out = lax.map(block, (qb, cq, starts))
    return out.transpose(1, 2, 0, 3, 4).reshape(b, h, t, d)

def _mlstm(q, k, v, i_pre, f_pre):
    b, h, t, d = q.shape
    nc = t // ML_CHUNK
    k = k * (d ** -0.5)
    itil = i_pre.transpose(0, 2, 1).reshape(b, h, nc, ML_CHUNK)
    logf = jax.nn.log_sigmoid(f_pre).transpose(0, 2, 1).reshape(b, h, nc, ML_CHUNK)
    bcum = jnp.cumsum(logf, axis=-1)
    bend = bcum[..., -1]
    wlog = bend[..., None] - bcum + itil
    qc = q.reshape(b, h, nc, ML_CHUNK, d)
    kc = k.reshape(b, h, nc, ML_CHUNK, d)
    vc = v.reshape(b, h, nc, ML_CHUNK, d)

    def step(carry, xs):
        cmat, nvec, m = carry
        kx, vx, wx, bx = xs
        m_new = jnp.maximum(bx + m, wx.max(-1))
        decay = jnp.exp(bx + m - m_new)
        ws = jnp.exp(wx - m_new[..., None])
        c_new = decay[..., None, None] * cmat + jnp.einsum('bhs,bhsd,bhse->bhde', ws, vx, kx)
        n_new = decay[..., None] * nvec + jnp.einsum('bhs,bhse->bhe', ws, kx)
        return (c_new, n_new, m_new), (cmat, nvec, m)

    init = (jnp.zeros((b, h, d, d), jnp.float32), jnp.zeros((b, h, d), jnp.float32),
            jnp.zeros((b, h), jnp.float32))
    xs = (kc.transpose(2, 0, 1, 3, 4), vc.transpose(2, 0, 1, 3, 4),
          wlog.transpose(2, 0, 1, 3), bend.transpose(2, 0, 1))
    _, (cs, ns, ms) = lax.scan(step, init, xs)
    cs = cs.transpose(1, 2, 0, 3, 4)
    ns = ns.transpose(1, 2, 0, 3)
    ms = ms.transpose(1, 2, 0)

    causal = jnp.tril(jnp.ones((ML_CHUNK, ML_CHUNK), dtype=bool))
    logd = bcum[..., :, None] - bcum[..., None, :] + itil[..., None, :]
    logd = jnp.where(causal, logd, -jnp.inf)
    m_inter = bcum + ms[..., None]
    m_j = jnp.maximum(m_inter, logd.max(-1))
    smat = jnp.einsum('bhcjd,bhcsd->bhcjs', qc, kc) * jnp.exp(logd - m_j[..., None])
    inter = jnp.exp(m_inter - m_j)
    num = (inter[..., None] * jnp.einsum('bhcde,bhcje->bhcjd', cs, qc)
           + jnp.einsum('bhcjs,bhcsd->bhcjd', smat, vc))
    den = inter * jnp.einsum('bhce,bhcje->bhcj', ns, qc) + smat.sum(-1)
    hout = num / jnp.maximum(jnp.abs(den), jnp.exp(-m_j))[..., None]
    return hout.reshape(b, h, t, d)

def _moba_attention(q, k, v, slopes):
    b, h, t, d = q.shape
    nb = -(-t // MOBA_BLOCK)
    pad = nb * MOBA_BLOCK - t
    kb = jnp.pad(k, ((0, 0), (0, 0), (0, pad), (0, 0))).reshape(b, h, nb, MOBA_BLOCK, d)
    vb = jnp.pad(v, ((0, 0), (0, 0), (0, pad), (0, 0))).reshape(b, h, nb, MOBA_BLOCK, d)
    kmean = kb.mean(axis=3)
    qblk = jnp.arange(t) // MOBA_BLOCK
    gate = jnp.einsum('bhtd,bhnd->bhtn', q, kmean)
    gate = jnp.where(jnp.arange(nb)[None, :] < qblk[:, None], gate, -jnp.inf)
    topk = min(MOBA_TOPK, nb)
    _, sel = lax.top_k(gate, topk)
    valid = sel < qblk[:, None]
    nq = t // Q_BLOCK
    xs = (q.reshape(b, h, nq, Q_BLOCK, d).transpose(2, 0, 1, 3, 4),
          sel.reshape(b, h, nq, Q_BLOCK, topk).transpose(2, 0, 1, 3, 4),
          valid.reshape(b, h, nq, Q_BLOCK, topk).transpose(2, 0, 1, 3, 4),
          jnp.arange(nq))
    bi = jnp.arange(b)[:, None, None, None]
    hi = jnp.arange(h)[None, :, None, None]
    scale = HEAD_DIM ** -0.5
    offs = jnp.arange(MOBA_BLOCK)

    def block(args):
        qc, selc, validc, ci = args
        qpos = ci * Q_BLOCK + jnp.arange(Q_BLOCK)
        ks = kb[bi, hi, selc]
        vs = vb[bi, hi, selc]
        kpos_sel = selc[..., None] * MOBA_BLOCK + offs
        dist_sel = (qpos[:, None, None] - kpos_sel).astype(jnp.float32)
        s_sel = (jnp.einsum('bhqd,bhqkld->bhqkl', qc, ks) * scale
                 - slopes[:, None, None, None] * dist_sel)
        s_sel = jnp.where(validc[..., None], s_sel, -jnp.inf)
        own = (ci * Q_BLOCK) // MOBA_BLOCK
        ko = lax.dynamic_index_in_dim(kb, own, axis=2, keepdims=False)
        vo = lax.dynamic_index_in_dim(vb, own, axis=2, keepdims=False)
        dist_own = qpos[:, None] - (own * MOBA_BLOCK + offs)[None, :]
        s_own = (jnp.einsum('bhqd,bhld->bhql', qc, ko) * scale
                 - slopes[:, None, None] * dist_own.astype(jnp.float32))
        s_own = jnp.where(dist_own >= 0, s_own, -jnp.inf)
        s_all = jnp.concatenate([s_sel.reshape(b, h, Q_BLOCK, topk * MOBA_BLOCK), s_own], axis=-1)
        p = jax.nn.softmax(s_all, axis=-1)
        p_sel = p[..., :topk * MOBA_BLOCK].reshape(b, h, Q_BLOCK, topk, MOBA_BLOCK)
        p_own = p[..., topk * MOBA_BLOCK:]
        return (jnp.einsum('bhqkl,bhqkld->bhqd', p_sel, vs)
                + jnp.einsum('bhql,bhld->bhqd', p_own, vo))

    out = lax.map(block, xs)
    return out.transpose(1, 2, 0, 3, 4).reshape(b, h, t, d)

def _mixer(hn, w_in, fox_f_bias, fox_q_g, fox_k_g, ml_conv_w, ml_conv_b, ml_i_bias,
           ml_f_bias, ml_h_g, moba_q_g, moba_k_g):
    proj = (hn @ w_in).astype(jnp.float32)
    idx = [int(i) for i in np.cumsum(SPLIT_SIZES)[:-1]]
    fq, fk, fv, ff, mq, mk, mv, mi, mf, mo, bq, bk, bv = jnp.split(proj, idx, axis=-1)
    y_fox = _fox_attention(_rms(_to_heads(fq, FOX_HEADS), fox_q_g),
                           _rms(_to_heads(fk, FOX_HEADS), fox_k_g),
                           _to_heads(fv, FOX_HEADS),
                           ff + fox_f_bias.astype(jnp.float32))
    qk = jax.nn.silu(_causal_conv(jnp.concatenate([mq, mk], axis=-1), ml_conv_w, ml_conv_b))
    mq, mk = jnp.split(qk, 2, axis=-1)
    h_ml = _mlstm(_to_heads(mq, ML_HEADS), _to_heads(mk, ML_HEADS), _to_heads(mv, ML_HEADS),
                  mi + ml_i_bias.astype(jnp.float32), mf + ml_f_bias.astype(jnp.float32))
    y_ml = _from_heads(_rms(h_ml)) * ml_h_g.astype(jnp.float32) * jax.nn.sigmoid(mo)
    y_moba = _moba_attention(_rms(_to_heads(bq, MOBA_HEADS), moba_q_g),
                             _rms(_to_heads(bk, MOBA_HEADS), moba_k_g),
                             _to_heads(bv, MOBA_HEADS), _alibi_slopes(MOBA_HEADS))
    return jnp.concatenate([_from_heads(y_fox), y_ml, _from_heads(y_moba)], axis=-1)

def second_inputs(seed: int = 0) -> dict:
    key = jax.random.key(seed)
    ks = jax.random.split(key, 22)
    n = jax.random.normal
    f32 = jnp.float32
    return {
        'x': n(ks[0], (BATCH, SEQ, D_MODEL), f32),
        'c': n(ks[1], (BATCH, D_MODEL), f32),
        'w_ada': n(ks[2], (DEPTH, D_MODEL, 6 * D_MODEL), f32) * (0.5 * D_MODEL ** -0.5),
        'b_ada': n(ks[3], (DEPTH, 6 * D_MODEL), f32) * 0.01,
        'norm1_g': 1.0 + 0.02 * n(ks[4], (DEPTH, D_MODEL), f32),
        'norm2_g': 1.0 + 0.02 * n(ks[5], (DEPTH, D_MODEL), f32),
        'w_in': n(ks[6], (DEPTH, D_MODEL, IN_COLS), f32) * D_MODEL ** -0.5,
        'fox_f_bias': 2.0 + 0.1 * n(ks[7], (DEPTH, FOX_HEADS), f32),
        'fox_q_g': 1.0 + 0.02 * n(ks[8], (DEPTH, HEAD_DIM), f32),
        'fox_k_g': 1.0 + 0.02 * n(ks[9], (DEPTH, HEAD_DIM), f32),
        'ml_conv_w': n(ks[10], (DEPTH, ML_CONV, 2 * ML_W), f32) * ML_CONV ** -0.5,
        'ml_conv_b': 0.01 * n(ks[11], (DEPTH, 2 * ML_W), f32),
        'ml_i_bias': 0.1 * n(ks[12], (DEPTH, ML_HEADS), f32),
        'ml_f_bias': 3.0 + 0.1 * n(ks[13], (DEPTH, ML_HEADS), f32),
        'ml_h_g': 1.0 + 0.02 * n(ks[14], (DEPTH, ML_W), f32),
        'moba_q_g': 1.0 + 0.02 * n(ks[15], (DEPTH, HEAD_DIM), f32),
        'moba_k_g': 1.0 + 0.02 * n(ks[16], (DEPTH, HEAD_DIM), f32),
        'w_out': n(ks[17], (DEPTH, D_MODEL, D_MODEL), f32) * D_MODEL ** -0.5,
        'w_gate_up': n(ks[18], (DEPTH, D_MODEL, 2 * D_FF), f32) * D_MODEL ** -0.5,
        'w_down': n(ks[19], (DEPTH, D_FF, D_MODEL), f32) * D_FF ** -0.5,
    }

def second_block(x, c, w_ada, b_ada, norm1_g, norm2_g, w_in, fox_f_bias, fox_q_g, fox_k_g,
              ml_conv_w, ml_conv_b, ml_i_bias, ml_f_bias, ml_h_g, moba_q_g, moba_k_g,
              w_out, w_gate_up, w_down):
    for l in range(DEPTH):
        mod = jax.nn.silu(c) @ w_ada[l] + b_ada[l]
        sh1, sc1, g1, sh2, sc2, g2 = jnp.split(mod[:, None, :], 6, axis=-1)
        hn = (_rms(x, norm1_g[l]) * (1 + sc1) + sh1).astype(x.dtype)
        y = _mixer(hn, w_in[l], fox_f_bias[l], fox_q_g[l], fox_k_g[l], ml_conv_w[l],
                   ml_conv_b[l], ml_i_bias[l], ml_f_bias[l], ml_h_g[l], moba_q_g[l], moba_k_g[l])
        x = x + g1 * (y.astype(x.dtype) @ w_out[l])
        hn = (_rms(x, norm2_g[l]) * (1 + sc2) + sh2).astype(x.dtype)
        gate, up = jnp.split(hn @ w_gate_up[l], 2, axis=-1)
        x = x + g2 * ((jax.nn.silu(gate) * up) @ w_down[l])
    return x


def setup_inputs(seed=0):
    out = dict(first_inputs(seed))
    for name, value in second_inputs(seed + 1).items():
        if name != "x":
            out[name + "_2"] = value
    return out


def reference(
    x, positions, g_attn_norm, w_in, w_pool, b_pool, pool_scale, g_q_a, w_q_b, g_kv_a, w_kv_b,
    g_out_pool, g_out_attn, w_out, g_ffn_norm, w_router, b_router, w_gate_up, b_gate_up, w_down,
    b_down, g_final, c_2, w_ada_2, b_ada_2, norm1_g_2, norm2_g_2, w_in_2, fox_f_bias_2,
    fox_q_g_2, fox_k_g_2, ml_conv_w_2, ml_conv_b_2, ml_i_bias_2, ml_f_bias_2, ml_h_g_2,
    moba_q_g_2, moba_k_g_2, w_out_2, w_gate_up_2, w_down_2,
):
    x = first_block(
        x, positions, g_attn_norm, w_in, w_pool, b_pool, pool_scale, g_q_a, w_q_b, g_kv_a,
        w_kv_b, g_out_pool, g_out_attn, w_out, g_ffn_norm, w_router, b_router, w_gate_up,
        b_gate_up, w_down, b_down, g_final,
    )
    return second_block(
        x, c_2, w_ada_2, b_ada_2, norm1_g_2, norm2_g_2, w_in_2, fox_f_bias_2, fox_q_g_2,
        fox_k_g_2, ml_conv_w_2, ml_conv_b_2, ml_i_bias_2, ml_f_bias_2, ml_h_g_2, moba_q_g_2,
        moba_k_g_2, w_out_2, w_gate_up_2, w_down_2,
    )


_drawn_inputs = setup_inputs


def setup_inputs(seed=0):
    import zlib

    import numpy as np

    out = dict(_drawn_inputs(seed))
    spreads = {}
    factors = {'b_gate_up': 8.0,
     'b_down': 8.0,
     'b_ada_2': 5.238,
     'norm1_g_2': 8.0,
     'norm2_g_2': 8.0,
     'fox_f_bias_2': 8.0,
     'fox_q_g_2': 8.0,
     'fox_k_g_2': 8.0,
     'ml_conv_b_2': 64.0,
     'ml_i_bias_2': 64.0,
     'ml_f_bias_2': 8.0,
     'ml_h_g_2': 53.041,
     'moba_q_g_2': 8.0,
     'moba_k_g_2': 8.0}
    for name, (base, spread) in spreads.items():
        noise = np.random.default_rng([zlib.crc32(name.encode()), seed]).standard_normal(out[name].shape)
        drawn = base * np.exp(spread * noise) if base else spread * noise
        out[name] = __import__('jax').numpy.asarray(drawn.astype(out[name].dtype))
    for name, factor in factors.items():
        out[name] = (out[name] * factor).astype(out[name].dtype)
    return out
```

```python
from contextlib import ExitStack

import concourse.bass as bass
from concourse import mybir

F32 = mybir.dt.float32
BF16 = mybir.dt.bfloat16
I32 = mybir.dt.int32
ALU = mybir.AluOpType
ACT = mybir.ActivationFunctionType
AX = mybir.AxisListType

P = 128
D = 1024
T = 256
NT = T // P
KD = D // P
EPS = 1e-6
INV_2PI = 0.15915494309189535
TWO_PI = (6.28125, 1.93500518798828125e-3, 3.0199159795074593e-07)
PI_IN, HALF_PI = 3.1415925, 1.5707963267948966
RSQRT_GUESS = float(0x5F3759DF)
ROUND = 12582912.0
NEG = -1.0e30
BIG = 3.0e38

D_POOL, GROUPS = 512, 4
WINDOWS = (2, 4, 8, 16)
Q_LORA, KV_LORA, ROPE, NOPE, VDIM, HEADS = 256, 128, 32, 64, 64, 8
HALF = ROPE // 2
QK = NOPE + ROPE
IN1 = D_POOL + Q_LORA + KV_LORA + ROPE
EXPERTS, TOPK, FE = 32, 4, 1024
LIMIT, ALPHA = 7.0, 1.702
CAP = 64
PASSES = T // CAP
OVER = NT * P * TOPK // (CAP + 1)

HD = 64
FOX, ML, MOBA = 6, 4, 6
SOFT = FOX + MOBA
C_FQ, C_FK, C_FV, C_FF = 0, 384, 768, 1152
C_MQ, C_MK, C_MV, C_MI, C_MF, C_MO = 1158, 1414, 1670, 1926, 1930, 1934
C_BQ, C_BK, C_BV, IN2 = 2190, 2574, 2958, 3342
CONV = 4
D_FF = 2816
FT = D_FF // P

SLOTS, SLOT = 12, 2048
CW = SLOT // KD


def split(n, w):
    return [(a, min(w, n - a)) for a in range(0, n, w)]


IN1_CHUNKS = split(IN1, CW)
IN2_CHUNKS = split(IN2, CW)
IN2_GATES = C_MO // CW + 1
ADA_CHUNKS = [(g, k) for g in range(3) for k in range(KD)]
PAIRS = D_FF // CW

N_IN1 = 0
N_QB = N_IN1 + len(IN1_CHUNKS)
N_KVB = N_QB + 1
N_ADA = N_KVB + 1
N_OUT1 = N_ADA + len(ADA_CHUNKS)
N_MOE = N_OUT1 + 4
N_IN2 = N_MOE + EXPERTS * SLOTS
N_OUT2 = N_IN2 + len(IN2_CHUNKS)
N_GU2 = N_OUT2 + 4
N_DN2 = N_GU2 + 2 * PAIRS
N_END = N_DN2 + FT // 2

VEC_ROWS = {}
_at = 0
for _name, _n in (("c_2", 8), ("norm1_g_2", 8), ("norm2_g_2", 8), ("g_attn_norm", 8), ("g_ffn_norm", 8),
                  ("g_q_a", 2), ("g_kv_a", 1), ("pool_scale", 4), ("b_pool", 4), ("g_out_pool", 4),
                  ("g_out_attn", 4), ("ml_conv_w_2", 16), ("ml_conv_b_2", 4), ("ml_h_g_2", 2),
                  ("fox_q_g_2", 1), ("fox_k_g_2", 1), ("moba_q_g_2", 1), ("moba_k_g_2", 1)):
    VEC_ROWS[_name] = (_at, _n)
    _at += _n
NVEC = _at

CONST = {}
VEC_DMAS = len(VEC_ROWS) + 4
_at = 0
for _name, _n in (("ident", P), ("ones", P), ("tri_inc", P), ("tri_exc", P), ("mask", P), ("iota", PASSES * P),
                  ("slope", NT * MOBA), ("inv", HALF), ("pass_expert", 96), ("pass_block", 96), ("pass_floor", 96),
                  ("pass_rank", 16), ("pick", EXPERTS + 1)):
    CONST[_name] = (_at, _n)
    _at += _n
NCONST = _at

STAT_W = (2, 4, 0, 2, 2, 2, 2, 48, 8, 2)
STAT_AT = [sum(STAT_W[:i]) for i in range(len(STAT_W))]
NSTAT = sum(STAT_W)
S_ATTN, S_LAT, S_POOL, S_AOUT, S_FFN, S_FINAL, S_NORM1, S_HEADS, S_ML, S_NORM2 = range(10)

SIGNALS = """x_in const_in band_in vec_in pos_in wpool_in bias14_in gfin_in bada_in bgu_in bdown_in router_in
brouter_in bf_const vec_turned vec_cols c_ready rows_ready rows_turned cols_dve cols_act proj_kept
lat_rows lat_turned lat_cols qkv_kept trig_arg trig_ready q_roped k_roped qk_turned q_cols k_cols
diff_done diff_kept mixed_done pool_sq pool_sum pool_cols ada_kept mod_turned mod_cols
scores_done rowmax_ready probs_ready smat_ready probs_turned pt_kept pv_done o_free att_rows att_turned att_cols
pool_steps up_steps o_up_steps o_steps logits_done shifted exp_ready routed ranks_done ranks_kept
gates_turned gates_kept lists_ready bias_split
picked sel_ready selb_ready gathered xg_ready clipped sig_ready act_ready act_turned actt_ready yb_ready
sel_turned selt_ready scattered
o_loaded o_picked o_gathered o_xg o_gu o_clipped o_sig o_act o_act_turned o_actt o_down o_yb o_sel_turned
o_selt o_scattered o_ring_back
moe_done ff_ready ff_ln decay_ready cum_done cum_kept cumt_turned bias_rows conv_in conv_turned
conv_sum conv_silu qk_sq sq_used heads_ready heads_turned heads_cols ml_exp ml_m ml_guard ml_sig
bcast_done bcast_kept gate_used silu_ready h_ready h_turned h_cols out_ready out_stored""".split()


class Steps:

    def __init__(self, eng, own, signals):
        self.eng, self.own, self.signals, self.n, self.told = eng, own, signals, 0, {}

    def step(self, ins):
        self.n += 1
        ins.then_inc(self.own, 1)
        self.eng.wait_ge(self.own, self.n)

    def tell(self, ins, name):
        self.told[name] = self.told.get(name, 0) + 1
        ins.then_inc(self.signals[name], 1)
        self.eng.wait_ge(self.signals[name], self.told[name])


def two_blocks(nc, ins, consts, band, out):
    with ExitStack() as ctx:
        def sb(name, shape, dt=F32):
            return ctx.enter_context(nc.sbuf_tensor(name, shape, dt))

        def sem(name):
            return ctx.enter_context(nc.semaphore(name))

        ring = sb("ring", [P, SLOTS, SLOT])
        x_sb = sb("x_sb", [P, NT, D])
        rows = sb("rows", [P, NT, D])
        cols = sb("cols", [P, KD, T])
        work = sb("work", [P, 7488])
        qk = sb("qk", [P, 16, T])
        probs = sb("probs", [P, 2, 384])
        probs_flat = probs[:, :, :].rearrange("p a b -> p (a b)")
        pt = sb("pt", [P, 2, 384])
        mod = sb("mod", [P, 3, 512])
        gfin = sb("gfin", [P, D])
        gate_b = sb("gate_b", [P, D])
        cst = sb("cst", [P, NCONST])
        vec = sb("vec", [NVEC, P])
        vcol = sb("vcol", [P, NVEC])
        modc = sb("modc", [P, 48])
        modg = sb("modg", [P, 16])
        c_rep = sb("c_rep", [P, KD, 32])
        wide = sb("wide", [P, 1036])
        router = sb("router", [P, KD, EXPERTS])
        wpool = sb("wpool", [P, GROUPS, P])
        maskb = sb("maskb", [P, P], BF16)
        identb = sb("identb", [P, P], BF16)
        ms = sb("ms", [P, NSTAT])
        rs = sb("rs", [P, NSTAT])
        rsqrt_tmp = sb("rsqrt_tmp", [P, 48])
        rmax = sb("rmax", [P, 16, NT])
        nmax = sb("nmax", [P, 16, NT])
        psum_row = sb("psum_row", [P, 16, NT])
        rank = sb("rank", [P, NT, EXPERTS + 1])
        gates = sb("gates", [P, NT, EXPERTS + 1])
        pos_i = sb("pos_i", [P, NT], I32)
        lists = sb("lists", [1, 36], I32)
        den_all = sb("den_all", [P, 16, NT])
        pool_nop = sb("pool_nop", [1, 4])
        bias14 = sb("bias14", [P, 14])
        trig = sb("trig", [P, 2, NT, HALF])
        PS = ctx.enter_context(nc.psum_tensor("PS", [P, 8, 512], F32))

        sig = {name: sem(name) for name in SIGNALS}
        landed = [sem(f"slot{i}_landed") for i in range(SLOTS)]
        chunk_used = sem("chunk_used")
        dve_own, act_own = sem("dve_order"), sem("act_order")

        def const(name, parts=P):
            a, n = CONST[name]
            return cst[0:parts, a:a + n]

        def col(name, i=0):
            return vcol[:, VEC_ROWS[name][0] + i:VEC_ROWS[name][0] + i + 1]

        def stat(tile, request):
            return tile[:, STAT_AT[request]:STAT_AT[request] + STAT_W[request]]

        ident, ones = const("ident"), const("ones")

        proj1 = work[:, 0:NT * IN1].rearrange("p (t n) -> p t n", t=NT)
        b_at = NT * IN1
        band_sb = work[:, b_at:b_at + 2048].rearrange("p (g s t) -> p g s t", g=GROUPS, s=NT)
        q_rows = work[:, b_at + 2048:b_at + 3584].rearrange("p (t h n) -> p t h n", t=NT, h=HEADS)
        kv_rows = work[:, b_at + 3584:b_at + 5632].rearrange("p (t h n) -> p t h n", t=NT, h=HEADS)
        k_rows = rows[:, :, 0:HEADS * QK].rearrange("p t (h n) -> p t h n", h=HEADS)
        lat_rows = pt[:, :, 0:384]
        lat = cols[:, 0:3, :]
        diff = work[:, b_at:b_at + 1024].rearrange("p (g t) -> p g t", g=GROUPS)
        pooled = work[:, b_at + 1024:b_at + 2048].rearrange("p (g t) -> p g t", g=GROUPS)
        pool_sq = work[:, 0:1024].rearrange("p (g t) -> p g t", g=GROUPS)
        pool_ms, pool_rs, pool_tmp = (work[:, a:a + T] for a in (1024, 1280, 1536))
        rope_tmp = [wide[:, i * 256:(i + 1) * 256].rearrange("p (t h n) -> p t h n", t=NT, h=HEADS)
                    for i in range(4)]
        ang, turns = (wide[:, a:a + NT * HALF].rearrange("p (t n) -> p t n", t=NT) for a in (0, NT * HALF))
        att = rows[:, :, 0:512]
        sel_g = work[:, 0:128].rearrange("p (t s) -> p t s", t=NT)
        sel_s = work[:, 128:384].rearrange("p (t s) -> p t s", t=NT)
        sel_t = work[:, 384:640]
        xg = work[:, 640:1152].rearrange("p (k s) -> p k s", k=KD)
        g_min, act_buf, sg, act_t, yb = (work[:, a:a + 512] for a in range(1152, 1152 + 5 * 512, 512))
        u_clip = work[:, 3712:4224]
        sel_b = work[0:96, 4224:4256].bitcast(BF16)
        bgu_f = work[0:96, 4256:6304]
        lg = work[:, 6304:6376].rearrange("p (t e) -> p t e", t=NT)
        lr = work[:, 6376:6448].rearrange("p (t e) -> p t e", t=NT)
        top = work[:, 6448:6464].rearrange("p (t e) -> p t e", t=NT)
        chosen = work[:, 6464:6528].rearrange("p (t e) -> p t e", t=NT)
        gexp = work[:, 6528:6592].rearrange("p (t e) -> p t e", t=NT)
        small = work[:, 6592:6720]
        gates_t = work[0:EXPERTS, 6720:6976]
        lr_row, list_f = work[0:1, 7296:7392], work[0:1, 7392:7440]
        brouter = work[:, 6976:7008]
        zero_k = work[0:1, 7040:7296].bitcast(BF16)
        list_eq = work[0:1, 0:1536].rearrange("p (j i) -> p j i", j=16)
        list_w = work[0:1, 1536:3072].rearrange("p (j i) -> p j i", j=16)
        bias_b = wide[0:96, 0:1024].bitcast(BF16)
        bdown_sb = gate_b[0:EXPERTS, :]
        proj = work[:, 0:NT * IN2].rearrange("p (t n) -> p t n", t=NT)
        tail = work[:, NT * IN2:7488]
        bias_r = tail[0:16, 0:T]
        bias_c = tail[:, 256:288].rearrange("p (t h) -> p t h", t=NT)
        logf, fg, cum = (tail[:, a:a + 20].rearrange("p (t h) -> p t h", t=NT) for a in (288, 308, 328))
        ml_e = tail[:, 348:732]
        guard, den = (tail[:, a:a + 8].rearrange("p (h t) -> p h t", t=NT) for a in (732, 740))
        rinv = tail[:, 748:764].rearrange("p (h t) -> p h t", t=NT)
        sq_buf = [rows[:, b, 0:768] for b in range(2)]
        conv_x = wide[:, :].rearrange("p (c t) -> p c t", c=CONV)
        h_t = work[:, 0:FT * T].rearrange("p (f t) -> p f t", f=FT)
        h_sil = work[:, FT * T:FT * T + 1024].rearrange("p (b n) -> p b n", b=2)
        h_rows = rows[:, :, 0:512]

        def slot(n):
            return ring[:, n % SLOTS, :]

        def bank(b):
            return PS[:, b, :]

        def by_rows(w, r0, n_cols, tiles):
            return w[r0:r0 + tiles * P, :].rearrange("(k p) n -> p k n", p=P)

        def chunk_source(n):
            if n < N_QB:
                a, w = IN1_CHUNKS[n]
                return ins["w_in"][0][:, a:a + w].rearrange("(k p) n -> p k n", p=P), KD, w
            if n == N_QB:
                return ins["w_q_b"][0].rearrange("(k p) n -> p k n", p=P), 2, HEADS * QK
            if n == N_KVB:
                return ins["w_kv_b"][0].rearrange("(k p) n -> p k n", p=P), 1, 1024
            if n < N_OUT1:
                g, k = ADA_CHUNKS[n - N_ADA]
                return ins["w_ada_2"][0][k * P:(k + 1) * P, g * SLOT:(g + 1) * SLOT].rearrange(
                    "(k p) n -> p k n", p=P), 1, SLOT
            if n < N_MOE:
                return by_rows(ins["w_out"][0], (n - N_OUT1) * 2 * P, D, 2), 2, D
            n_ = n
            if n_ < N_OUT2:
                a, w = IN2_CHUNKS[n_ - N_IN2]
                return ins["w_in_2"][0][:, a:a + w].rearrange("(k p) n -> p k n", p=P), KD, w
            if n_ < N_GU2:
                return by_rows(ins["w_out_2"][0], (n_ - N_OUT2) * 2 * P, D, 2), 2, D
            if n_ < N_DN2:
                j, up = divmod(n_ - N_GU2, 2)
                a = up * D_FF + j * CW
                return ins["w_gate_up_2"][0][:, a:a + CW].rearrange("(k p) n -> p k n", p=P), KD, CW
            return by_rows(ins["w_down_2"][0], (n_ - N_DN2) * 2 * P, D, 2), 2, D

        def chunk(n):
            _, k, w = chunk_source(n)
            return slot(n)[:, 0:k * w].rearrange("p (k n) -> p k n", k=k)

        gu_dram = ins["w_gate_up"][0].rearrange("e (k p) n -> (e k) p n", p=P)
        dn_dram = ins["w_down"][0].rearrange("e (s k p) n -> (e s) p k n", p=P, k=2)

        heads2 = [(h // 2, 3 + h // 2, HD * (h % 2), C_FV + HD * h, h) for h in range(FOX)]
        heads2 += [(6 + h // 2, 9 + h // 2, HD * (h % 2), C_BV + HD * h, FOX + h) for h in range(MOBA)]
        heads2 += [(12 + h // 2, 14 + h // 2, HD * (h % 2), C_MV + HD * h, SOFT + h) for h in range(ML)]

        def attention_heads(block_no):
            if block_no == 1:
                for h in range(HEADS):
                    yield (h, qk[0:QK, h, :], qk[0:QK, 8 + h, :],
                           lambda kt, h=h: kv_rows[:, kt, h, NOPE:NOPE + VDIM], None, False, h * VDIM)
            else:
                for i, (qt, kt_, base, v, row) in enumerate(heads2):
                    first = 0 if i < FOX else FOX if i < SOFT else SOFT
                    yield (HEADS + i, qk[base:base + HD, qt, :], qk[base:base + HD, kt_, :],
                           lambda kt, v=v: proj[:, kt, v:v + HD], row, i >= SOFT, (i - first) * HD)

        def scores_used(eng, g):
            if g < HEADS + SOFT:
                eng.wait_ge(sig["probs_ready"], g + 1)
            else:
                eng.wait_ge(sig["smat_ready"], g + 1 - HEADS - SOFT)

        GROUP_OF = {1: [(0, HEADS)], 2: [(0, FOX), (FOX, SOFT), (SOFT, SOFT + ML)]}
        ATT_SCALE = {1: float(QK) ** -0.5, 2: float(HD) ** -0.5}

        block = ctx.enter_context(nc.Block())

        @block.sync
        def _(sp):
            def load(n):
                src, k, w = chunk_source(n)
                if n >= SLOTS:
                    sp.wait_ge(chunk_used, n - SLOTS + 1)
                dst = slot(n)[:, 0:k * w].rearrange("p (k n) -> p k n", k=k)
                sp.dma_start(dst, src).then_inc(landed[n % SLOTS], 16)

            for n in range(N_MOE):
                load(n)
            with sp.Fori(0, EXPERTS) as e:
                for c in range(SLOTS):
                    s = (N_MOE + c) % SLOTS
                    sp.wait_ge(chunk_used, e * SLOTS + (N_MOE + c - SLOTS + 1))
                    if c < KD:
                        sp.dma_start(ring[:, s, :], gu_dram[bass.ds(e * KD + c, 1), :, :]
                                     .rearrange("o p n -> (o p) n")).then_inc(landed[s], 16)
                    else:
                        sp.dma_start(ring[:, s, :].rearrange("p (o k n) -> p o k n", o=1, k=2),
                                     dn_dram[bass.ds(e * 4 + (c - KD), 1), :, :, :]
                                     .rearrange("o p k n -> p o k n")).then_inc(landed[s], 16)
            sp.wait_ge(sig["lists_ready"], 1)
            n_over = sp.value_load(lists[0:1, 32:33], min_val=0, max_val=16)
            with sp.If(n_over > 0):
                sp.wait_ge(chunk_used, N_IN2)
                with sp.Fori(0, OVER) as j:
                    with sp.If(j < n_over):
                        e = sp.value_load(lists[0:1, bass.ds(j, 1)], min_val=0, max_val=EXPERTS - 1)
                        for c in range(SLOTS):
                            if c < KD:
                                sp.dma_start(ring[:, c, :], gu_dram[bass.ds(e * KD + c, 1), :, :]
                                             .rearrange("o p n -> (o p) n")).then_inc(sig["o_loaded"], 16)
                            else:
                                sp.dma_start(ring[:, c, :].rearrange("p (o k n) -> p o k n", o=1, k=2),
                                             dn_dram[bass.ds(e * 4 + (c - KD), 1), :, :, :]
                                             .rearrange("o p k n -> p o k n")).then_inc(sig["o_loaded"], 16)
                        sp.wait_ge(sig["o_down"], j + 1)
                        sp.sem_inc(sig["o_ring_back"], 1)
            for n in range(N_IN2, N_END):
                load(n)
            sp.wait_ge(sig["out_stored"], 16 * 4)

        @block.tensor
        def _(pe):
            def need(n):
                pe.wait_ge(landed[n % SLOTS], 16 * (n // SLOTS + 1))

            turned = [0]

            def turn_rows(wait_rows):
                pe.wait_ge(sig["rows_ready"], wait_rows)
                for k in range(KD):
                    for t in range(NT):
                        mm = pe.transpose(bank(k // 2)[:, (k % 2) * T + t * P:][:, 0:P],
                                          rows[:, t, k * P:(k + 1) * P], ident)
                    if k % 2:
                        mm.then_inc(sig["rows_turned"], 1)
                turned[0] += 1

            def need_cols():
                pe.wait_ge(sig["cols_dve"], 4 * turned[0])
                pe.wait_ge(sig["cols_act"], 4 * turned[0])

            pe.wait_ge(sig["const_in"], 16)
            pe.wait_ge(sig["vec_in"], VEC_DMAS * 16)
            pe.transpose(bank(6)[:, 0:NVEC], vec[:, :], ident[0:NVEC, 0:NVEC]).then_inc(sig["vec_turned"], 1)

            def project(chunks, base_n, banks, first):
                for c, (a, w) in enumerate(chunks):
                    n = base_n + c
                    b = banks[c % 2]
                    if c >= 2:
                        pe.wait_ge(sig["proj_kept"], first + c - 1)
                    need(n)
                    for t in range(NT):
                        for k in range(KD):
                            mm = pe.matmul(bank(b)[:, t * w:(t + 1) * w], cols[:, k, t * P:(t + 1) * P],
                                           chunk(n)[:, k, :], start=(k == 0), stop=(k == KD - 1))
                    mm.then_inc(chunk_used, 1)

            turn_rows(2)
            need_cols()
            project(IN1_CHUNKS, N_IN1, (4, 5), 0)

            pe.wait_ge(sig["lat_rows"], 4)
            for i in range(3):
                for t in range(NT):
                    mm = pe.transpose(bank(i // 2)[:, (i % 2) * T + t * P:][:, 0:P],
                                      lat_rows[:, t, i * P:(i + 1) * P], ident)
            mm.then_inc(sig["lat_turned"], 1)
            pe.wait_ge(sig["band_in"], 16)
            for g in range(GROUPS):
                for s in range(NT):
                    mm = pe.matmul(bank(2 + g // 2)[:, (g % 2) * T:(g % 2 + 1) * T],
                                   proj1[:, s, g * P:(g + 1) * P], band_sb[:, g, s, :],
                                   start=(s == 0), stop=(s == NT - 1))
            mm.then_inc(sig["diff_done"], 1)
            pe.wait_ge(sig["lat_cols"], 1)
            need(N_QB)
            for t in range(NT):
                for a, w in ((0, 512), (512, 256)):
                    for k in range(2):
                        mm = pe.matmul(bank(4 + 2 * t + a // 512)[:, 0:w], lat[:, k, t * P:(t + 1) * P],
                                       chunk(N_QB)[:, k, a:a + w], start=(k == 0), stop=(k == 1))
            mm.then_inc(chunk_used, 1)
            need(N_KVB)
            for t in range(NT):
                pe.wait_ge(sig["qkv_kept"], 2 * (t + 1))
                for a in (0, 512):
                    mm = pe.matmul(bank(4 + 2 * t + a // 512), lat[:, 2, t * P:(t + 1) * P],
                                   chunk(N_KVB)[:, 0, a:a + 512], start=True, stop=True)
            mm.then_inc(chunk_used, 1)
            pe.wait_ge(sig["diff_kept"], 2)
            pe.wait_ge(sig["wpool_in"], 16)
            for g in range(GROUPS):
                mm = pe.matmul(bank(2 + g // 2)[:, (g % 2) * T:(g % 2 + 1) * T], wpool[:, g, :],
                               diff[:, g, :], start=True, stop=True)
            mm.then_inc(sig["mixed_done"], 1)
            for which, src, roped, at in (("q_cols", q_rows, "q_roped", 0), ("k_cols", k_rows, "k_roped", 1)):
                pe.wait_ge(sig[roped], 1)
                for b in range(4):
                    bb = (0, 1, 4, 5)[b]
                    if at == 0 and b < 2:
                        pe.wait_ge(sig["lat_cols"], 1)
                    if at == 0 and b == 2:
                        pe.wait_ge(sig["qkv_kept"], 8)
                    if at == 1:
                        pe.wait_ge(sig["q_cols"], b + 1)
                    for h in (2 * b, 2 * b + 1):
                        for t in range(NT):
                            mm = pe.transpose(bank(bb)[0:QK, (h % 2) * T + t * P:][:, 0:P], src[:, t, h, :], ident)
                    mm.then_inc(sig["qk_turned"], 1)
            pe.wait_ge(sig["pool_sq"], 1)
            for g in range(GROUPS):
                mm = pe.matmul(bank(6)[:, 0:T], ones, pool_sq[:, g, :], start=(g == 0), stop=(g == GROUPS - 1))
            mm.then_inc(sig["pool_sum"], 1)

            def ada(n):
                g, k = ADA_CHUNKS[n - N_ADA]
                if k == 0:
                    pe.wait_ge(sig["c_ready"], 1)
                    if g:
                        pe.wait_ge(sig["ada_kept"], g)
                    else:
                        pe.wait_ge(sig["qkv_kept"], 8)
                need(n)
                for j in range(4):
                    mm = pe.matmul(bank(7)[32 * j:32 * j + 32, :], c_rep[:, k, :], slot(n)[:, j * 512:(j + 1) * 512],
                                   start=(k == 0), stop=(k == KD - 1))
                mm.then_inc(chunk_used, 1)

            def attention(block_no, extra=()):
                heads = list(attention_heads(block_no))
                extra = list(extra)
                for lo, hi in GROUP_OF[block_no]:
                    for i in range(lo, hi + 2):
                        if i < hi:
                            g, q, k, v, row, ml, _ = heads[i]
                            s = bank(g % 2)
                            if block_no == 2 and g == HEADS:
                                pe.wait_ge(sig["bias_rows"], 1)
                            if g >= 2:
                                scores_used(pe, g - 2)
                            for t in range(NT):
                                a, w = (0, P) if t == 0 else (P, T)
                                plain = ml or (row is None)
                                pe.matmul(s[:, a:a + w], q[:, t * P:(t + 1) * P], k[:, 0:w], start=True, stop=ml)
                                if ml:
                                    d = bank(6 + g % 2)
                                    pe.matmul(d[:, a:a + w], ident[0:16, row:row + 1].to_broadcast([16, P]),
                                              bias_r[:, 0:w], start=True, stop=False)
                                    mm = pe.matmul(d[:, t * T:t * T + P], identb[:, :], maskb[:, :], start=False, stop=True)
                                    continue
                                if not plain:
                                    pe.matmul(s[:, a:a + w], ident[0:16, row:row + 1].to_broadcast([16, P]),
                                              bias_r[:, 0:w], start=False, stop=False)
                                mm = pe.matmul(s[:, t * T:t * T + P], identb[:, :], maskb[:, :], start=False, stop=True)
                            mm.then_inc(sig["scores_done"], 1)
                            for n in extra[:3]:
                                ada(n)
                            extra = extra[3:]
                        if lo < i <= hi:
                            g = heads[i - 1][0]
                            scores_used(pe, g)
                            if g >= 2:
                                pe.wait_ge(sig["pt_kept"], g - 1)
                            for b in range(3):
                                mm = pe.transpose(bank(2 + g % 2)[:, b * P:(b + 1) * P],
                                                  probs[:, g % 2, b * P:(b + 1) * P], ident)
                            mm.then_inc(sig["probs_turned"], 1)
                        if i >= lo + 2:
                            g, _, _, v, _, _, oc = heads[i - 2]
                            pe.wait_ge(sig["pt_kept"], g + 1)
                            if i == lo + 2:
                                if g:
                                    pe.wait_ge(sig["o_free"], {HEADS: 1, HEADS + FOX: 2, HEADS + SOFT: 3}[g])
                            pe.matmul(bank(4)[:, oc:oc + HD], pt[:, g % 2, 0:P], v(0), start=True, stop=True)
                            pe.matmul(bank(5)[:, oc:oc + HD], pt[:, g % 2, P:2 * P], v(0), start=True, stop=False)
                            mm = pe.matmul(bank(5)[:, oc:oc + HD], pt[:, g % 2, 2 * P:3 * P], v(1),
                                           start=False, stop=True)
                            mm.then_inc(sig["pv_done"], 1)

            pe.wait_ge(sig["k_cols"], 4)
            pe.wait_ge(sig["pool_cols"], 4)
            attention(1, range(N_ADA, N_OUT1))

            for g in range(3):
                pe.wait_ge(sig["ada_kept"], g + 1)
                if g:
                    pe.wait_ge(sig["mod_cols"], g)
                for q in range(4):
                    mm = pe.transpose(bank(6)[:, q * P:(q + 1) * P], mod[:, g, q * P:(q + 1) * P], ident)
                mm.then_inc(sig["mod_turned"], 1)

            pe.wait_ge(sig["att_rows"], 2)
            for f in range(4):
                for t in range(NT):
                    mm = pe.transpose(bank(f // 2)[:, (f % 2) * T + t * P:][:, 0:P], att[:, t, f * P:(f + 1) * P], ident)
            mm.then_inc(sig["att_turned"], 1)

            def project_out(base_n):
                for c in range(4):
                    need(base_n + c)
                    for k in (2 * c, 2 * c + 1):
                        for t in range(NT):
                            for h in range(2):
                                mm = pe.matmul(bank(2 * t + h), cols[:, k, t * P:(t + 1) * P],
                                               chunk(base_n + c)[:, k % 2, h * 512:(h + 1) * 512],
                                               start=(k == 0), stop=(k == KD - 1))
                    mm.then_inc(chunk_used, 1)

            pe.wait_ge(sig["att_cols"], 4)
            pe.wait_ge(sig["pool_cols"], 4)
            project_out(N_OUT1)

            turn_rows(4)
            need_cols()
            pe.wait_ge(sig["router_in"], 16)
            for t in range(NT):
                for k in range(KD):
                    mm = pe.matmul(bank(4)[:, t * EXPERTS:(t + 1) * EXPERTS], cols[:, k, t * P:(t + 1) * P],
                                   router[:, k, :], start=(k == 0), stop=(k == KD - 1))
            mm.then_inc(sig["logits_done"], 1)
            pe.wait_ge(sig["routed"], 1)
            pe.matmul(bank(5)[:, 0:32], const("tri_exc"), chosen[:, 0, :], start=True, stop=True)
            pe.matmul(bank(5)[:, 32:64], ones, chosen[:, 0, :], start=True, stop=False)
            pe.matmul(bank(5)[:, 32:64], const("tri_exc"), chosen[:, 1, :], start=False, stop=True)
            pe.matmul(bank(5)[:, 64:96], ones, chosen[:, 0, :], start=True, stop=False)
            pe.matmul(bank(5)[:, 64:96], ones, chosen[:, 1, :], start=False, stop=True).then_inc(sig["ranks_done"], 1)
            pe.wait_ge(sig["ranks_kept"], 1)
            for t in range(NT):
                mm = pe.transpose(bank(6)[0:EXPERTS, t * P:(t + 1) * P], gates[:, t, 0:EXPERTS], ident)
            mm.then_inc(sig["gates_turned"], 1)
            pe.wait_ge(sig["gates_kept"], 1)
            pe.wait_ge(sig["bdown_in"], 16)
            for t in range(NT):
                for h in range(2):
                    pe.matmul(bank(4 + 2 * t + h), gates_t[:, t * P:(t + 1) * P],
                              bdown_sb[:, h * 512:(h + 1) * 512], start=True, stop=False)

            def moe_gather(done):
                for k in range(KD):
                    for t in range(NT):
                        mm = pe.matmul(bank(2)[:, k * CAP:(k + 1) * CAP], rows[:, t, k * P:(k + 1) * P],
                                       sel_g[:, t, :], start=(t == 0), stop=(t == NT - 1))
                mm.then_inc(done, 1)

            def moe_gate_up(weights, used):
                for b in range(2):
                    for h in range(2):
                        pe.matmul(bank(b)[CAP * h:CAP * (h + 1), :], sel_b[:, :],
                                  bias_b[:, b * FE + h * 512:b * FE + (h + 1) * 512], start=True, stop=False)
                for k in range(KD):
                    w = weights(k)
                    for b in range(2):
                        for h in range(2):
                            mm = pe.matmul(bank(b)[CAP * h:CAP * (h + 1), :], xg[:, k, :],
                                           w[:, b * FE + h * 512:b * FE + (h + 1) * 512],
                                           start=False, stop=(k == KD - 1))
                    used(mm, k)

            def moe_turn_sel(done):
                for t in range(NT):
                    mm = pe.transpose(bank(3)[:, t * P:(t + 1) * P], sel_s[:, t, :], ident)
                mm.then_inc(done, 1)

            def moe_turn_act(done):
                for j in range(4):
                    mm = pe.transpose(bank(0)[:, j * P:(j + 1) * P], act_buf[:, j * P:(j + 1) * P], ident)
                mm.then_inc(done, 1)

            def moe_down(weights, used):
                for s in range(4):
                    w = weights(s)
                    for f in (2 * s, 2 * s + 1):
                        lhs = act_t[:, (f % 4) * P + CAP * (f // 4):][:, 0:CAP]
                        for h in range(2):
                            mm = pe.matmul(bank(3)[CAP * h:CAP * (h + 1), :], lhs,
                                           w[:, (f % 2) * D + h * 512:(f % 2) * D + (h + 1) * 512],
                                           start=(f == 0), stop=(f == 7))
                    used(mm, s)

            def moe_scatter(done):
                for t in range(NT):
                    for h in range(2):
                        mm = pe.matmul(bank(4 + 2 * t + h), sel_t[CAP * h:CAP * (h + 1), t * P:(t + 1) * P],
                                       yb[CAP * h:CAP * (h + 1), :], start=False, stop=False)
                mm.then_inc(done, 1)

            pe.wait_ge(sig["picked"], 1)
            moe_gather(sig["gathered"])
            pe.wait_ge(sig["bias_split"], 1)
            with pe.Fori(0, EXPERTS) as e:
                def ring_w(first):
                    def get(i):
                        s = (N_MOE + first + i) % SLOTS
                        pe.wait_ge(landed[s], e * 16 + 16 * ((N_MOE + first + i) // SLOTS + 1))
                        return ring[:, s, :]
                    return get

                pe.wait_ge(sig["selb_ready"], e + 1)
                pe.wait_ge(sig["xg_ready"], e + 1)
                moe_gate_up(ring_w(0), lambda mm, k: mm.then_inc(chunk_used, 1))
                pe.wait_ge(sig["yb_ready"], e + 1)
                moe_scatter(sig["scattered"])
                pe.wait_ge(sig["sel_ready"], e + 1)
                moe_turn_sel(sig["sel_turned"])
                pe.wait_ge(sig["picked"], e + 2)
                moe_gather(sig["gathered"])
                pe.wait_ge(sig["act_ready"], e + 1)
                moe_turn_act(sig["act_turned"])
                pe.wait_ge(sig["actt_ready"], e + 1)
                pe.wait_ge(sig["selt_ready"], e + 1)
                moe_down(ring_w(KD), lambda mm, s: mm.then_inc(chunk_used, 1))
            pe.wait_ge(sig["yb_ready"], EXPERTS + 1)
            moe_scatter(sig["o_scattered"])

            n_over = pe.value_load(lists[0:1, 32:33], min_val=0, max_val=16)
            with pe.If(n_over > 0):
                with pe.Fori(0, OVER) as j:
                    with pe.If(j < n_over):
                        pe.wait_ge(sig["o_picked"], j + 1)
                        moe_gather(sig["o_gathered"])
                        moe_turn_sel(sig["o_sel_turned"])
                        pe.wait_ge(sig["o_xg"], j + 1)
                        pe.wait_ge(sig["o_loaded"], j * (16 * SLOTS) + 16 * SLOTS)
                        moe_gate_up(lambda k: ring[:, k, :],
                                    lambda mm, k: mm.then_inc(sig["o_gu"], 1) if k == KD - 1 else None)
                        pe.wait_ge(sig["o_act"], j + 1)
                        moe_turn_act(sig["o_act_turned"])
                        pe.wait_ge(sig["o_actt"], j + 1)
                        pe.wait_ge(sig["o_selt"], j + 1)
                        moe_down(lambda s: ring[:, KD + s, :],
                                 lambda mm, s: mm.then_inc(sig["o_down"], 1) if s == 3 else None)
                        pe.wait_ge(sig["o_yb"], j + 1)
                        moe_scatter(sig["o_scattered"])
            for t in range(NT):
                for h in range(2):
                    mm = pe.matmul(bank(4 + 2 * t + h), zero_k[:, 0:P], zero_k[:, 0:512],
                                   start=False, stop=True)
            mm.then_inc(sig["moe_done"], 1)

            turn_rows(6)
            need_cols()
            project(IN2_CHUNKS, N_IN2, (4, 5), len(IN1_CHUNKS))

            pe.wait_ge(sig["decay_ready"], 1)
            pe.matmul(bank(6)[:, 0:10], const("tri_inc"), logf[:, 0, :], start=True, stop=True)
            pe.matmul(bank(6)[:, 16:26], ones, logf[:, 0, :], start=True, stop=False)
            pe.matmul(bank(6)[:, 16:26], const("tri_inc"), logf[:, 1, :], start=False, stop=True).then_inc(
                sig["cum_done"], 1)
            for i in range(6):
                pe.wait_ge(sig["heads_ready"], 4)
                if i >= 2:
                    pe.wait_ge(sig["heads_cols"], i - 1)
                else:
                    pe.wait_ge(sig["cols_dve"], 12)
                for f in (2 * i, 2 * i + 1):
                    c = (C_FQ + f * P) if f < 6 else (C_BQ + (f - 6) * P)
                    for t in range(NT):
                        mm = pe.transpose(bank(i % 2)[:, (f % 2) * T + t * P:][:, 0:P], proj[:, t, c:c + P], ident)
                mm.then_inc(sig["heads_turned"], 1)
            for f in range(4):
                for t in range(NT):
                    mm = pe.transpose(bank(2 + f // 2)[:, (f % 2) * T + t * P:][:, 0:P],
                                      proj[:, t, C_MQ + f * P:C_MQ + (f + 1) * P], ident)
            mm.then_inc(sig["conv_turned"], 1)
            pe.wait_ge(sig["cum_kept"], 1)
            for t in range(NT):
                mm = pe.transpose(bank(7)[0:16, t * P:(t + 1) * P], bias_c[:, t, :], ident)
            mm.then_inc(sig["cumt_turned"], 1)
            pe.wait_ge(sig["heads_cols"], 6)
            pe.wait_ge(sig["conv_silu"], 4)
            attention(2)

            def spread(g, j0, first):
                if first:
                    pe.wait_ge(sig["bcast_kept"], first)
                for i in range(2):
                    j = j0 + i
                    mm = pe.matmul(bank(6 + i), ident[:, 32 * j:32 * j + 1].to_broadcast([P, P]), mod[:, g, :],
                                   start=True, stop=True)
                mm.then_inc(sig["bcast_done"], 1)

            turn_rows(7)
            spread(1, 0, 0)
            need_cols()
            project_out(N_OUT2)
            turn_rows(9)
            spread(2, 2, 1)
            need_cols()

            for j in range(PAIRS + 1):
                if j < PAIRS:
                    if j >= 2:
                        pe.wait_ge(sig["h_ready"], j - 1)
                    if j == 1:
                        pe.wait_ge(sig["bcast_kept"], 2)
                    for up in range(2):
                        n = N_GU2 + 2 * j + up
                        need(n)
                        for t in range(NT):
                            for k in range(KD):
                                mm = pe.matmul(bank(4 + 2 * (j % 2) + up)[:, t * CW:(t + 1) * CW],
                                               cols[:, k, t * P:(t + 1) * P], chunk(n)[:, k, :],
                                               start=(k == 0), stop=(k == KD - 1))
                        mm.then_inc(chunk_used, 1)
                if j >= 1:
                    i = j - 1
                    pe.wait_ge(sig["h_ready"], i + 1)
                    if i >= 2:
                        pe.wait_ge(sig["h_cols"], i - 1)
                    for f in range(2):
                        for t in range(NT):
                            mm = pe.transpose(bank(i % 2)[:, f * T + t * P:][:, 0:P],
                                              h_rows[:, i % 2, t * CW + f * P:t * CW + (f + 1) * P], ident)
                    mm.then_inc(sig["h_turned"], 1)
            for c in range(FT // 2):
                need(N_DN2 + c)
                if c == 0:
                    pe.wait_ge(sig["h_cols"], PAIRS)
                for f in (2 * c, 2 * c + 1):
                    for t in range(NT):
                        for h in range(2):
                            mm = pe.matmul(bank(4 + 2 * t + h), h_t[:, f, t * P:(t + 1) * P],
                                           chunk(N_DN2 + c)[:, f % 2, h * 512:(h + 1) * 512],
                                           start=(f == 0), stop=(f == FT - 1))
                mm.then_inc(chunk_used, 1)

        @block.scalar
        def _(act):
            do = Steps(act, act_own, sig)

            def load(dst, src, name):
                act.dma_start(dst, src).then_inc(sig[name], 16)

            load(x_sb[:, :, :], ins["x"][0].rearrange("(t p) n -> p t n", p=P), "x_in")
            load(cst[:, :], consts, "const_in")
            for name, (at, n) in VEC_ROWS.items():
                src = ins[name]
                if name in ("fox_q_g_2", "fox_k_g_2", "moba_q_g_2", "moba_k_g_2"):
                    load(vec[at:at + 1, 0:HD], src, "vec_in")
                    load(vec[at:at + 1, HD:P], src, "vec_in")
                elif name == "ml_conv_w_2":
                    load(vec[at:at + n, :], src[0].rearrange("j (c p) -> (j c) p", p=P), "vec_in")
                elif name == "b_pool":
                    load(vec[at:at + n, :], src[0], "vec_in")
                else:
                    load(vec[at:at + n, :], src.rearrange("o (k p) -> (o k) p", p=P), "vec_in")
            load(band_sb, band, "band_in")
            act.dma_start(pos_i[:, :], ins["positions"][0].rearrange("(t p) -> p t", p=P),
                          allow_slow_non_contiguous=True).then_inc(sig["pos_in"], 16)
            load(wpool[:, :, :], ins["w_pool"][0].rearrange("g c d -> c g d"), "wpool_in")
            for j in range(4):
                load(mod[32 * j:32 * j + 32, :, :],
                     ins["b_ada_2"][0].rearrange("(g j n) -> j g n", g=3, j=4)[j].partition_broadcast(32), "bada_in")
            load(router[:, :, :], ins["w_router"][0].rearrange("(k p) e -> p k e", p=P), "router_in")
            load(bdown_sb, ins["b_down"][0], "bdown_in")
            load(gfin[:, :], ins["g_final"].partition_broadcast(P), "gfin_in")
            load(bias14[:, 0:6], ins["fox_f_bias_2"][0].partition_broadcast(P), "bias14_in")
            load(bias14[:, 6:10], ins["ml_f_bias_2"][0].partition_broadcast(P), "bias14_in")
            load(bias14[:, 10:14], ins["ml_i_bias_2"][0].partition_broadcast(P), "bias14_in")

            turned = [0]

            def keep_cols(scale, shift=None):
                turned[0] += 1
                for k in range(4, KD):
                    act.wait_ge(sig["rows_turned"], 4 * (turned[0] - 1) + k // 2 + 1)
                    ins_ = nc.scalar.activation(cols[:, k, :], bank(k // 2)[:, (k % 2) * T:(k % 2 + 1) * T],
                                                ACT.Identity, scale=scale(k) if scale else 1.0,
                                                bias=shift(k) if shift else 0.0)
                    do.tell(ins_, "cols_act")

            act.wait_ge(sig["vec_cols"], 1)
            a = VEC_ROWS["c_2"][0]
            do.tell(nc.scalar.activation(c_rep[:, :, :], vcol[:, a:a + KD].unsqueeze(2).to_broadcast([P, KD, 32]),
                                         ACT.Silu), "c_ready")
            keep_cols(lambda k: col("g_attn_norm", k))

            def keep_proj(dst, chunks, banks, base_n):
                for c, (a, w) in enumerate(chunks):
                    act.wait_ge(chunk_used, base_n + c + 1)
                    do.tell(nc.scalar.copy(dst[:, :, a:a + w],
                                           bank(banks[c % 2])[:, 0:NT * w].rearrange("p (t n) -> p t n", t=NT)),
                            "proj_kept")

            keep_proj(proj1, IN1_CHUNKS, (4, 5), N_IN1)
            act.wait_ge(sig["trig_arg"], 1)
            do.tell(nc.scalar.activation(trig[:, :, :, :], trig[:, :, :, :], ACT.Sin), "trig_ready")
            act.wait_ge(sig["diff_done"], 1)
            for b in range(2):
                do.tell(nc.scalar.copy(diff[:, 2 * b:2 * b + 2, :],
                                       bank(2 + b).rearrange("p (g t) -> p g t", g=2)), "diff_kept")
            flat_q = q_rows.rearrange("p t h n -> p t (h n)")
            flat_kv = kv_rows.rearrange("p t h n -> p t (h n)")
            act.wait_ge(chunk_used, N_QB + 1)
            for t in range(NT):
                for a, w in ((0, 512), (512, 256)):
                    do.tell(nc.scalar.copy(flat_q[:, t, a:a + w], bank(4 + 2 * t + a // 512)[:, 0:w]), "qkv_kept")
            act.wait_ge(chunk_used, N_KVB + 1)
            for t in range(NT):
                for a in (0, 512):
                    do.tell(nc.scalar.copy(flat_kv[:, t, a:a + 512], bank(4 + 2 * t + a // 512)), "qkv_kept")
            for b in range(4):
                act.wait_ge(sig["qk_turned"], b + 1)
                do.tell(nc.scalar.copy(qk[0:QK, 2 * b:2 * b + 2, :],
                                       bank((0, 1, 4, 5)[b])[0:QK, :].rearrange("p (h t) -> p h t", h=2)), "q_cols")

            def attention(block_no):
                heads = list(attention_heads(block_no))
                scale = ATT_SCALE[block_no]
                for lo, hi in GROUP_OF[block_no]:
                    for i in range(lo, hi + 1):
                        if i < hi:
                            g, _, _, _, _, ml, _ = heads[i]
                            b = g % 2
                            src = bank(6 + b) if ml else bank(b)
                            dst = ml_e if ml else probs[:, b, :]
                            act.wait_ge(sig["rowmax_ready"], g + 1)
                            if ml:
                                if i > lo:
                                    scores_used(act, g - 1)
                            elif g >= 2:
                                act.wait_ge(sig["probs_turned"], g - 1)
                            for t in range(NT):
                                a, w = (0, P) if t == 0 else (P, T)
                                kw = {} if ml else {"accum_out": psum_row[:, i % 16, t:t + 1]}
                                ins_ = nc.scalar.activation(dst[:, a:a + w], src[:, a:a + w], ACT.Exp,
                                                            bias=nmax[:, i % 16, t:t + 1],
                                                            scale=1.0 if ml else scale, **kw)
                                if t == 0:
                                    do.step(ins_)
                                elif ml:
                                    do.tell(ins_, "ml_exp")
                                else:
                                    do.tell(ins_, "probs_ready")
                        if i > lo:
                            g = heads[i - 1][0]
                            act.wait_ge(sig["probs_turned"], g + 1)
                            if g >= 2:
                                act.wait_ge(sig["pv_done"], g - 1)
                            do.tell(nc.scalar.copy(pt[:, g % 2, :], bank(2 + g % 2)[:, 0:384]), "pt_kept")

            attention(1)
            act.wait_ge(sig["att_turned"], 1)
            for f in range(4):
                do.tell(nc.scalar.activation(cols[:, 4 + f, :], bank(f // 2)[:, (f % 2) * T:(f % 2 + 1) * T],
                                             ACT.Copy, scale=col("g_out_attn", f)), "att_cols")
            load(bgu_f[0:32, :], ins["b_gate_up"][0], "bgu_in")
            load(bgu_f[32:64, :], ins["b_gate_up"][0], "bgu_in")
            load(bgu_f[64:96, :], ins["b_gate_up"][0], "bgu_in")
            load(brouter, ins["b_router"][0].partition_broadcast(P), "brouter_in")
            keep_cols(lambda k: col("g_ffn_norm", k))
            act.wait_ge(sig["shifted"], 1)
            for t in range(NT):
                do.step(nc.scalar.activation(gexp[:, t, :], lg[:, t, 0:EXPERTS], ACT.Exp, bias=small[:, t:t + 1]))
            for t in range(NT):
                ins_ = nc.scalar.activation(small[:, 8 + 4 * t:12 + 4 * t], top[:, t, 4:8], ACT.Exp,
                                            bias=small[:, t:t + 1], accum_out=small[:, 2 + t:3 + t])
                do.tell(ins_, "exp_ready")
            act.wait_ge(sig["gates_turned"], 1)
            do.tell(nc.scalar.copy(gates_t, bank(6)[0:EXPERTS, 0:T]), "gates_kept")

            def keep_sel(done):
                return nc.scalar.copy(sel_t, bank(3)[:, 0:T]).then_inc(done, 1)

            def sigmoid(done):
                return nc.scalar.activation(sg, g_min, ACT.Sigmoid, scale=ALPHA).then_inc(done, 1)

            def keep_act(done):
                return nc.scalar.copy(act_t, bank(0)).then_inc(done, 1)

            def keep_y(done):
                return nc.scalar.copy(yb, bank(3)).then_inc(done, 1)

            act.wait_ge(sig["lists_ready"], 1)
            nc.scalar.activation(sel_t, const("iota")[:, 0:T], ACT.Copy, scale=0.0)
            nc.scalar.activation(yb, const("iota"), ACT.Copy, scale=0.0).then_inc(sig["yb_ready"], 1)
            with act.Fori(0, EXPERTS) as e:
                act.wait_ge(sig["clipped"], e + 1)
                sigmoid(sig["sig_ready"])
                act.wait_ge(sig["sel_turned"], e + 1)
                act.wait_ge(sig["scattered"], e + 1)
                keep_sel(sig["selt_ready"])
                act.wait_ge(sig["act_turned"], e + 1)
                keep_act(sig["actt_ready"])
                act.wait_ge(chunk_used, e * SLOTS + (N_MOE + SLOTS))
                keep_y(sig["yb_ready"])
            n_over = act.value_load(lists[0:1, 32:33], min_val=0, max_val=16)
            with act.If(n_over > 0):
                with act.Fori(0, OVER) as j:
                    with act.If(j < n_over):
                        act.wait_ge(sig["o_sel_turned"], j + 1)
                        act.wait_ge(sig["o_scattered"], j + 1)
                        keep_sel(sig["o_selt"])
                        act.wait_ge(sig["o_clipped"], j + 1)
                        sigmoid(sig["o_sig"])
                        act.wait_ge(sig["o_act_turned"], j + 1)
                        keep_act(sig["o_actt"])
                        act.wait_ge(sig["o_down"], j + 1)
                        keep_y(sig["o_yb"])

            keep_cols(lambda k: modg[:, k:k + 1], lambda k: modc[:, k:k + 1])
            keep_proj(proj, IN2_CHUNKS, (4, 5), N_IN2)
            act.wait_ge(sig["ff_ready"], 1)
            do.step(nc.scalar.activation(logf, logf, ACT.Exp))
            do.tell(nc.scalar.activation(logf, logf, ACT.Ln, bias=1.0), "ff_ln")
            for i, c in enumerate((C_FQ, C_BQ)):
                for t in range(NT):
                    n = 2 * i + t
                    if n >= 2:
                        act.wait_ge(sig["sq_used"], n - 1)
                    do.tell(nc.scalar.activation(sq_buf[n % 2], proj[:, t, c:c + 768], ACT.Square), "qk_sq")
            for i in range(6):
                act.wait_ge(sig["heads_turned"], i + 1)
                gname = ("fox_q_g_2", "fox_k_g_2", "moba_q_g_2", "moba_k_g_2")
                for f in (2 * i, 2 * i + 1):
                    ins_ = nc.scalar.activation(qk[:, f, :], bank(i % 2)[:, (f % 2) * T:(f % 2 + 1) * T], ACT.Copy,
                                                scale=col(gname[f // 3]))
                    if f % 2:
                        do.tell(ins_, "heads_cols")
                    else:
                        do.step(ins_)
            act.wait_ge(sig["conv_turned"], 1)
            for b in range(2):
                ins_ = nc.scalar.copy(conv_x[:, 2 * b:2 * b + 2, 3:3 + T],
                                      bank(2 + b).rearrange("p (c t) -> p c t", c=2))
                do.tell(ins_, "conv_in")
            for c in range(4):
                act.wait_ge(sig["conv_sum"], c + 1)
                do.tell(nc.scalar.activation(qk[:, 12 + c, :], qk[:, 12 + c, :], ACT.Silu,
                                             bias=col("ml_conv_b_2", c)), "conv_silu")
            attention(2)
            act.wait_ge(sig["ml_m"], 1)
            do.tell(nc.scalar.activation(guard, guard, ACT.Exp, scale=-1.0), "ml_guard")
            do.tell(nc.scalar.activation(proj[:, :, C_MO:C_MO + 256], proj[:, :, C_MO:C_MO + 256], ACT.Sigmoid),
                    "ml_sig")

            def keep_bcast(n):
                act.wait_ge(sig["bcast_done"], n)
                do.step(nc.scalar.copy(gate_b[:, 0:512], bank(6)))
                do.tell(nc.scalar.copy(gate_b[:, 512:1024], bank(7)), "bcast_kept")

            keep_cols(lambda k: col("ml_h_g_2", 1) if k == 4 else 1.0)
            keep_bcast(1)
            keep_cols(lambda k: modg[:, 8 + k:9 + k], lambda k: modc[:, 24 + k:25 + k])
            act.wait_ge(sig["gate_used"], 1)
            keep_bcast(2)
            for j in range(PAIRS + 1):
                if j < PAIRS:
                    act.wait_ge(chunk_used, N_GU2 + 2 * j + 1)
                    if j >= 2:
                        act.wait_ge(sig["h_ready"], j - 1)
                    do.tell(nc.scalar.activation(h_sil[:, j % 2, :], bank(4 + 2 * (j % 2)), ACT.Silu), "silu_ready")
                if j >= 1:
                    i = j - 1
                    act.wait_ge(sig["h_turned"], i + 1)
                    do.tell(nc.scalar.copy(h_t[:, 2 * i:2 * i + 2, :],
                                           bank(i % 2).rearrange("p (f t) -> p f t", f=2)), "h_cols")
            for i in range(4):
                t, h = divmod(i, 2)
                act.wait_ge(sig["out_ready"], i + 1)
                act.dma_start(out[0, t * P:(t + 1) * P, h * 512:(h + 1) * 512],
                              x_sb[:, t, h * 512:(h + 1) * 512]).then_inc(sig["out_stored"], 16)
            act.wait_ge(sig["out_stored"], 16 * 4)

        @block.vector
        def _(dve):
            v = nc.vector
            do = Steps(dve, dve_own, sig)

            def rsqrt(dst, src, tmp):
                do.step(v.tensor_scalar(dst.bitcast(I32), src.bitcast(I32), 1, None, ALU.logical_shift_right))
                do.step(v.tensor_scalar(dst.bitcast(I32), dst.bitcast(I32), -1.0, RSQRT_GUESS, ALU.mult, ALU.add))
                for _ in range(3):
                    do.step(v.tensor_tensor(tmp, dst, src, ALU.mult))
                    do.step(v.scalar_tensor_tensor(out=tmp, in0=tmp, scalar=-0.5, in1=dst, op0=ALU.mult, op1=ALU.mult))
                    do.step(v.scalar_tensor_tensor(out=dst, in0=tmp, scalar=1.5, in1=dst, op0=ALU.add, op1=ALU.mult))

            def rstd(request, n):
                src, dst = stat(ms, request), stat(rs, request)
                do.step(v.tensor_scalar(src, src, 1.0 / n, EPS, ALU.mult, ALU.add))
                rsqrt(dst, src, rsqrt_tmp[:, 0:STAT_W[request]])
                return dst

            def scaled(request, src, dst, width, name):
                st = stat(ms, request)
                for t in range(NT):
                    do.step(v.tensor_tensor_reduce(out=dst(t), in0=src(t), in1=src(t), scale=1.0, scalar=0.0,
                                                   op0=ALU.mult, op1=ALU.add, accum_out=st[:, t:t + 1]))
                r_ = rstd(request, width)
                for t in range(NT):
                    do.tell(v.tensor_scalar(dst(t), src(t), r_[:, t:t + 1], None, ALU.mult), name)

            turned = [0]

            def keep_cols(scale, shift=None):
                turned[0] += 1
                for k in range(4):
                    dve.wait_ge(sig["rows_turned"], 4 * (turned[0] - 1) + k // 2 + 1)
                    src = bank(k // 2)[:, (k % 2) * T:(k % 2 + 1) * T]
                    if shift:
                        ins_ = v.tensor_scalar(cols[:, k, :], src, scale(k), shift(k), ALU.mult, ALU.add)
                    else:
                        ins_ = v.tensor_scalar(cols[:, k, :], src, scale(k), None, ALU.mult)
                    do.tell(ins_, "cols_dve")

            dve.wait_ge(sig["const_in"], 16)
            do.step(v.tensor_copy(identb[:, :], ident))
            do.tell(v.tensor_copy(maskb[:, :], const("mask")), "bf_const")
            dve.wait_ge(sig["x_in"], 16)
            scaled(S_ATTN, lambda t: x_sb[:, t, :], lambda t: rows[:, t, :], D, "rows_ready")
            dve.wait_ge(sig["vec_turned"], 1)
            do.tell(v.tensor_copy(vcol[:, :], bank(6)[:, 0:NVEC]), "vec_cols")
            keep_cols(lambda k: col("g_attn_norm", k))

            dve.wait_ge(sig["pos_in"], 16)
            do.step(v.tensor_copy(ms[:, 0:NT], pos_i[:, :]))
            for t in range(NT):
                do.step(v.tensor_scalar(ang[:, t, :], const("inv"), ms[:, t:t + 1], None, ALU.mult))
            do.step(v.tensor_scalar(turns, ang, INV_2PI, None, ALU.mult))
            do.step(v.tensor_scalar(turns, turns, ROUND, None, ALU.add))
            do.step(v.tensor_scalar(turns, turns, -ROUND, None, ALU.add))
            for part in TWO_PI:
                do.step(v.scalar_tensor_tensor(out=ang, in0=turns, scalar=-part, in1=ang, op0=ALU.mult, op1=ALU.add))
            do.step(v.tensor_scalar(trig[:, 0, :, :], ang, PI_IN, -PI_IN, ALU.min, ALU.max))
            do.step(v.scalar_tensor_tensor(out=ang, in0=trig[:, 0, :, :], scalar=-1.0, in1=trig[:, 0, :, :],
                                           op0=ALU.mult, op1=ALU.min))
            do.tell(v.tensor_scalar(trig[:, 1, :, :], ang, HALF_PI, None, ALU.add), "trig_arg")

            dve.wait_ge(sig["proj_kept"], len(IN1_CHUNKS))
            st = stat(ms, S_LAT)
            for i, (a, w) in enumerate(((D_POOL, Q_LORA), (D_POOL + Q_LORA, KV_LORA))):
                for t in range(NT):
                    do.step(v.tensor_tensor_reduce(out=lat_rows[:, t, a - D_POOL:a - D_POOL + w],
                                                   in0=proj1[:, t, a:a + w], in1=proj1[:, t, a:a + w], scale=1.0 / w,
                                                   scalar=0.0, op0=ALU.mult, op1=ALU.add,
                                                   accum_out=st[:, 2 * i + t:2 * i + t + 1]))
            r_ = rstd(S_LAT, 1)
            for i, (a, w) in enumerate(((D_POOL, Q_LORA), (D_POOL + Q_LORA, KV_LORA))):
                for t in range(NT):
                    do.tell(v.tensor_scalar(lat_rows[:, t, a - D_POOL:a - D_POOL + w], proj1[:, t, a:a + w],
                                            r_[:, 2 * i + t:2 * i + t + 1], None, ALU.mult), "lat_rows")
            dve.wait_ge(sig["lat_turned"], 1)
            for i in range(3):
                g_ = col("g_q_a", i) if i < 2 else col("g_kv_a")
                ins_ = v.tensor_scalar(lat[:, i, :], bank(i // 2)[:, (i % 2) * T:(i % 2 + 1) * T], g_, None, ALU.mult)
                if i < 2:
                    do.step(ins_)
                else:
                    do.tell(ins_, "lat_cols")

            def rope(x1, x2, y1, y2, heads_n):
                cos, sin = (trig[:, i, :, :].unsqueeze(2).to_broadcast([P, NT, heads_n, HALF]) for i in (1, 0))
                tmp = [r[:, :, 0:heads_n, :] for r in rope_tmp]
                for dst, a_, b_ in zip(tmp, (x1, x2, x2, x1), (cos, sin, cos, sin)):
                    do.step(v.tensor_tensor(dst, a_, b_, ALU.mult))
                return (v.tensor_tensor(y1, tmp[0], tmp[1], ALU.subtract), v.tensor_tensor(y2, tmp[2], tmp[3], ALU.add))

            dve.wait_ge(sig["trig_ready"], 1)
            k1 = proj1[:, :, IN1 - ROPE:IN1 - HALF].unsqueeze(2)
            k2 = proj1[:, :, IN1 - HALF:IN1].unsqueeze(2)
            for ins_ in rope(k1, k2, k1, k2, 1):
                do.step(ins_)
            dve.wait_ge(sig["rows_turned"], 4)
            for t in range(NT):
                do.step(v.tensor_copy(k_rows[:, t, :, NOPE:QK],
                                      proj1[:, t, IN1 - ROPE:IN1].unsqueeze(1).to_broadcast([P, HEADS, ROPE])))
            dve.wait_ge(sig["qkv_kept"], 4)
            q1, q2 = q_rows[:, :, :, NOPE:NOPE + HALF], q_rows[:, :, :, NOPE + HALF:QK]
            a_, b_ = rope(q1, q2, q1, q2, HEADS)
            do.step(a_)
            do.tell(b_, "q_roped")
            dve.wait_ge(sig["qkv_kept"], 8)
            do.tell(v.tensor_copy(k_rows[:, :, :, 0:NOPE], kv_rows[:, :, :, 0:NOPE]), "k_roped")

            dve.wait_ge(sig["mixed_done"], 1)
            for g in range(GROUPS):
                do.step(v.tensor_scalar(pooled[:, g, :], bank(2 + g // 2)[:, (g % 2) * T:(g % 2 + 1) * T],
                                        col("b_pool", g), col("pool_scale", g), ALU.add, ALU.mult))
            do.tell(v.tensor_tensor(pool_sq, pooled, pooled, ALU.mult), "pool_sq")
            for b in range(4):
                dve.wait_ge(sig["qk_turned"], 4 + b + 1)
                do.tell(v.tensor_copy(qk[0:QK, 8 + 2 * b:8 + 2 * b + 2, :],
                                      bank((0, 1, 4, 5)[b])[0:QK, :].rearrange("p (h t) -> p h t", h=2)), "k_cols")
            dve.wait_ge(sig["pool_sum"], 1)
            do.step(v.tensor_scalar(pool_ms, bank(6)[:, 0:T], 1.0 / D_POOL, EPS, ALU.mult, ALU.add))
            rsqrt(pool_rs, pool_ms, pool_tmp)
            for g in range(GROUPS):
                do.tell(v.scalar_tensor_tensor(out=cols[:, g, :], in0=pooled[:, g, :], scalar=col("g_out_pool", g),
                                               in1=pool_rs, op0=ALU.mult, op1=ALU.mult), "pool_cols")

            def keep_ada(g):
                dve.wait_ge(sig["bada_in"], 64)
                dve.wait_ge(chunk_used, N_ADA + KD * (g + 1))
                do.tell(v.tensor_tensor(mod[:, g, :], bank(7), mod[:, g, :], ALU.add), "ada_kept")

            def attention(block_no):
                heads = list(attention_heads(block_no))
                for lo, hi in GROUP_OF[block_no]:
                    for i in range(lo, hi):
                        g, _, _, _, _, ml, _ = heads[i]
                        src = bank((6 if ml else 0) + g % 2)
                        dve.wait_ge(sig["scores_done"], g + 1)
                        do.step(v.tensor_reduce(rmax[:, i, 0:1], src[:, 0:P], AX.X, ALU.max))
                        do.step(v.tensor_reduce(rmax[:, i, 1:2], src[:, P:3 * P], AX.X, ALU.max))
                        if ml:
                            do.tell(v.tensor_scalar(nmax[:, i, :], rmax[:, i, :], 0.0, -1.0, ALU.max, ALU.mult),
                                    "rowmax_ready")
                            dve.wait_ge(sig["ml_exp"], i - SOFT + 1)
                            dve.wait_ge(sig["probs_turned"], g - 1)
                            for t in range(NT):
                                a, w = (0, P) if t == 0 else (P, T)
                                ins_ = v.tensor_tensor_reduce(
                                    out=probs[:, g % 2, a:a + w], in0=bank(g % 2)[:, a:a + w], in1=ml_e[:, a:a + w],
                                    scale=float(HD) ** -0.5, scalar=0.0, op0=ALU.mult, op1=ALU.add,
                                    accum_out=psum_row[:, i, t:t + 1])
                                if t:
                                    do.tell(ins_, "smat_ready")
                                else:
                                    do.step(ins_)
                        else:
                            do.tell(v.tensor_scalar(nmax[:, i, :], rmax[:, i, :], -ATT_SCALE[block_no], None, ALU.mult),
                                    "rowmax_ready")
                        if block_no == 1 and i in (2, 5, 7):
                            keep_ada((2, 5, 7).index(i))
                    g = heads[hi - 1][0]
                    n = hi - lo
                    scores_used(dve, g)
                    if lo != SOFT:
                        do.step(v.reciprocal(den_all[:, lo:hi, :], psum_row[:, lo:hi, :]))
                    else:
                        do.step(v.tensor_scalar(guard, nmax[:, lo:hi, :], -1.0, None, ALU.mult))
                        do.tell(v.tensor_tensor(guard, guard, cum[:, :, 6:10].rearrange("p t h -> p h t"), ALU.add),
                                "ml_m")
                        dve.wait_ge(sig["ml_guard"], 1)
                        do.step(v.scalar_tensor_tensor(out=den, in0=psum_row[:, lo:hi, :], scalar=-1.0,
                                                       in1=psum_row[:, lo:hi, :], op0=ALU.mult, op1=ALU.max))
                        do.step(v.tensor_tensor(den, den, guard, ALU.max))
                        do.step(v.reciprocal(den_all[:, lo:hi, :], den))
                    dve.wait_ge(sig["pv_done"], g + 1)
                    at = {0: 0, FOX: 640, SOFT: 384}[lo]
                    if block_no == 2 and lo == 0:
                        dve.wait_ge(sig["qk_sq"], 4)
                    for t in range(NT):
                        ins_ = v.tensor_tensor(rows[:, t, at:at + n * HD].rearrange("p (h d) -> p h d", h=n),
                                               bank(4 + t)[:, 0:n * HD].rearrange("p (h d) -> p h d", h=n),
                                               den_all[:, lo:hi, t:t + 1].to_broadcast([P, n, HD]), ALU.mult)
                        if t:
                            do.tell(ins_, "o_free")
                        else:
                            do.step(ins_)

            attention(1)
            st = stat(ms, S_AOUT)
            for t in range(NT):
                do.step(v.tensor_tensor_reduce(out=rows[:, t, 512:1024], in0=att[:, t, :], in1=att[:, t, :], scale=1.0,
                                               scalar=0.0, op0=ALU.mult, op1=ALU.add, accum_out=st[:, t:t + 1]))
            r_ = rstd(S_AOUT, 512)
            for t in range(NT):
                do.tell(v.tensor_scalar(att[:, t, :], att[:, t, :], r_[:, t:t + 1], None, ALU.mult), "att_rows")
            for g in range(3):
                dve.wait_ge(sig["mod_turned"], g + 1)
                do.tell(v.tensor_copy(modc[:, 16 * g:16 * g + 16].rearrange("p (j q) -> p j q", j=4),
                                      bank(6).rearrange("p (q j r) -> p j q r", q=4, j=4)[:, :, :, 0]), "mod_cols")
            for i, (at, name) in enumerate(((8, "norm1_g_2"), (32, "norm2_g_2"))):
                a = VEC_ROWS[name][0]
                do.step(v.scalar_tensor_tensor(out=modg[:, 8 * i:8 * i + 8], in0=modc[:, at:at + 8], scalar=1.0,
                                               in1=vcol[:, a:a + 8], op0=ALU.add, op1=ALU.mult))

            dve.wait_ge(chunk_used, N_OUT1 + 4)
            for i in range(4):
                t, h = divmod(i, 2)
                xs = x_sb[:, t, h * 512:(h + 1) * 512]
                do.step(v.tensor_tensor(xs, bank(i), xs, ALU.add))
            scaled(S_FFN, lambda t: x_sb[:, t, :], lambda t: rows[:, t, :], D, "rows_ready")
            keep_cols(lambda k: col("g_ffn_norm", k))

            do.step(v.memset(lg[:, :, EXPERTS:EXPERTS + 4], BIG))
            do.step(v.memset(rank[:, :, :], -1.0))
            do.step(v.memset(gates[:, :, :], 0.0))
            dve.wait_ge(sig["logits_done"], 1)
            dve.wait_ge(sig["brouter_in"], 16)
            do.step(v.tensor_tensor(lg[:, :, 0:EXPERTS],
                                    bank(4)[:, 0:NT * EXPERTS].rearrange("p (t e) -> p t e", t=NT),
                                    brouter.unsqueeze(1).to_broadcast([P, NT, EXPERTS]), ALU.add))
            for t in range(NT):
                do.step(v.max(top[:, t, :], lg[:, t, :]))
                do.step(v.match_replace(out=lr[:, t, :], in_to_replace=top[:, t, :], in_values=lg[:, t, :],
                                        imm_value=-BIG))
            do.step(v.tensor_scalar(small[:, 0:NT], top[:, :, 4], -1.0, None, ALU.mult))
            do.tell(v.tensor_tensor(chosen, lr[:, :, 0:EXPERTS], lg[:, :, 0:EXPERTS], ALU.not_equal), "routed")
            do.tell(v.tensor_copy(small[:, 4:6], small[:, 0:2]), "shifted")
            dve.wait_ge(sig["exp_ready"], 2)
            do.step(v.reciprocal(small[:, 4:6], small[:, 2:4]))
            for t in range(NT):
                do.step(v.scalar_tensor_tensor(out=gates[:, t, 0:EXPERTS], in0=gexp[:, t, :],
                                               scalar=small[:, 4 + t:5 + t], in1=chosen[:, t, :],
                                               op0=ALU.mult, op1=ALU.mult))
            dve.wait_ge(sig["ranks_done"], 1)
            counts = bank(5)[0:1, 64:96].unsqueeze(1).to_broadcast([1, 3, EXPERTS])
            flag, upto = small[0:1, 16:112], lr_row
            do.step(v.tensor_tensor(flag.rearrange("p (b e) -> p b e", b=3), counts,
                                    const("pass_floor", 1).rearrange("p (b e) -> p b e", b=3), ALU.is_gt))
            do.step(v.scalar_tensor_tensor(out=gexp, in0=bank(5)[:, 0:64].rearrange("p (t e) -> p t e", t=NT),
                                           scalar=1.0, in1=chosen, op0=ALU.add, op1=ALU.mult))
            do.tell(v.tensor_scalar(rank[:, :, 0:EXPERTS], gexp, 1.0, None, ALU.subtract), "ranks_kept")
            do.step(v.tensor_tensor_scan(out=upto, data0=ones[0:1, 0:96], data1=flag, initial=0.0,
                                         op0=ALU.mult, op1=ALU.add))
            do.step(v.tensor_tensor(list_eq, upto.unsqueeze(1).to_broadcast([1, 16, 96]),
                                    const("pass_rank", 1).unsqueeze(2).to_broadcast([1, 16, 96]), ALU.is_equal))
            do.step(v.tensor_tensor(list_eq, list_eq, flag.unsqueeze(1).to_broadcast([1, 16, 96]), ALU.mult))
            for i, name in enumerate(("pass_expert", "pass_block")):
                do.step(v.tensor_tensor(list_w, list_eq, const(name, 1).unsqueeze(1).to_broadcast([1, 16, 96]),
                                        ALU.mult))
                do.step(v.tensor_reduce(list_f[:, 16 * i:16 * i + 16], list_w, AX.X, ALU.add))
            do.step(v.tensor_copy(list_f[:, 32:33], upto[:, 95:96]))
            do.tell(v.tensor_copy(lists[:, 0:33], list_f[:, 0:33]), "lists_ready")

            iota = const("iota")

            def pick_gather(e, at, done):
                for t in range(NT):
                    ins_ = v.tensor_scalar(sel_g[:, t, :], iota[:, at], rank[:, t, bass.ds(e, 1)], None, ALU.is_equal)
                    if t:
                        ins_.then_inc(done, 1)

            def pick_scatter(e, at, done):
                for t in range(NT):
                    ins_ = v.tensor_scalar(sel_s[:, t, :], iota[:, at], rank[:, t, bass.ds(e, 1)],
                                           gates[:, t, bass.ds(e, 1)], ALU.is_equal, ALU.mult)
                    if t and done is not None:
                        ins_.then_inc(done, 1)

            def pick_bias(e, done):
                v.tensor_scalar(sel_b, ones[0:96, 0:CAP], const("pick", 96)[:, bass.ds(e, 1)], None,
                                ALU.mult).then_inc(done, 1)

            def keep_x(done):
                a = VEC_ROWS["g_ffn_norm"][0]
                v.tensor_tensor(xg, bank(2).rearrange("p (k s) -> p k s", k=KD),
                                vcol[:, a:a + KD].unsqueeze(2).to_broadcast([P, KD, CAP]), ALU.mult).then_inc(done, 1)

            def gate_up(clipped, n, up_done, up_n):
                v.tensor_scalar(g_min, bank(0), LIMIT, None, ALU.min).then_inc(clipped, 1)
                v.tensor_scalar(u_clip, bank(1), -LIMIT, LIMIT, ALU.max, ALU.min).then_inc(up_done, 1)
                dve.wait_ge(clipped, n)
                dve.wait_ge(up_done, up_n)
                v.scalar_tensor_tensor(out=u_clip, in0=u_clip, scalar=1.0, in1=g_min, op0=ALU.add,
                                       op1=ALU.mult).then_inc(up_done, 1)

            dve.wait_ge(sig["gates_kept"], 1)
            pick_gather(0, slice(0, CAP), sig["picked"])
            pick_bias(0, sig["selb_ready"])
            dve.wait_ge(sig["gathered"], 1)
            keep_x(sig["xg_ready"])
            with dve.Fori(0, EXPERTS) as e:
                pick_scatter(e, slice(0, P), sig["sel_ready"])
                pick_gather(e + 1, slice(0, CAP), sig["picked"])
                dve.wait_ge(chunk_used, e * SLOTS + (N_MOE + KD))
                gate_up(sig["clipped"], e + 1, sig["up_steps"], e * 2 + 1)
                pick_bias(e + 1, sig["selb_ready"])
                dve.wait_ge(sig["up_steps"], e * 2 + 2)
                dve.wait_ge(sig["sig_ready"], e + 1)
                v.tensor_tensor(act_buf, u_clip, sg, ALU.mult).then_inc(sig["act_ready"], 1)
                dve.wait_ge(sig["gathered"], e + 2)
                keep_x(sig["xg_ready"])
                dve.wait_ge(sig["xg_ready"], e + 2)
            n_over = dve.value_load(lists[0:1, 32:33], min_val=0, max_val=16)
            with dve.If(n_over > 0):
                with dve.Fori(0, OVER) as j:
                    with dve.If(j < n_over):
                        e = dve.value_load(lists[0:1, bass.ds(j, 1)], min_val=0, max_val=EXPERTS - 1)
                        b = dve.value_load(lists[0:1, bass.ds(j + 16, 1)], min_val=0, max_val=PASSES - 1)
                        dve.wait_ge(sig["o_scattered"], j + 1)
                        pick_scatter(e, bass.ds(b * P, P), sig["o_steps"])
                        pick_gather(e, bass.ds(b * P, CAP), sig["o_steps"])
                        pick_bias(e, sig["o_picked"])
                        dve.wait_ge(sig["o_gathered"], j + 1)
                        keep_x(sig["o_xg"])
                        dve.wait_ge(sig["o_gu"], j + 1)
                        gate_up(sig["o_clipped"], j + 1, sig["o_up_steps"], j * 2 + 1)
                        dve.wait_ge(sig["o_up_steps"], j * 2 + 2)
                        dve.wait_ge(sig["o_sig"], j + 1)
                        v.tensor_tensor(act_buf, u_clip, sg, ALU.mult).then_inc(sig["o_act"], 1)

            dve.wait_ge(sig["moe_done"], 1)
            for i in range(4):
                t, h = divmod(i, 2)
                xs = x_sb[:, t, h * 512:(h + 1) * 512]
                do.step(v.tensor_tensor(xs, bank(4 + i), xs, ALU.add))
            st = stat(ms, S_FINAL)
            for t in range(NT):
                do.step(v.tensor_tensor_reduce(out=rows[:, t, :], in0=x_sb[:, t, :], in1=x_sb[:, t, :], scale=1.0,
                                               scalar=0.0, op0=ALU.mult, op1=ALU.add, accum_out=st[:, t:t + 1]))
            r_ = rstd(S_FINAL, D)
            dve.wait_ge(sig["gfin_in"], 16)
            for t in range(NT):
                do.step(v.scalar_tensor_tensor(out=x_sb[:, t, :], in0=x_sb[:, t, :], scalar=r_[:, t:t + 1],
                                               in1=gfin[:, :], op0=ALU.mult, op1=ALU.mult))

            scaled(S_NORM1, lambda t: x_sb[:, t, :], lambda t: rows[:, t, :], D, "rows_ready")
            keep_cols(lambda k: modg[:, k:k + 1], lambda k: modc[:, k:k + 1])
            do.step(v.memset(conv_x[:, :, 0:3], 0.0))
            dve.wait_ge(sig["proj_kept"], len(IN1_CHUNKS) + IN2_GATES)
            dve.wait_ge(sig["bias14_in"], 48)

            def bias_of(a, n):
                return bias14[:, a:a + n].unsqueeze(1).to_broadcast([P, NT, n])

            do.step(v.tensor_tensor(fg[:, :, 0:6], proj[:, :, C_FF:C_FF + FOX], bias_of(0, 6), ALU.add))
            do.step(v.tensor_tensor(fg[:, :, 6:10], proj[:, :, C_MF:C_MF + ML], bias_of(6, 4), ALU.add))
            do.step(v.tensor_tensor(bias_c[:, :, 12:16], proj[:, :, C_MI:C_MI + ML], bias_of(10, 4), ALU.add))
            do.tell(v.scalar_tensor_tensor(out=logf, in0=fg, scalar=-1.0, in1=fg, op0=ALU.mult, op1=ALU.min), "ff_ready")
            dve.wait_ge(sig["ff_ln"], 1)
            do.step(v.tensor_scalar(fg, fg, 0.0, None, ALU.min))
            do.tell(v.tensor_tensor(logf, fg, logf, ALU.subtract), "decay_ready")
            st = stat(ms, S_HEADS)
            for n in range(4):
                dve.wait_ge(sig["qk_sq"], n + 1)
                do.tell(v.tensor_reduce(st[:, 12 * n:12 * n + 12], sq_buf[n % 2].rearrange("p (h d) -> p h d", h=12),
                                        AX.X, ALU.add), "sq_used")
            r_ = rstd(S_HEADS, HD)
            for n in range(4):
                i, t = divmod(n, 2)
                c = (C_FQ, C_BQ)[i]
                view = proj[:, t, c:c + 768].rearrange("p (h d) -> p h d", h=12)
                do.tell(v.tensor_tensor(view, view, r_[:, 12 * n:12 * n + 12].unsqueeze(2).to_broadcast([P, 12, HD]),
                                        ALU.mult), "heads_ready")
            dve.wait_ge(sig["cum_done"], 1)
            for t in range(NT):
                do.step(v.tensor_copy(cum[:, t, :], bank(6)[:, 16 * t:16 * t + 10]))
            do.step(v.tensor_scalar(bias_c[:, :, 0:FOX], cum[:, :, 0:FOX], -float(HD) ** 0.5, None, ALU.mult))
            do.step(v.tensor_copy(bias_c[:, :, FOX:SOFT], const("slope").rearrange("p (t h) -> p t h", t=NT)))
            do.tell(v.tensor_tensor(bias_c[:, :, 12:16], bias_c[:, :, 12:16], cum[:, :, 6:10], ALU.subtract),
                    "cum_kept")
            dve.wait_ge(sig["conv_in"], 2)
            for c in range(4):
                dst = qk[:, 12 + c, :]
                for j in range(CONV):
                    w_ = col("ml_conv_w_2", 4 * j + c)
                    src = conv_x[:, c, j:j + T]
                    if j == 0:
                        do.step(v.tensor_scalar(dst, src, w_, None, ALU.mult))
                        continue
                    ins_ = v.scalar_tensor_tensor(out=dst, in0=src, scalar=w_, in1=dst, op0=ALU.mult, op1=ALU.add)
                    if j == CONV - 1:
                        do.tell(ins_, "conv_sum")
                    else:
                        do.step(ins_)
            dve.wait_ge(sig["cumt_turned"], 1)
            do.tell(v.tensor_copy(bias_r, bank(7)[0:16, 0:T]), "bias_rows")
            attention(2)
            y_ml = rows[:, :, 384:640].rearrange("p t (h d) -> p t h d", h=ML)
            ml_sq = probs_flat[:, 0:512].rearrange("p (t h d) -> p t h d", t=NT, h=ML)
            st, r_ = (stat(x_, S_ML).rearrange("p (t h) -> p t h", t=NT) for x_ in (ms, rs))
            dve.wait_ge(sig["probs_turned"], HEADS + SOFT + ML)
            for t in range(NT):
                do.step(v.tensor_tensor(ml_sq[:, t], y_ml[:, t], y_ml[:, t], ALU.mult))
                do.step(v.tensor_reduce(st[:, t, :], ml_sq[:, t], AX.X, ALU.add))
            rstd(S_ML, HD)
            dve.wait_ge(sig["ml_sig"], 1)
            for t in range(NT):
                do.step(v.tensor_tensor(y_ml[:, t], y_ml[:, t], r_[:, t, :].unsqueeze(2).to_broadcast([P, ML, HD]),
                                        ALU.mult))
            do.tell(v.tensor_tensor(rows[:, :, 384:640], rows[:, :, 384:640], proj[:, :, C_MO:C_MO + 256], ALU.mult),
                    "rows_ready")
            keep_cols(lambda k: col("ml_h_g_2", 0) if k == 3 else 1.0)

            def add_gated(base, tell):
                for i in range(4):
                    t, h = divmod(i, 2)
                    g_, xs = gate_b[:, h * 512:(h + 1) * 512], x_sb[:, t, h * 512:(h + 1) * 512]
                    tmp = rows[:, t, h * 512:(h + 1) * 512]
                    do.step(v.tensor_tensor(tmp, bank(base + i), g_, ALU.mult))
                    ins_ = v.tensor_tensor(xs, xs, tmp, ALU.add)
                    if tell == "out_ready" or i == 3:
                        do.tell(ins_, tell)
                    else:
                        do.step(ins_)

            dve.wait_ge(chunk_used, N_OUT2 + 4)
            dve.wait_ge(sig["bcast_kept"], 1)
            add_gated(0, "gate_used")
            scaled(S_NORM2, lambda t: x_sb[:, t, :], lambda t: rows[:, t, :], D, "rows_ready")
            keep_cols(lambda k: modg[:, 8 + k:9 + k], lambda k: modc[:, 24 + k:25 + k])
            dve.wait_ge(sig["rows_turned"], 20)
            for j in range(PAIRS):
                dve.wait_ge(sig["silu_ready"], j + 1)
                dve.wait_ge(chunk_used, N_GU2 + 2 * j + 2)
                if j >= 2:
                    dve.wait_ge(sig["h_turned"], j - 1)
                do.tell(v.tensor_tensor(h_rows[:, j % 2, :], h_sil[:, j % 2, :], bank(5 + 2 * (j % 2)), ALU.mult),
                        "h_ready")
            dve.wait_ge(sig["bcast_kept"], 2)
            dve.wait_ge(sig["h_turned"], PAIRS)
            dve.wait_ge(chunk_used, N_END)
            add_gated(4, "out_ready")

        @block.gpsimd
        def _(pool):
            pool.wait_ge(sig["bgu_in"], 48)
            nc.gpsimd.memset(zero_k, 0.0)
            steps = 0
            for lo, hi, rest in ((0, 96, True), (32, 64, False), (64, 96, True), (64, 96, False)):
                nc.gpsimd.tensor_copy(bias_b[lo:hi, :], bgu_f[lo:hi, :]).then_inc(sig["pool_steps"], 1)
                steps += 1
                pool.wait_ge(sig["pool_steps"], steps)
                if rest:
                    nc.gpsimd.tensor_tensor(bgu_f[lo:hi, :], bgu_f[lo:hi, :], bias_b[lo:hi, :],
                                            ALU.subtract).then_inc(sig["pool_steps"], 1)
                    steps += 1
                    pool.wait_ge(sig["pool_steps"], steps)
            nc.gpsimd.memset(pool_nop[:, :], 0.0).then_inc(sig["bias_split"], 1)


_INS = ["x", "positions", "g_attn_norm", "w_in", "w_pool", "b_pool", "pool_scale", "g_q_a", "w_q_b", "g_kv_a", "w_kv_b",
        "g_out_pool", "g_out_attn", "w_out", "g_ffn_norm", "w_router", "b_router", "w_gate_up", "b_gate_up", "w_down",
        "b_down", "g_final", "c_2", "w_ada_2", "b_ada_2", "norm1_g_2", "norm2_g_2", "w_in_2", "fox_f_bias_2",
        "fox_q_g_2", "fox_k_g_2", "ml_conv_w_2", "ml_conv_b_2", "ml_i_bias_2", "ml_f_bias_2", "ml_h_g_2",
        "moba_q_g_2", "moba_k_g_2", "w_out_2", "w_gate_up_2", "w_down_2"]


def shape_constants():
    import numpy as np

    c = np.zeros((P, NCONST), np.float32)

    def put(name, a):
        at, n = CONST[name]
        c[:np.shape(a)[0], at:at + n] = a

    i = np.arange(P)
    put("ident", np.eye(P))
    put("ones", np.ones((P, P)))
    put("tri_inc", i[:, None] <= i[None, :])
    put("tri_exc", i[:, None] < i[None, :])
    put("mask", np.where(i[None, :] <= i[:, None], 0.0, NEG))
    put("iota", np.tile((np.arange(PASSES)[:, None] * CAP + i[None, :] % CAP).reshape(1, -1), (P, 1)))
    slopes = np.float32(2.0) ** (np.float32(-8.0) * np.arange(1, MOBA + 1, dtype=np.float32) / np.float32(MOBA))
    tok = np.arange(NT)[None, :, None] * P + i[:, None, None]
    put("slope", (tok * slopes[None, None, :] * np.float32(HD ** 0.5)).reshape(P, -1))
    put("inv", np.tile((np.float32(10000.0) ** (-np.arange(HALF, dtype=np.float32) / np.float32(HALF)))[None], (P, 1)))
    j = np.arange(96)
    put("pass_expert", (j % EXPERTS)[None])
    put("pass_block", (j // EXPERTS + 1)[None])
    put("pass_floor", ((j // EXPERTS + 1) * CAP)[None])
    put("pass_rank", np.arange(1, 17)[None])
    put("pick", (i[:, None] % EXPERTS == np.arange(EXPERTS + 1)[None, :]) & (np.arange(EXPERTS + 1)[None, :] < EXPERTS))
    t = np.arange(T)
    band = np.zeros((T, GROUPS, T), np.float32)
    for g, w in enumerate(WINDOWS):
        inside = (t[:, None] <= t[None, :]) & (t[:, None] > t[None, :] - w)
        band[:, g, :] = inside / np.minimum(t + 1, w)[None, :].astype(np.float32) - np.eye(T)
    band = band.reshape(NT, P, GROUPS, T).transpose(1, 2, 0, 3)
    return c, np.ascontiguousarray(band)


def kernel(**inputs):
    import numpy as _np
    import concourse.bacc as _bacc
    from concourse import mybir as _mybir
    from concourse.bass_utils import run_bass_kernel_spmd as _run

    nc = _bacc.Bacc("TRN2", target_bir_lowering=False, num_devices=1)
    arrays, aps = {}, {}
    consts, band = shape_constants()
    for name in _INS + ["consts", "band"]:
        a = consts if name == "consts" else band if name == "band" else _np.ascontiguousarray(inputs[name])
        arrays[f"in_{name}_dram"] = a
        aps[name] = nc.dram_tensor(f"in_{name}_dram", a.shape, _mybir.dt.from_np(a.dtype), kind="ExternalInput").ap()
    out = nc.dram_tensor("out_0_dram", (1, T, D), _mybir.dt.float32, kind="ExternalOutput").ap()
    two_blocks(nc, aps, aps.pop("consts"), aps.pop("band"), out)
    r = _run(nc, [arrays], core_ids=[0])
    return r.results[0]["out_0_dram"]
```

```python
from contextlib import ExitStack

import concourse.bass as bass
from concourse import mybir

F32 = mybir.dt.float32
BF16 = mybir.dt.bfloat16
I32 = mybir.dt.int32
ALU = mybir.AluOpType
ACT = mybir.ActivationFunctionType
AX = mybir.AxisListType

P = 128
D = 1024
T = 256
NT = T // P
KD = D // P
EPS = 1e-6
INV_2PI = 0.15915494309189535
TWO_PI = (6.28125, 1.93500518798828125e-3, 3.0199159795074593e-07)
PI_IN, HALF_PI = 3.1415925, 1.5707963267948966
RSQRT_GUESS = float(0x5F3759DF)
ROUND = 12582912.0
NEG = -1.0e30
BIG = 3.0e38

D_POOL, GROUPS = 512, 4
WINDOWS = (2, 4, 8, 16)
Q_LORA, KV_LORA, ROPE, NOPE, VDIM, HEADS = 256, 128, 32, 64, 64, 8
HALF = ROPE // 2
QK = NOPE + ROPE
IN1 = D_POOL + Q_LORA + KV_LORA + ROPE
EXPERTS, TOPK, FE = 32, 4, 1024
LIMIT, ALPHA = 7.0, 1.702
CAP = 64
PASSES = T // CAP
OVER = NT * P * TOPK // (CAP + 1)

HD = 64
FOX, ML, MOBA = 6, 4, 6
SOFT = FOX + MOBA
C_FQ, C_FK, C_FV, C_FF = 0, 384, 768, 1152
C_MQ, C_MK, C_MV, C_MI, C_MF, C_MO = 1158, 1414, 1670, 1926, 1930, 1934
C_BQ, C_BK, C_BV, IN2 = 2190, 2574, 2958, 3342
CONV = 4
D_FF = 2816
FT = D_FF // P

SLOTS, SLOT = 12, 2048
CW = SLOT // KD


def split(n, w):
    return [(a, min(w, n - a)) for a in range(0, n, w)]


IN1_CHUNKS = sorted(split(IN1, CW), key=lambda c: (c[0] < D_POOL, c[0]))
IN2_CHUNKS = split(IN2, CW)
IN2_GATES = C_MO // CW + 1
ADA_CHUNKS = [(g, k) for g in range(3) for k in range(KD)]
PAIRS = D_FF // CW

ADA_FIRST, ADA_MID = 2, 18
N_IN1 = ADA_FIRST
N_QB = N_IN1 + len(IN1_CHUNKS)
N_KVB = N_QB + 1
N_OUT1 = N_KVB + 1 + ADA_MID - ADA_FIRST
N_MOE = N_OUT1 + 4 + len(ADA_CHUNKS) - ADA_MID
N_IN2 = N_MOE + EXPERTS * SLOTS
N_OUT2 = N_IN2 + len(IN2_CHUNKS)
N_GU2 = N_OUT2 + 4
N_DN2 = N_GU2 + 2 * PAIRS
N_END = N_DN2 + FT // 2



def ada_at(i):
    return i if i < ADA_FIRST else N_KVB + 1 + i - ADA_FIRST if i < ADA_MID else N_OUT1 + 4 + i - ADA_MID


ADA_OF = {ada_at(i): gk for i, gk in enumerate(ADA_CHUNKS)}

VEC_ROWS = {}
_at = 0
for _name, _n in (("c_2", 8), ("g_attn_norm", 8), ("g_q_a", 2), ("g_kv_a", 1), ("pool_scale", 4), ("b_pool", 4),
                  ("g_out_pool", 4), ("norm1_g_2", 8), ("norm2_g_2", 8), ("g_ffn_norm", 8), ("g_out_attn", 4), ("ml_conv_w_2", 16), ("ml_conv_b_2", 4), ("ml_h_g_2", 2),
                  ("fox_q_g_2", 1), ("fox_k_g_2", 1), ("moba_q_g_2", 1), ("moba_k_g_2", 1)):
    VEC_ROWS[_name] = (_at, _n)
    _at += _n
NVEC = _at
VEC_FIRST = list(VEC_ROWS)[:7]
NVEC_FIRST = VEC_ROWS["norm1_g_2"][0]

CONST = {}
VEC_DMAS = len(VEC_ROWS) - len(VEC_FIRST) + 4
_at = 0
for _name, _n in (("ident", P), ("ones", P), ("tri_inc", P), ("tri_exc", P), ("mask", P), ("iota", PASSES * P),
                  ("slope", NT * MOBA), ("inv", HALF), ("pass_expert", 96), ("pass_block", 96), ("pass_floor", 96),
                  ("pass_rank", 16), ("pick", EXPERTS + 1)):
    CONST[_name] = (_at, _n)
    _at += _n
NCONST = _at
CONST_FIRST = 2 * P

STAT_W = (2, 4, 4, 2, 2, 2, 48, 8, 2)
STAT_AT = [sum(STAT_W[:i]) for i in range(len(STAT_W))]
NSTAT = sum(STAT_W)
S_ATTN, S_LAT, S_MIX, S_FFN, S_FINAL, S_NORM1, S_HEADS, S_ML, S_NORM2 = range(9)

SIGNALS = """x0_in x1_in const_in const2_in band_in vec_in vec2_in pos_in wpool_in bias14_in gfin_in bada_in bgu_in bdown_in router_in
brouter_in bf_const vec_turned vec_cols vec2_turned vec2_cols c_ready rows_ready rows_turned cols_dve cols_act proj_kept
lat_rows lat_turned lat_cols qkv_kept trig_arg trig_ready q_roped k_roped qk_turned q_cols k_cols
diff_done diff_kept mixed_done pooled_kept pool_sq pool_sum pool_cols ada_kept mod_turned mod_cols
out_half x_added scores_done rowmax_ready probs_ready smat_ready probs_turned pt_kept pv_done o_free att_rows att_turned att_cols
pool_steps up_steps o_up_steps o_steps logits_done shifted exp_ready routed ranks_done ranks_kept
lists_ready bias_split
picked sel_ready selb_ready seld_ready gathered xg_ready clipped sig_ready act_ready act_turned actt_ready yb_ready
sel_turned selt_ready scattered
o_loaded o_picked o_gathered o_xg o_gu o_clipped o_sig o_act o_act_turned o_actt o_down o_yb o_sel_turned
o_selt o_scattered o_ring_back
moe_done ff_ready ff_ln decay_ready cum_done cum_kept cumt_turned bias_rows conv_in conv_turned
conv_sum conv_silu qk_sq sq_used heads_ready heads_turned heads_cols ml_exp ml_m ml_guard ml_sig
bcast_done bcast_kept gate_used silu_ready h_ready h_turned h_cols out_ready out_stored""".split()


class Steps:

    def __init__(self, eng, own, signals):
        self.eng, self.own, self.signals, self.n, self.told = eng, own, signals, 0, {}

    def step(self, ins):
        self.n += 1
        ins.then_inc(self.own, 1)
        self.eng.wait_ge(self.own, self.n)

    def tell(self, ins, name):
        self.told[name] = self.told.get(name, 0) + 1
        ins.then_inc(self.signals[name], 1)
        self.eng.wait_ge(self.signals[name], self.told[name])


def two_blocks(nc, ins, consts, band, out):
    with ExitStack() as ctx:
        def sb(name, shape, dt=F32):
            return ctx.enter_context(nc.sbuf_tensor(name, shape, dt))

        def sem(name):
            return ctx.enter_context(nc.semaphore(name))

        ring = sb("ring", [P, SLOTS, SLOT])
        x_sb = sb("x_sb", [P, NT, D])
        rows = sb("rows", [P, NT, D])
        cols = sb("cols", [P, KD, T])
        work = sb("work", [P, 7488])
        qk = sb("qk", [P, 16, T])
        probs = sb("probs", [P, 2, 384])
        probs_flat = probs[:, :, :].rearrange("p a b -> p (a b)")
        pt = sb("pt", [P, 2, 384])
        mod = sb("mod", [P, 3, 512])
        gfin = sb("gfin", [P, D])
        gate_b = sb("gate_b", [P, D])
        bdown_b = sb("bdown_b", [96, D], BF16)
        cst = sb("cst", [P, NCONST])
        vec = sb("vec", [NVEC, P])
        vcol = sb("vcol", [P, NVEC])
        modc = sb("modc", [P, 48])
        modg = sb("modg", [P, 16])
        c_rep = sb("c_rep", [P, KD, 32])
        wide = sb("wide", [P, 1036])
        router = sb("router", [P, KD, EXPERTS])
        wpool = sb("wpool", [P, GROUPS, P])
        maskb = sb("maskb", [P, P], BF16)
        identb = sb("identb", [P, P], BF16)
        ms = sb("ms", [P, NSTAT])
        rs = sb("rs", [P, NSTAT])
        rsqrt_tmp = sb("rsqrt_tmp", [P, 48])
        rmax = sb("rmax", [P, 16, NT])
        nmax = sb("nmax", [P, 16, NT])
        psum_row = sb("psum_row", [P, 16, NT])
        rank = sb("rank", [P, NT, EXPERTS + 1])
        gates = sb("gates", [P, NT, EXPERTS + 1])
        pos_i = sb("pos_i", [P, NT], I32)
        lists = sb("lists", [1, 36], I32)
        den_all = sb("den_all", [P, 16, NT])
        brouter = sb("brouter", [P, EXPERTS])
        bias14 = sb("bias14", [P, 14])
        trig = sb("trig", [P, 2, NT, HALF])
        PS = ctx.enter_context(nc.psum_tensor("PS", [P, 8, 512], F32))

        sig = {name: sem(name) for name in SIGNALS}
        landed = [sem(f"slot{i}_landed") for i in range(SLOTS)]
        chunk_used = sem("chunk_used")
        dve_own, act_own = sem("dve_order"), sem("act_order")

        def const(name, parts=P):
            a, n = CONST[name]
            return cst[0:parts, a:a + n]

        def col(name, i=0):
            return vcol[:, VEC_ROWS[name][0] + i:VEC_ROWS[name][0] + i + 1]

        def stat(tile, request):
            return tile[:, STAT_AT[request]:STAT_AT[request] + STAT_W[request]]

        ident, ones = const("ident"), const("ones")

        proj1 = work[:, 0:NT * IN1].rearrange("p (t n) -> p t n", t=NT)
        b_at = NT * IN1
        band_sb = work[:, b_at:b_at + 2048].rearrange("p (g s t) -> p g s t", g=GROUPS, s=NT)
        q_rows = work[:, b_at + 2048:b_at + 3584].rearrange("p (t h n) -> p t h n", t=NT, h=HEADS)
        kv_rows = work[:, b_at + 3584:b_at + 5632].rearrange("p (t h n) -> p t h n", t=NT, h=HEADS)
        k_rows = rows[:, :, 0:HEADS * QK].rearrange("p t (h n) -> p t h n", h=HEADS)
        lat_rows = pt[:, :, 0:384]
        lat = cols[:, 0:3, :]
        diff = work[:, b_at:b_at + 1024].rearrange("p (g t) -> p g t", g=GROUPS)
        pooled = work[:, b_at + 1024:b_at + 2048].rearrange("p (g t) -> p g t", g=GROUPS)
        pool_sq = work[:, 0:1024].rearrange("p (g t) -> p g t", g=GROUPS)
        bgu_f = qk[0:96, 0:8, :].rearrange("p a b -> p (a b)")
        rope_area = qk[:, 8:12, :].rearrange("p a b -> p (a b)")
        rope_tmp = [rope_area[:, i * 256:(i + 1) * 256].rearrange("p (t h n) -> p t h n", t=NT, h=HEADS)
                    for i in range(4)]
        ang, turns = (rope_area[:, a:a + NT * HALF].rearrange("p (t n) -> p t n", t=NT) for a in (0, NT * HALF))
        att = rows[:, :, 0:512]
        sel_g = work[:, 0:128].rearrange("p (t s) -> p t s", t=NT)
        sel_s = work[:, 128:384].rearrange("p (t s) -> p t s", t=NT)
        sel_t = work[:, 384:640]
        xg = work[:, 640:1152].rearrange("p (k s) -> p k s", k=KD)
        g_min, act_buf, sg, act_t, yb = (work[:, a:a + 512] for a in range(1152, 1152 + 5 * 512, 512))
        u_clip = work[:, 3712:4224]
        sel_b = work[0:96, 4224:4256].bitcast(BF16)
        sel_d = work[0:96, 4256:4288].bitcast(BF16)
        lg = work[:, 6304:6376].rearrange("p (t e) -> p t e", t=NT)
        lr = work[:, 6376:6448].rearrange("p (t e) -> p t e", t=NT)
        top = work[:, 6448:6464].rearrange("p (t e) -> p t e", t=NT)
        chosen = work[:, 6464:6528].rearrange("p (t e) -> p t e", t=NT)
        gexp = work[:, 6528:6592].rearrange("p (t e) -> p t e", t=NT)
        small = work[:, 6592:6720]
        lr_row, list_f = work[0:1, 7296:7392], work[0:1, 7392:7440]
        list_eq, list_w = (qk[0:1, a:a + 6, :].rearrange("p a b -> p (a b)").rearrange("p (j i) -> p j i", j=16)
                           for a in (0, 6))
        bias_b = wide[0:96, 0:1024].bitcast(BF16)
        bdown_f = gate_b[0:96, :]
        proj = work[:, 0:NT * IN2].rearrange("p (t n) -> p t n", t=NT)
        tail = work[:, NT * IN2:7488]
        bias_r = tail[0:16, 0:T]
        bias_c = tail[:, 256:288].rearrange("p (t h) -> p t h", t=NT)
        logf, fg, cum = (tail[:, a:a + 20].rearrange("p (t h) -> p t h", t=NT) for a in (288, 308, 328))
        ml_e = tail[:, 348:732]
        guard, den = (tail[:, a:a + 8].rearrange("p (h t) -> p h t", t=NT) for a in (732, 740))
        rinv = tail[:, 748:764].rearrange("p (h t) -> p h t", t=NT)
        sq_buf = [rows[:, b, 0:768] for b in range(2)]
        conv_x = wide[:, :].rearrange("p (c t) -> p c t", c=CONV)
        h_t = work[:, 0:FT * T].rearrange("p (f t) -> p f t", f=FT)
        h_sil = work[:, FT * T:FT * T + 1024].rearrange("p (b n) -> p b n", b=2)
        h_rows = rows[:, :, 0:512]

        def slot(n):
            return ring[:, n % SLOTS, :]

        def bank(b):
            return PS[:, b, :]

        def by_rows(w, r0, n_cols, tiles):
            return w[r0:r0 + tiles * P, :].rearrange("(k p) n -> p k n", p=P)

        def chunk_source(n):
            if n in ADA_OF:
                g, k = ADA_OF[n]
                return ins["w_ada_2"][0][k * P:(k + 1) * P, g * SLOT:(g + 1) * SLOT].rearrange(
                    "(k p) n -> p k n", p=P), 1, SLOT
            if n < N_QB:
                a, w = IN1_CHUNKS[n - N_IN1]
                return ins["w_in"][0][:, a:a + w].rearrange("(k p) n -> p k n", p=P), KD, w
            if n == N_QB:
                return ins["w_q_b"][0].rearrange("(k p) n -> p k n", p=P), 2, HEADS * QK
            if n == N_KVB:
                return ins["w_kv_b"][0].rearrange("(k p) n -> p k n", p=P), 1, 1024
            if n < N_MOE:
                return by_rows(ins["w_out"][0], (n - N_OUT1) * 2 * P, D, 2), 2, D
            n_ = n
            if n_ < N_OUT2:
                a, w = IN2_CHUNKS[n_ - N_IN2]
                return ins["w_in_2"][0][:, a:a + w].rearrange("(k p) n -> p k n", p=P), KD, w
            if n_ < N_GU2:
                return by_rows(ins["w_out_2"][0], (n_ - N_OUT2) * 2 * P, D, 2), 2, D
            if n_ < N_DN2:
                j, up = divmod(n_ - N_GU2, 2)
                a = up * D_FF + j * CW
                return ins["w_gate_up_2"][0][:, a:a + CW].rearrange("(k p) n -> p k n", p=P), KD, CW
            return by_rows(ins["w_down_2"][0], (n_ - N_DN2) * 2 * P, D, 2), 2, D

        def chunk(n):
            _, k, w = chunk_source(n)
            return slot(n)[:, 0:k * w].rearrange("p (k n) -> p k n", k=k)

        gu_dram = ins["w_gate_up"][0].rearrange("e (k p) n -> (e k) p n", p=P)
        dn_dram = ins["w_down"][0].rearrange("e (s k p) n -> (e s) p k n", p=P, k=2)

        heads2 = [(h // 2, 3 + h // 2, HD * (h % 2), C_FV + HD * h, h) for h in range(FOX)]
        heads2 += [(6 + h // 2, 9 + h // 2, HD * (h % 2), C_BV + HD * h, FOX + h) for h in range(MOBA)]
        heads2 += [(12 + h // 2, 14 + h // 2, HD * (h % 2), C_MV + HD * h, SOFT + h) for h in range(ML)]

        def attention_heads(block_no):
            if block_no == 1:
                for h in range(HEADS):
                    yield (h, qk[0:QK, h, :], qk[0:QK, 8 + h, :],
                           lambda kt, h=h: kv_rows[:, kt, h, NOPE:NOPE + VDIM], None, False, h * VDIM)
            else:
                for i, (qt, kt_, base, v, row) in enumerate(heads2):
                    first = 0 if i < FOX else FOX if i < SOFT else SOFT
                    yield (HEADS + i, qk[base:base + HD, qt, :], qk[base:base + HD, kt_, :],
                           lambda kt, v=v: proj[:, kt, v:v + HD], row, i >= SOFT, (i - first) * HD)

        def scores_used(eng, g):
            if g < HEADS + SOFT:
                eng.wait_ge(sig["probs_ready"], g + 1)
            else:
                eng.wait_ge(sig["smat_ready"], g + 1 - HEADS - SOFT)

        GROUP_OF = {1: [(0, HEADS)], 2: [(0, FOX), (FOX, SOFT), (SOFT, SOFT + ML)]}
        ATT_SCALE = {1: float(QK) ** -0.5, 2: float(HD) ** -0.5}

        block = ctx.enter_context(nc.Block())

        @block.sync
        def _(sp):
            def load(n):
                src, k, w = chunk_source(n)
                if n >= SLOTS:
                    sp.wait_ge(chunk_used, n - SLOTS + 1)
                dst = slot(n)[:, 0:k * w].rearrange("p (k n) -> p k n", k=k)
                sp.dma_start(dst, src).then_inc(landed[n % SLOTS], 16)

            def load_small(dst, src, name, **kw):
                sp.dma_start(dst, src, **kw).then_inc(sig[name], 16)

            x_rows = ins["x"][0].rearrange("(t p) n -> p t n", p=P)
            load_small(x_sb[:, 0, :], x_rows[:, 0, :], "x0_in")
            load_small(x_sb[:, 1, :], x_rows[:, 1, :], "x1_in")
            load_small(cst[:, 0:CONST_FIRST], consts[:, 0:CONST_FIRST], "const_in")
            for n in range(SLOTS):
                load(n)
                if n == 2:
                    load_small(cst[:, CONST_FIRST:NCONST], consts[:, CONST_FIRST:NCONST], "const2_in")
                    load_small(pos_i[:, :], ins["positions"][0].rearrange("(t p) -> p t", p=P), "pos_in",
                          allow_slow_non_contiguous=True)
                if n == 3:
                    for i in range(3):
                        load_small(bgu_f[32 * i:32 * i + 32, :], ins["b_gate_up"][0], "bgu_in")
                if n == 5:
                    load_small(band_sb, band, "band_in")
                if n == 7:
                    load_small(wpool[:, :, :], ins["w_pool"][0].rearrange("g c d -> c g d"), "wpool_in")
                if n == 8:
                    for j in range(4):
                        load_small(mod[32 * j:32 * j + 32, :, :],
                              ins["b_ada_2"][0].rearrange("(g j n) -> j g n", g=3, j=4)[j].partition_broadcast(32),
                              "bada_in")
            for name, (at, n) in VEC_ROWS.items():
                src = ins[name]
                if name in VEC_FIRST:
                    continue
                if name in ("fox_q_g_2", "fox_k_g_2", "moba_q_g_2", "moba_k_g_2"):
                    load_small(vec[at:at + 1, 0:HD], src, "vec2_in")
                    load_small(vec[at:at + 1, HD:P], src, "vec2_in")
                elif name == "ml_conv_w_2":
                    load_small(vec[at:at + n, :], src[0].rearrange("j (c p) -> (j c) p", p=P), "vec2_in")
                else:
                    load_small(vec[at:at + n, :], src.rearrange("o (k p) -> (o k) p", p=P), "vec2_in")
            for n in range(SLOTS, N_MOE):
                load(n)
                if n == SLOTS:
                    for i in range(3):
                        load_small(bdown_f[32 * i:32 * i + 32, :], ins["b_down"][0], "bdown_in")
                if n == SLOTS + 2:
                    load_small(router[:, :, :], ins["w_router"][0].rearrange("(k p) e -> p k e", p=P), "router_in")
                    load_small(brouter[:, :], ins["b_router"][0].partition_broadcast(P), "brouter_in")
                if n == N_OUT1:
                    load_small(gfin[:, :], ins["g_final"].partition_broadcast(P), "gfin_in")
                    load_small(bias14[:, 0:6], ins["fox_f_bias_2"][0].partition_broadcast(P), "bias14_in")
                    load_small(bias14[:, 6:10], ins["ml_f_bias_2"][0].partition_broadcast(P), "bias14_in")
                    load_small(bias14[:, 10:14], ins["ml_i_bias_2"][0].partition_broadcast(P), "bias14_in")
            with sp.Fori(0, EXPERTS) as e:
                for c in range(SLOTS):
                    s = (N_MOE + c) % SLOTS
                    sp.wait_ge(chunk_used, e * SLOTS + (N_MOE + c - SLOTS + 1))
                    if c < KD:
                        sp.dma_start(ring[:, s, :], gu_dram[bass.ds(e * KD + c, 1), :, :]
                                     .rearrange("o p n -> (o p) n")).then_inc(landed[s], 16)
                    else:
                        sp.dma_start(ring[:, s, :].rearrange("p (o k n) -> p o k n", o=1, k=2),
                                     dn_dram[bass.ds(e * 4 + (c - KD), 1), :, :, :]
                                     .rearrange("o p k n -> p o k n")).then_inc(landed[s], 16)
            sp.wait_ge(sig["lists_ready"], 1)
            n_over = sp.value_load(lists[0:1, 32:33], min_val=0, max_val=16)
            with sp.If(n_over > 0):
                sp.wait_ge(chunk_used, N_IN2)
                with sp.Fori(0, OVER) as j:
                    with sp.If(j < n_over):
                        e = sp.value_load(lists[0:1, bass.ds(j, 1)], min_val=0, max_val=EXPERTS - 1)
                        for c in range(SLOTS):
                            if c < KD:
                                sp.dma_start(ring[:, c, :], gu_dram[bass.ds(e * KD + c, 1), :, :]
                                             .rearrange("o p n -> (o p) n")).then_inc(sig["o_loaded"], 16)
                            else:
                                sp.dma_start(ring[:, c, :].rearrange("p (o k n) -> p o k n", o=1, k=2),
                                             dn_dram[bass.ds(e * 4 + (c - KD), 1), :, :, :]
                                             .rearrange("o p k n -> p o k n")).then_inc(sig["o_loaded"], 16)
                        sp.wait_ge(sig["o_down"], j + 1)
                        sp.sem_inc(sig["o_ring_back"], 1)
            for n in range(N_IN2, N_END):
                load(n)
            sp.wait_ge(sig["out_stored"], 16 * 4)

        @block.tensor
        def _(pe):
            def need(n):
                pe.wait_ge(landed[n % SLOTS], 16 * (n // SLOTS + 1))

            turned = [0]

            def turn_rows(wait_rows, by_tile=True):
                for t in range(NT):
                    pe.wait_ge(sig["rows_ready"], wait_rows - (NT - 1 - t if by_tile else 0))
                    for k in range(KD):
                        mm = pe.transpose(bank(k // 2)[:, (k % 2) * T + t * P:][:, 0:P],
                                          rows[:, t, k * P:(k + 1) * P], ident)
                        if t == NT - 1 and k % 2:
                            mm.then_inc(sig["rows_turned"], 1)
                turned[0] += 1

            def need_cols():
                pe.wait_ge(sig["cols_dve"], 4 * turned[0])
                pe.wait_ge(sig["cols_act"], 4 * turned[0])

            pe.wait_ge(sig["const_in"], 16)
            pe.wait_ge(sig["vec_in"], len(VEC_FIRST) * 16)
            pe.transpose(bank(6)[:, 0:NVEC_FIRST], vec[0:NVEC_FIRST, :],
                         ident[0:NVEC_FIRST, 0:NVEC_FIRST]).then_inc(sig["vec_turned"], 1)

            def ada(i):
                g, k = ADA_CHUNKS[i]
                if i == 0:
                    pe.wait_ge(sig["c_ready"], 1)
                elif k == 0:
                    pe.wait_ge(sig["ada_kept"], g)
                n = ada_at(i)
                need(n)
                for j in range(4):
                    mm = pe.matmul(bank(7)[32 * j:32 * j + 32, :], c_rep[:, k, :], slot(n)[:, j * 512:(j + 1) * 512],
                                   start=(k == 0), stop=(k == KD - 1))
                mm.then_inc(chunk_used, 1)

            for i in range(ADA_FIRST):
                ada(i)

            def project(chunks, base_n, banks, first):
                for c, (a, w) in enumerate(chunks):
                    n = base_n + c
                    b = banks[c % 2]
                    if c >= 2:
                        pe.wait_ge(sig["proj_kept"], first + c - 1)
                    need(n)
                    for t in range(NT):
                        for k in range(KD):
                            mm = pe.matmul(bank(b)[:, t * w:(t + 1) * w], cols[:, k, t * P:(t + 1) * P],
                                           chunk(n)[:, k, :], start=(k == 0), stop=(k == KD - 1))
                    mm.then_inc(chunk_used, 1)

            turn_rows(2)
            need_cols()
            project(IN1_CHUNKS, N_IN1, (4, 5), 0)

            pe.wait_ge(sig["lat_rows"], 4)
            for i in range(3):
                for t in range(NT):
                    mm = pe.transpose(bank(i // 2)[:, (i % 2) * T + t * P:][:, 0:P],
                                      lat_rows[:, t, i * P:(i + 1) * P], ident)
            mm.then_inc(sig["lat_turned"], 1)
            pe.wait_ge(sig["proj_kept"], len(IN1_CHUNKS))
            pe.wait_ge(sig["lat_cols"], 1)
            need(N_QB)
            for b, t, at, a, w in ((4, 0, 0, 0, 512), (5, 1, 0, 0, 512), (6, 0, 0, 512, 256), (6, 1, 256, 512, 256)):
                for k in range(2):
                    mm = pe.matmul(bank(b)[:, at:at + w], lat[:, k, t * P:(t + 1) * P],
                                   chunk(N_QB)[:, k, a:a + w], start=(k == 0), stop=(k == 1))
            mm.then_inc(chunk_used, 1)
            need(N_KVB)
            for t in range(NT):
                if t:
                    pe.wait_ge(sig["qkv_kept"], 2)
                for a in (0, 512):
                    mm = pe.matmul(bank(4 * t + a // 512), lat[:, 2, t * P:(t + 1) * P],
                                   chunk(N_KVB)[:, 0, a:a + 512], start=True, stop=True)
            mm.then_inc(chunk_used, 1)
            pe.wait_ge(sig["band_in"], 16)
            for g in range(GROUPS):
                for s in range(NT):
                    mm = pe.matmul(bank(2 + g // 2)[:, (g % 2) * T:(g % 2 + 1) * T],
                                   proj1[:, s, g * P:(g + 1) * P], band_sb[:, g, s, :],
                                   start=(s == 0), stop=(s == NT - 1))
            mm.then_inc(sig["diff_done"], 1)

            def turn_heads(which, src, b):
                for h in (2 * b, 2 * b + 1):
                    for t in range(NT):
                        mm = pe.transpose(bank((0, 1, 4, 5)[b])[0:QK, (h % 2) * T + t * P:][:, 0:P],
                                          src[:, t, h, :], ident)
                mm.then_inc(sig["qk_turned"], 1)

            pe.wait_ge(sig["q_roped"], 1)
            pe.wait_ge(sig["qkv_kept"], 7)
            for b in range(4):
                turn_heads("q", q_rows, b)
            pe.wait_ge(sig["diff_kept"], 2)
            pe.wait_ge(sig["wpool_in"], 16)
            for g in range(GROUPS):
                mm = pe.matmul(bank(2 + g // 2)[:, (g % 2) * T:(g % 2 + 1) * T], wpool[:, g, :],
                               diff[:, g, :], start=True, stop=True)
            mm.then_inc(sig["mixed_done"], 1)
            pe.wait_ge(sig["k_roped"], 1)
            for b in range(4):
                pe.wait_ge(sig["q_cols"], b + 1)
                turn_heads("k", k_rows, b)
            pe.wait_ge(sig["vec2_in"], VEC_DMAS * 16)
            pe.transpose(bank(6)[:, 0:NVEC], vec[:, :], ident[0:NVEC, 0:NVEC]).then_inc(sig["vec2_turned"], 1)
            for i in range(ADA_FIRST, 6):
                ada(i)

            def pool_sums():
                pe.wait_ge(sig["pool_sq"], 1)
                pe.wait_ge(sig["vec2_cols"], 1)
                for t in range(NT):
                    for g in range(GROUPS):
                        mm = pe.matmul(bank(6)[:, t:t + 1], pool_sq[:, g, t * P:(t + 1) * P], ones[:, 0:1],
                                       start=(g == 0), stop=(g == GROUPS - 1))
                mm.then_inc(sig["pool_sum"], 1)

            def attention(block_no, extra=None):
                heads = list(attention_heads(block_no))
                for lo, hi in GROUP_OF[block_no]:
                    for i in range(lo, hi + 2):
                        if i < hi:
                            g, q, k, v, row, ml, _ = heads[i]
                            s = bank(g % 2)
                            if block_no == 2 and g == HEADS:
                                pe.wait_ge(sig["bias_rows"], 1)
                            if g >= 2:
                                scores_used(pe, g - 2)
                            for t in range(NT):
                                a, w = (0, P) if t == 0 else (P, T)
                                plain = ml or (row is None)
                                pe.matmul(s[:, a:a + w], q[:, t * P:(t + 1) * P], k[:, 0:w], start=True, stop=ml)
                                if ml:
                                    d = bank(6 + g % 2)
                                    pe.matmul(d[:, a:a + w], ident[0:16, row:row + 1].to_broadcast([16, P]),
                                              bias_r[:, 0:w], start=True, stop=False)
                                    mm = pe.matmul(d[:, t * T:t * T + P], identb[:, :], maskb[:, :], start=False, stop=True)
                                    continue
                                if not plain:
                                    pe.matmul(s[:, a:a + w], ident[0:16, row:row + 1].to_broadcast([16, P]),
                                              bias_r[:, 0:w], start=False, stop=False)
                                mm = pe.matmul(s[:, t * T:t * T + P], identb[:, :], maskb[:, :], start=False, stop=True)
                            mm.then_inc(sig["scores_done"], 1)
                            for other in (extra or {}).get(i, ()):
                                other()
                        if lo < i <= hi:
                            g = heads[i - 1][0]
                            scores_used(pe, g)
                            if g >= 2:
                                pe.wait_ge(sig["pt_kept"], g - 1)
                            elif g == 0:
                                pe.wait_ge(sig["pooled_kept"], 1)
                            for b in range(3):
                                mm = pe.transpose(bank(2 + g % 2)[:, b * P:(b + 1) * P],
                                                  probs[:, g % 2, b * P:(b + 1) * P], ident)
                            mm.then_inc(sig["probs_turned"], 1)
                        if i >= lo + 2:
                            g, _, _, v, _, _, oc = heads[i - 2]
                            pe.wait_ge(sig["pt_kept"], g + 1)
                            if i == lo + 2:
                                if g:
                                    pe.wait_ge(sig["o_free"], {HEADS: 1, HEADS + FOX: 2, HEADS + SOFT: 3}[g])
                            pe.matmul(bank(4)[:, oc:oc + HD], pt[:, g % 2, 0:P], v(0), start=True, stop=True)
                            pe.matmul(bank(5)[:, oc:oc + HD], pt[:, g % 2, P:2 * P], v(0), start=True, stop=False)
                            mm = pe.matmul(bank(5)[:, oc:oc + HD], pt[:, g % 2, 2 * P:3 * P], v(1),
                                           start=False, stop=True)
                            mm.then_inc(sig["pv_done"], 1)

            pe.wait_ge(sig["k_cols"], 4)

            def adas(lo, hi):
                return [lambda i=i: ada(i) for i in range(lo, hi)]

            attention(1, {0: adas(6, 8), 1: adas(8, 9), 2: [pool_sums] + adas(9, 10), 3: adas(10, 12), 4: adas(12, 14),
                          5: adas(14, 16), 6: adas(16, 17), 7: adas(17, ADA_MID)})

            def out_columns(base_n, c, k, t):
                for h in range(2):
                    mm = pe.matmul(bank(2 * t + h), cols[:, k, t * P:(t + 1) * P],
                                   chunk(base_n + c)[:, k % 2, h * 512:(h + 1) * 512],
                                   start=(k == 0), stop=(k == KD - 1))
                return mm

            def project_out_start(base_n):
                for c in range(2):
                    need(base_n + c)
                    for k in (2 * c, 2 * c + 1):
                        for t in range(NT):
                            mm = out_columns(base_n, c, k, t)
                    mm.then_inc(chunk_used, 1)

            def project_out_end(base_n):
                need(base_n + 2)
                need(base_n + 3)
                for t in range(NT):
                    for k in range(4, KD):
                        mm = out_columns(base_n, k // 2, k, t)
                        if t and k % 2:
                            mm.then_inc(chunk_used, 1)
                        elif k == KD - 1:
                            mm.then_inc(sig["out_half"], 1)

            pe.wait_ge(sig["pool_cols"], 4)
            project_out_start(N_OUT1)
            pe.wait_ge(sig["att_rows"], 2)
            for f in range(4):
                for t in range(NT):
                    mm = pe.transpose(bank(4 + f // 2)[:, (f % 2) * T + t * P:][:, 0:P], att[:, t, f * P:(f + 1) * P],
                                      ident)
            mm.then_inc(sig["att_turned"], 1)
            pe.wait_ge(sig["att_cols"], 4)
            project_out_end(N_OUT1)

            def turn_mod(g, b):
                pe.wait_ge(sig["ada_kept"], g + 1)
                for q in range(4):
                    mm = pe.transpose(bank(b)[:, q * P:(q + 1) * P], mod[:, g, q * P:(q + 1) * P], ident)
                mm.then_inc(sig["mod_turned"], 1)

            for i in range(ADA_MID, len(ADA_CHUNKS)):
                ada(i)
            turn_mod(0, 6)
            turn_mod(1, 5)

            pe.wait_ge(sig["x_added"], 4)
            turn_rows(4)
            need_cols()
            pe.wait_ge(sig["router_in"], 16)
            for t in range(NT):
                for k in range(KD):
                    mm = pe.matmul(bank(4)[:, t * EXPERTS:(t + 1) * EXPERTS], cols[:, k, t * P:(t + 1) * P],
                                   router[:, k, :], start=(k == 0), stop=(k == KD - 1))
            mm.then_inc(sig["logits_done"], 1)
            pe.wait_ge(sig["mod_cols"], 2)
            turn_mod(2, 6)
            pe.wait_ge(sig["routed"], 1)
            pe.matmul(bank(5)[:, 0:32], const("tri_exc"), chosen[:, 0, :], start=True, stop=True)
            pe.matmul(bank(5)[:, 32:64], ones, chosen[:, 0, :], start=True, stop=False)
            pe.matmul(bank(5)[:, 32:64], const("tri_exc"), chosen[:, 1, :], start=False, stop=True)
            pe.matmul(bank(5)[:, 64:96], ones, chosen[:, 0, :], start=True, stop=False)
            pe.matmul(bank(5)[:, 64:96], ones, chosen[:, 1, :], start=False, stop=True).then_inc(sig["ranks_done"], 1)

            def zeros(n):
                return identb[0:1, 1:2].to_broadcast([1, n])

            def add_zero(**when):
                for t in range(NT):
                    for h in range(2):
                        mm = pe.matmul(bank(4 + 2 * t + h), zeros(P), zeros(512), **when)
                return mm

            def moe_gather(done):
                for k in range(KD):
                    for t in range(NT):
                        mm = pe.matmul(bank(2)[:, k * CAP:(k + 1) * CAP], rows[:, t, k * P:(k + 1) * P],
                                       sel_g[:, t, :], start=(t == 0), stop=(t == NT - 1))
                mm.then_inc(done, 1)

            def moe_gate_up(weights, used):
                for b in range(2):
                    for h in range(2):
                        pe.matmul(bank(b)[CAP * h:CAP * (h + 1), :], sel_b[:, :],
                                  bias_b[:, b * FE + h * 512:b * FE + (h + 1) * 512], start=True, stop=False)
                for k in range(KD):
                    w = weights(k)
                    for b in range(2):
                        for h in range(2):
                            mm = pe.matmul(bank(b)[CAP * h:CAP * (h + 1), :], xg[:, k, :],
                                           w[:, b * FE + h * 512:b * FE + (h + 1) * 512],
                                           start=False, stop=(k == KD - 1))
                    used(mm, k)

            def moe_turn_sel(done):
                for t in range(NT):
                    mm = pe.transpose(bank(3)[:, t * P:(t + 1) * P], sel_s[:, t, :], ident)
                mm.then_inc(done, 1)

            def moe_turn_act(done):
                for j in range(4):
                    mm = pe.transpose(bank(0)[:, j * P:(j + 1) * P], act_buf[:, j * P:(j + 1) * P], ident)
                mm.then_inc(done, 1)

            def moe_down(weights, used):
                for h in range(2):
                    pe.matmul(bank(3)[CAP * h:CAP * (h + 1), :], sel_d[:, :], bdown_b[:, h * 512:(h + 1) * 512],
                              start=True, stop=False)
                for s in range(4):
                    w = weights(s)
                    for f in (2 * s, 2 * s + 1):
                        lhs = act_t[:, (f % 4) * P + CAP * (f // 4):][:, 0:CAP]
                        for h in range(2):
                            mm = pe.matmul(bank(3)[CAP * h:CAP * (h + 1), :], lhs,
                                           w[:, (f % 2) * D + h * 512:(f % 2) * D + (h + 1) * 512],
                                           start=False, stop=(f == 7))
                    used(mm, s)

            def moe_scatter(done):
                for t in range(NT):
                    for h in range(2):
                        mm = pe.matmul(bank(4 + 2 * t + h), sel_t[CAP * h:CAP * (h + 1), t * P:(t + 1) * P],
                                       yb[CAP * h:CAP * (h + 1), :], start=False, stop=False)
                mm.then_inc(done, 1)

            pe.wait_ge(sig["picked"], 1)
            moe_gather(sig["gathered"])
            pe.wait_ge(sig["mod_cols"], 3)
            add_zero(start=True, stop=False)
            pe.wait_ge(sig["bias_split"], 2)
            with pe.Fori(0, EXPERTS) as e:
                def ring_w(first):
                    def get(i):
                        s = (N_MOE + first + i) % SLOTS
                        pe.wait_ge(landed[s], e * 16 + 16 * ((N_MOE + first + i) // SLOTS + 1))
                        return ring[:, s, :]
                    return get

                pe.wait_ge(sig["selb_ready"], e + 1)
                pe.wait_ge(sig["xg_ready"], e + 1)
                moe_gate_up(ring_w(0), lambda mm, k: mm.then_inc(chunk_used, 1))
                pe.wait_ge(sig["yb_ready"], e + 1)
                moe_scatter(sig["scattered"])
                pe.wait_ge(sig["sel_ready"], e + 1)
                moe_turn_sel(sig["sel_turned"])
                pe.wait_ge(sig["picked"], e + 2)
                moe_gather(sig["gathered"])
                pe.wait_ge(sig["act_ready"], e + 1)
                moe_turn_act(sig["act_turned"])
                pe.wait_ge(sig["actt_ready"], e + 1)
                pe.wait_ge(sig["selt_ready"], e + 1)
                pe.wait_ge(sig["seld_ready"], e + 1)
                moe_down(ring_w(KD), lambda mm, s: mm.then_inc(chunk_used, 1))
            pe.wait_ge(sig["yb_ready"], EXPERTS + 1)
            moe_scatter(sig["o_scattered"])

            pe.wait_ge(sig["lists_ready"], 1)
            n_over = pe.value_load(lists[0:1, 32:33], min_val=0, max_val=16)
            with pe.If(n_over > 0):
                with pe.Fori(0, OVER) as j:
                    with pe.If(j < n_over):
                        pe.wait_ge(sig["o_picked"], j + 1)
                        moe_gather(sig["o_gathered"])
                        moe_turn_sel(sig["o_sel_turned"])
                        pe.wait_ge(sig["o_xg"], j + 1)
                        pe.wait_ge(sig["o_loaded"], j * (16 * SLOTS) + 16 * SLOTS)
                        moe_gate_up(lambda k: ring[:, k, :],
                                    lambda mm, k: mm.then_inc(sig["o_gu"], 1) if k == KD - 1 else None)
                        pe.wait_ge(sig["o_act"], j + 1)
                        moe_turn_act(sig["o_act_turned"])
                        pe.wait_ge(sig["o_actt"], j + 1)
                        pe.wait_ge(sig["o_selt"], j + 1)
                        moe_down(lambda s: ring[:, KD + s, :],
                                 lambda mm, s: mm.then_inc(sig["o_down"], 1) if s == 3 else None)
                        pe.wait_ge(sig["o_yb"], j + 1)
                        moe_scatter(sig["o_scattered"])
            add_zero(start=False, stop=True).then_inc(sig["moe_done"], 1)

            turn_rows(6)
            need_cols()
            project(IN2_CHUNKS, N_IN2, (4, 5), len(IN1_CHUNKS))

            pe.wait_ge(sig["decay_ready"], 1)
            pe.matmul(bank(6)[:, 0:10], const("tri_inc"), logf[:, 0, :], start=True, stop=True)
            pe.matmul(bank(6)[:, 16:26], ones, logf[:, 0, :], start=True, stop=False)
            pe.matmul(bank(6)[:, 16:26], const("tri_inc"), logf[:, 1, :], start=False, stop=True).then_inc(
                sig["cum_done"], 1)
            for i in range(6):
                pe.wait_ge(sig["heads_ready"], 4)
                if i >= 2:
                    pe.wait_ge(sig["heads_cols"], i - 1)
                else:
                    pe.wait_ge(sig["cols_dve"], 12)
                for f in (2 * i, 2 * i + 1):
                    c = (C_FQ + f * P) if f < 6 else (C_BQ + (f - 6) * P)
                    for t in range(NT):
                        mm = pe.transpose(bank(i % 2)[:, (f % 2) * T + t * P:][:, 0:P], proj[:, t, c:c + P], ident)
                mm.then_inc(sig["heads_turned"], 1)
            for f in range(4):
                for t in range(NT):
                    mm = pe.transpose(bank(2 + f // 2)[:, (f % 2) * T + t * P:][:, 0:P],
                                      proj[:, t, C_MQ + f * P:C_MQ + (f + 1) * P], ident)
            mm.then_inc(sig["conv_turned"], 1)
            pe.wait_ge(sig["cum_kept"], 1)
            for t in range(NT):
                mm = pe.transpose(bank(7)[0:16, t * P:(t + 1) * P], bias_c[:, t, :], ident)
            mm.then_inc(sig["cumt_turned"], 1)
            pe.wait_ge(sig["heads_cols"], 6)
            pe.wait_ge(sig["conv_silu"], 4)
            attention(2)

            def spread(g, j0, first):
                if first:
                    pe.wait_ge(sig["bcast_kept"], first)
                for i in range(2):
                    j = j0 + i
                    mm = pe.matmul(bank(6 + i), ident[:, 32 * j:32 * j + 1].to_broadcast([P, P]), mod[:, g, :],
                                   start=True, stop=True)
                mm.then_inc(sig["bcast_done"], 1)

            turn_rows(7, by_tile=False)
            spread(1, 0, 0)
            need_cols()
            project_out_start(N_OUT2)
            project_out_end(N_OUT2)
            pe.wait_ge(sig["gate_used"], 4)
            turn_rows(9)
            spread(2, 2, 1)
            need_cols()

            for j in range(PAIRS + 1):
                if j < PAIRS:
                    if j >= 2:
                        pe.wait_ge(sig["h_ready"], j - 1)
                    if j == 1:
                        pe.wait_ge(sig["bcast_kept"], 2)
                    for up in range(2):
                        n = N_GU2 + 2 * j + up
                        need(n)
                        for t in range(NT):
                            for k in range(KD):
                                mm = pe.matmul(bank(4 + 2 * (j % 2) + up)[:, t * CW:(t + 1) * CW],
                                               cols[:, k, t * P:(t + 1) * P], chunk(n)[:, k, :],
                                               start=(k == 0), stop=(k == KD - 1))
                        mm.then_inc(chunk_used, 1)
                if j >= 1:
                    i = j - 1
                    pe.wait_ge(sig["h_ready"], i + 1)
                    if i >= 2:
                        pe.wait_ge(sig["h_cols"], i - 1)
                    for f in range(2):
                        for t in range(NT):
                            mm = pe.transpose(bank(i % 2)[:, f * T + t * P:][:, 0:P],
                                              h_rows[:, i % 2, t * CW + f * P:t * CW + (f + 1) * P], ident)
                    mm.then_inc(sig["h_turned"], 1)
            for c in range(FT // 2):
                need(N_DN2 + c)
                if c == 0:
                    pe.wait_ge(sig["h_cols"], PAIRS)
                for f in (2 * c, 2 * c + 1):
                    for t in range(NT):
                        for h in range(2):
                            mm = pe.matmul(bank(4 + 2 * t + h), h_t[:, f, t * P:(t + 1) * P],
                                           chunk(N_DN2 + c)[:, f % 2, h * 512:(h + 1) * 512],
                                           start=(f == 0), stop=(f == FT - 1))
                mm.then_inc(chunk_used, 1)

        @block.scalar
        def _(act):
            do = Steps(act, act_own, sig)

            for name in VEC_FIRST:
                at, n = VEC_ROWS[name]
                src = ins[name][0] if name == "b_pool" else ins[name].rearrange("o (k p) -> (o k) p", p=P)
                act.dma_start(vec[at:at + n, :], src).then_inc(sig["vec_in"], 16)

            turned = [0]

            def keep_cols(scale, shift=None):
                turned[0] += 1
                for k in range(4, KD):
                    act.wait_ge(sig["rows_turned"], 4 * (turned[0] - 1) + k // 2 + 1)
                    ins_ = nc.scalar.activation(cols[:, k, :], bank(k // 2)[:, (k % 2) * T:(k % 2 + 1) * T],
                                                ACT.Identity, scale=scale(k) if scale else 1.0,
                                                bias=shift(k) if shift else 0.0)
                    do.tell(ins_, "cols_act")

            act.wait_ge(sig["vec_cols"], 1)
            a = VEC_ROWS["c_2"][0]
            do.tell(nc.scalar.activation(c_rep[:, :, :], vcol[:, a:a + KD].unsqueeze(2).to_broadcast([P, KD, 32]),
                                         ACT.Silu), "c_ready")
            keep_cols(lambda k: col("g_attn_norm", k))

            def keep_proj(dst, chunks, banks, base_n):
                for c, (a, w) in enumerate(chunks):
                    act.wait_ge(chunk_used, base_n + c + 1)
                    do.tell(nc.scalar.copy(dst[:, :, a:a + w],
                                           bank(banks[c % 2])[:, 0:NT * w].rearrange("p (t n) -> p t n", t=NT)),
                            "proj_kept")

            act.wait_ge(sig["trig_arg"], 1)
            do.tell(nc.scalar.activation(trig[:, :, :, :], trig[:, :, :, :], ACT.Sin), "trig_ready")
            keep_proj(proj1, IN1_CHUNKS, (4, 5), N_IN1)
            flat_q = q_rows.rearrange("p t h n -> p t (h n)")
            flat_kv = kv_rows.rearrange("p t h n -> p t (h n)")
            act.wait_ge(chunk_used, N_QB + 1)
            for t in range(NT):
                do.tell(nc.scalar.copy(flat_q[:, t, 0:512], bank(4 + t)), "qkv_kept")
            do.tell(nc.scalar.copy(flat_q[:, :, 512:768], bank(6).rearrange("p (t n) -> p t n", t=NT)), "qkv_kept")
            act.wait_ge(chunk_used, N_KVB + 1)
            for t in range(NT):
                for a in (0, 512):
                    do.tell(nc.scalar.copy(flat_kv[:, t, a:a + 512], bank(4 * t + a // 512)), "qkv_kept")
            act.wait_ge(sig["diff_done"], 1)
            for b in range(2):
                do.tell(nc.scalar.copy(diff[:, 2 * b:2 * b + 2, :],
                                       bank(2 + b).rearrange("p (g t) -> p g t", g=2)), "diff_kept")
            act.wait_ge(sig["bias_split"], 1)
            for b in range(4):
                act.wait_ge(sig["qk_turned"], b + 1)
                do.tell(nc.scalar.copy(qk[0:QK, 2 * b:2 * b + 2, :],
                                       bank((0, 1, 4, 5)[b])[0:QK, :].rearrange("p (h t) -> p h t", h=2)), "q_cols")

            def attention(block_no):
                heads = list(attention_heads(block_no))
                scale = ATT_SCALE[block_no]
                for lo, hi in GROUP_OF[block_no]:
                    for i in range(lo, hi + 1):
                        if i < hi:
                            g, _, _, _, _, ml, _ = heads[i]
                            b = g % 2
                            src = bank(6 + b) if ml else bank(b)
                            dst = ml_e if ml else probs[:, b, :]
                            act.wait_ge(sig["rowmax_ready"], g + 1)
                            if ml:
                                if i > lo:
                                    scores_used(act, g - 1)
                            elif g >= 2:
                                act.wait_ge(sig["probs_turned"], g - 1)
                            for t in range(NT):
                                a, w = (0, P) if t == 0 else (P, T)
                                kw = {} if ml else {"accum_out": psum_row[:, i % 16, t:t + 1]}
                                ins_ = nc.scalar.activation(dst[:, a:a + w], src[:, a:a + w], ACT.Exp,
                                                            bias=nmax[:, i % 16, t:t + 1],
                                                            scale=1.0 if ml else scale, **kw)
                                if t == 0:
                                    do.step(ins_)
                                elif ml:
                                    do.tell(ins_, "ml_exp")
                                else:
                                    do.tell(ins_, "probs_ready")
                        if i > lo:
                            g = heads[i - 1][0]
                            act.wait_ge(sig["probs_turned"], g + 1)
                            if g >= 2:
                                act.wait_ge(sig["pv_done"], g - 1)
                            do.tell(nc.scalar.copy(pt[:, g % 2, :], bank(2 + g % 2)[:, 0:384]), "pt_kept")

            attention(1)
            act.wait_ge(sig["att_turned"], 1)
            for f in range(4):
                do.tell(nc.scalar.activation(cols[:, 4 + f, :], bank(4 + f // 2)[:, (f % 2) * T:(f % 2 + 1) * T],
                                             ACT.Copy, scale=col("g_out_attn", f)), "att_cols")
            keep_cols(lambda k: col("g_ffn_norm", k))
            act.wait_ge(sig["shifted"], 1)
            for t in range(NT):
                do.step(nc.scalar.activation(gexp[:, t, :], lg[:, t, 0:EXPERTS], ACT.Exp, bias=small[:, t:t + 1]))
            for t in range(NT):
                ins_ = nc.scalar.activation(small[:, 8 + 4 * t:12 + 4 * t], top[:, t, 4:8], ACT.Exp,
                                            bias=small[:, t:t + 1], accum_out=small[:, 2 + t:3 + t])
                do.tell(ins_, "exp_ready")

            def keep_sel(done):
                return nc.scalar.copy(sel_t, bank(3)[:, 0:T]).then_inc(done, 1)

            def sigmoid(done):
                return nc.scalar.activation(sg, g_min, ACT.Sigmoid, scale=ALPHA).then_inc(done, 1)

            def keep_act(done):
                return nc.scalar.copy(act_t, bank(0)).then_inc(done, 1)

            def keep_y(done):
                return nc.scalar.copy(yb, bank(3)).then_inc(done, 1)

            nc.scalar.activation(sel_t, const("iota")[:, 0:T], ACT.Copy, scale=0.0)
            nc.scalar.activation(yb, const("iota"), ACT.Copy, scale=0.0).then_inc(sig["yb_ready"], 1)
            with act.Fori(0, EXPERTS) as e:
                act.wait_ge(sig["clipped"], e + 1)
                sigmoid(sig["sig_ready"])
                act.wait_ge(sig["sel_turned"], e + 1)
                act.wait_ge(sig["scattered"], e + 1)
                keep_sel(sig["selt_ready"])
                act.wait_ge(sig["act_turned"], e + 1)
                keep_act(sig["actt_ready"])
                act.wait_ge(chunk_used, e * SLOTS + (N_MOE + SLOTS))
                keep_y(sig["yb_ready"])
            act.wait_ge(sig["lists_ready"], 1)
            n_over = act.value_load(lists[0:1, 32:33], min_val=0, max_val=16)
            with act.If(n_over > 0):
                with act.Fori(0, OVER) as j:
                    with act.If(j < n_over):
                        act.wait_ge(sig["o_sel_turned"], j + 1)
                        act.wait_ge(sig["o_scattered"], j + 1)
                        keep_sel(sig["o_selt"])
                        act.wait_ge(sig["o_clipped"], j + 1)
                        sigmoid(sig["o_sig"])
                        act.wait_ge(sig["o_act_turned"], j + 1)
                        keep_act(sig["o_actt"])
                        act.wait_ge(sig["o_down"], j + 1)
                        keep_y(sig["o_yb"])

            keep_cols(lambda k: modg[:, k:k + 1], lambda k: modc[:, k:k + 1])
            keep_proj(proj, IN2_CHUNKS, (4, 5), N_IN2)
            act.wait_ge(sig["ff_ready"], 1)
            do.step(nc.scalar.activation(logf, logf, ACT.Exp))
            do.tell(nc.scalar.activation(logf, logf, ACT.Ln, bias=1.0), "ff_ln")
            for i, c in enumerate((C_FQ, C_BQ)):
                for t in range(NT):
                    n = 2 * i + t
                    if n >= 2:
                        act.wait_ge(sig["sq_used"], n - 1)
                    do.tell(nc.scalar.activation(sq_buf[n % 2], proj[:, t, c:c + 768], ACT.Square), "qk_sq")
            for i in range(6):
                act.wait_ge(sig["heads_turned"], i + 1)
                gname = ("fox_q_g_2", "fox_k_g_2", "moba_q_g_2", "moba_k_g_2")
                for f in (2 * i, 2 * i + 1):
                    ins_ = nc.scalar.activation(qk[:, f, :], bank(i % 2)[:, (f % 2) * T:(f % 2 + 1) * T], ACT.Copy,
                                                scale=col(gname[f // 3]))
                    if f % 2:
                        do.tell(ins_, "heads_cols")
                    else:
                        do.step(ins_)
            act.wait_ge(sig["conv_turned"], 1)
            for b in range(2):
                ins_ = nc.scalar.copy(conv_x[:, 2 * b:2 * b + 2, 3:3 + T],
                                      bank(2 + b).rearrange("p (c t) -> p c t", c=2))
                do.tell(ins_, "conv_in")
            for c in range(4):
                act.wait_ge(sig["conv_sum"], c + 1)
                do.tell(nc.scalar.activation(qk[:, 12 + c, :], qk[:, 12 + c, :], ACT.Silu,
                                             bias=col("ml_conv_b_2", c)), "conv_silu")
            attention(2)
            act.wait_ge(sig["ml_m"], 1)
            do.tell(nc.scalar.activation(guard, guard, ACT.Exp, scale=-1.0), "ml_guard")
            do.tell(nc.scalar.activation(proj[:, :, C_MO:C_MO + 256], proj[:, :, C_MO:C_MO + 256], ACT.Sigmoid),
                    "ml_sig")

            def keep_bcast(n):
                act.wait_ge(sig["bcast_done"], n)
                do.step(nc.scalar.copy(gate_b[:, 0:512], bank(6)))
                do.tell(nc.scalar.copy(gate_b[:, 512:1024], bank(7)), "bcast_kept")

            keep_cols(lambda k: col("ml_h_g_2", 1) if k == 4 else 1.0)
            keep_bcast(1)
            keep_cols(lambda k: modg[:, 8 + k:9 + k], lambda k: modc[:, 24 + k:25 + k])
            act.wait_ge(sig["gate_used"], 4)
            keep_bcast(2)
            for j in range(PAIRS + 1):
                if j < PAIRS:
                    act.wait_ge(chunk_used, N_GU2 + 2 * j + 1)
                    if j >= 2:
                        act.wait_ge(sig["h_ready"], j - 1)
                    do.tell(nc.scalar.activation(h_sil[:, j % 2, :], bank(4 + 2 * (j % 2)), ACT.Silu), "silu_ready")
                if j >= 1:
                    i = j - 1
                    act.wait_ge(sig["h_turned"], i + 1)
                    do.tell(nc.scalar.copy(h_t[:, 2 * i:2 * i + 2, :],
                                           bank(i % 2).rearrange("p (f t) -> p f t", f=2)), "h_cols")
            for i in range(4):
                t, h = divmod(i, 2)
                act.wait_ge(sig["out_ready"], i + 1)
                act.dma_start(out[0, t * P:(t + 1) * P, h * 512:(h + 1) * 512],
                              x_sb[:, t, h * 512:(h + 1) * 512]).then_inc(sig["out_stored"], 16)
            act.wait_ge(sig["out_stored"], 16 * 4)

        @block.vector
        def _(dve):
            v = nc.vector
            do = Steps(dve, dve_own, sig)

            def rsqrt(dst, src, tmp):
                do.step(v.tensor_scalar(dst.bitcast(I32), src.bitcast(I32), 1, None, ALU.logical_shift_right))
                do.step(v.tensor_scalar(dst.bitcast(I32), dst.bitcast(I32), -1.0, RSQRT_GUESS, ALU.mult, ALU.add))
                for _ in range(3):
                    do.step(v.tensor_tensor(tmp, dst, src, ALU.mult))
                    do.step(v.scalar_tensor_tensor(out=tmp, in0=tmp, scalar=-0.5, in1=dst, op0=ALU.mult, op1=ALU.mult))
                    do.step(v.scalar_tensor_tensor(out=dst, in0=tmp, scalar=1.5, in1=dst, op0=ALU.add, op1=ALU.mult))

            def rstd(request, n, t=None):
                at = slice(0, STAT_W[request]) if t is None else slice(t, t + 1)
                src, dst = stat(ms, request)[:, at], stat(rs, request)[:, at]
                do.step(v.tensor_scalar(src, src, 1.0 / n, EPS, ALU.mult, ALU.add))
                rsqrt(dst, src, rsqrt_tmp[:, 0:at.stop - at.start])
                return dst

            def norm_rows(request, t):
                do.step(v.tensor_tensor_reduce(out=rows[:, t, :], in0=x_sb[:, t, :], in1=x_sb[:, t, :], scale=1.0,
                                               scalar=0.0, op0=ALU.mult, op1=ALU.add,
                                               accum_out=stat(ms, request)[:, t:t + 1]))
                r_ = rstd(request, D, t)
                do.tell(v.tensor_scalar(rows[:, t, :], x_sb[:, t, :], r_, None, ALU.mult), "rows_ready")

            turned = [0]

            def keep_cols(scale, shift=None):
                turned[0] += 1
                for k in range(4):
                    dve.wait_ge(sig["rows_turned"], 4 * (turned[0] - 1) + k // 2 + 1)
                    src = bank(k // 2)[:, (k % 2) * T:(k % 2 + 1) * T]
                    if shift:
                        ins_ = v.tensor_scalar(cols[:, k, :], src, scale(k), shift(k), ALU.mult, ALU.add)
                    else:
                        ins_ = v.tensor_scalar(cols[:, k, :], src, scale(k), None, ALU.mult)
                    do.tell(ins_, "cols_dve")

            dve.wait_ge(sig["x0_in"], 16)
            norm_rows(S_ATTN, 0)
            dve.wait_ge(sig["vec_turned"], 1)
            do.tell(v.tensor_copy(vcol[:, 0:NVEC_FIRST], bank(6)[:, 0:NVEC_FIRST]), "vec_cols")
            dve.wait_ge(sig["x1_in"], 16)
            norm_rows(S_ATTN, 1)
            keep_cols(lambda k: col("g_attn_norm", k))
            dve.wait_ge(sig["const_in"], 16)
            dve.wait_ge(sig["const2_in"], 16)
            do.step(v.tensor_copy(identb[:, :], ident))
            do.tell(v.tensor_copy(maskb[:, :], const("mask")), "bf_const")

            dve.wait_ge(sig["pos_in"], 16)
            do.step(v.tensor_copy(ms[:, 0:NT], pos_i[:, :]))
            for t in range(NT):
                do.step(v.tensor_scalar(ang[:, t, :], const("inv"), ms[:, t:t + 1], None, ALU.mult))
            do.step(v.tensor_scalar(turns, ang, INV_2PI, None, ALU.mult))
            do.step(v.tensor_scalar(turns, turns, ROUND, None, ALU.add))
            do.step(v.tensor_scalar(turns, turns, -ROUND, None, ALU.add))
            for part in TWO_PI:
                do.step(v.scalar_tensor_tensor(out=ang, in0=turns, scalar=-part, in1=ang, op0=ALU.mult, op1=ALU.add))
            do.step(v.tensor_scalar(trig[:, 0, :, :], ang, PI_IN, -PI_IN, ALU.min, ALU.max))
            do.step(v.scalar_tensor_tensor(out=ang, in0=trig[:, 0, :, :], scalar=-1.0, in1=trig[:, 0, :, :],
                                           op0=ALU.mult, op1=ALU.min))
            do.tell(v.tensor_scalar(trig[:, 1, :, :], ang, HALF_PI, None, ALU.add), "trig_arg")

            dve.wait_ge(sig["proj_kept"], 2)
            st = stat(ms, S_LAT)
            for i, (a, w) in enumerate(((D_POOL, Q_LORA), (D_POOL + Q_LORA, KV_LORA))):
                for t in range(NT):
                    do.step(v.tensor_tensor_reduce(out=lat_rows[:, t, a - D_POOL:a - D_POOL + w],
                                                   in0=proj1[:, t, a:a + w], in1=proj1[:, t, a:a + w], scale=1.0 / w,
                                                   scalar=0.0, op0=ALU.mult, op1=ALU.add,
                                                   accum_out=st[:, 2 * i + t:2 * i + t + 1]))
            r_ = rstd(S_LAT, 1)
            for i, (a, w) in enumerate(((D_POOL, Q_LORA), (D_POOL + Q_LORA, KV_LORA))):
                for t in range(NT):
                    do.tell(v.tensor_scalar(lat_rows[:, t, a - D_POOL:a - D_POOL + w], proj1[:, t, a:a + w],
                                            r_[:, 2 * i + t:2 * i + t + 1], None, ALU.mult), "lat_rows")
            dve.wait_ge(sig["lat_turned"], 1)
            for i in range(3):
                g_ = col("g_q_a", i) if i < 2 else col("g_kv_a")
                ins_ = v.tensor_scalar(lat[:, i, :], bank(i // 2)[:, (i % 2) * T:(i % 2 + 1) * T], g_, None, ALU.mult)
                if i < 2:
                    do.step(ins_)
                else:
                    do.tell(ins_, "lat_cols")

            def rope(x1, x2, y1, y2, heads_n):
                cos, sin = (trig[:, i, :, :].unsqueeze(2).to_broadcast([P, NT, heads_n, HALF]) for i in (1, 0))
                tmp = [r[:, :, 0:heads_n, :] for r in rope_tmp]
                for dst, a_, b_ in zip(tmp, (x1, x2, x2, x1), (cos, sin, cos, sin)):
                    do.step(v.tensor_tensor(dst, a_, b_, ALU.mult))
                return (v.tensor_tensor(y1, tmp[0], tmp[1], ALU.subtract), v.tensor_tensor(y2, tmp[2], tmp[3], ALU.add))

            dve.wait_ge(sig["trig_ready"], 1)
            k1 = proj1[:, :, IN1 - ROPE:IN1 - HALF].unsqueeze(2)
            k2 = proj1[:, :, IN1 - HALF:IN1].unsqueeze(2)
            for ins_ in rope(k1, k2, k1, k2, 1):
                do.step(ins_)
            dve.wait_ge(sig["rows_turned"], 4)
            for t in range(NT):
                do.step(v.tensor_copy(k_rows[:, t, :, NOPE:QK],
                                      proj1[:, t, IN1 - ROPE:IN1].unsqueeze(1).to_broadcast([P, HEADS, ROPE])))
            dve.wait_ge(sig["qkv_kept"], 3)
            q1, q2 = q_rows[:, :, :, NOPE:NOPE + HALF], q_rows[:, :, :, NOPE + HALF:QK]
            a_, b_ = rope(q1, q2, q1, q2, HEADS)
            do.step(a_)
            do.tell(b_, "q_roped")
            dve.wait_ge(sig["qkv_kept"], 7)
            do.tell(v.tensor_copy(k_rows[:, :, :, 0:NOPE], kv_rows[:, :, :, 0:NOPE]), "k_roped")

            dve.wait_ge(sig["mixed_done"], 1)
            for g in range(GROUPS):
                (do.step if g < GROUPS - 1 else lambda i_: do.tell(i_, "pooled_kept"))(v.tensor_scalar(pooled[:, g, :], bank(2 + g // 2)[:, (g % 2) * T:(g % 2 + 1) * T],
                                        col("b_pool", g), col("pool_scale", g), ALU.add, ALU.mult))
            for b in range(4):
                dve.wait_ge(sig["qk_turned"], 4 + b + 1)
                do.tell(v.tensor_copy(qk[0:QK, 8 + 2 * b:8 + 2 * b + 2, :],
                                      bank((0, 1, 4, 5)[b])[0:QK, :].rearrange("p (h t) -> p h t", h=2)), "k_cols")
            dve.wait_ge(sig["vec2_turned"], 1)
            do.tell(v.tensor_copy(vcol[:, NVEC_FIRST:NVEC], bank(6)[:, NVEC_FIRST:NVEC]), "vec2_cols")

            def square_pooled():
                do.tell(v.tensor_tensor(pool_sq, pooled, pooled, ALU.mult), "pool_sq")

            def keep_pooled():
                for g in range(GROUPS):
                    do.tell(v.tensor_scalar(cols[:, g, :], pooled[:, g, :], col("g_out_pool", g), None, ALU.mult),
                            "pool_cols")

            def keep_pool_sums():
                dve.wait_ge(sig["pool_sum"], 1)
                do.step(v.tensor_copy(stat(ms, S_MIX)[:, 0:NT], bank(6)[:, 0:NT]))

            def keep_ada(g):
                dve.wait_ge(sig["bada_in"], 64)
                dve.wait_ge(chunk_used, ada_at(KD * g + KD - 1) + 1)
                do.tell(v.tensor_tensor(mod[:, g, :], bank(7), mod[:, g, :], ALU.add), "ada_kept")

            def attention(block_no, extra=None):
                heads = list(attention_heads(block_no))
                for lo, hi in GROUP_OF[block_no]:
                    for i in range(lo, hi):
                        g, _, _, _, _, ml, _ = heads[i]
                        src = bank((6 if ml else 0) + g % 2)
                        dve.wait_ge(sig["scores_done"], g + 1)
                        do.step(v.tensor_reduce(rmax[:, i, 0:1], src[:, 0:P], AX.X, ALU.max))
                        do.step(v.tensor_reduce(rmax[:, i, 1:2], src[:, P:3 * P], AX.X, ALU.max))
                        if ml:
                            do.tell(v.tensor_scalar(nmax[:, i, :], rmax[:, i, :], 0.0, -1.0, ALU.max, ALU.mult),
                                    "rowmax_ready")
                            dve.wait_ge(sig["ml_exp"], i - SOFT + 1)
                            dve.wait_ge(sig["probs_turned"], g - 1)
                            for t in range(NT):
                                a, w = (0, P) if t == 0 else (P, T)
                                ins_ = v.tensor_tensor_reduce(
                                    out=probs[:, g % 2, a:a + w], in0=bank(g % 2)[:, a:a + w], in1=ml_e[:, a:a + w],
                                    scale=float(HD) ** -0.5, scalar=0.0, op0=ALU.mult, op1=ALU.add,
                                    accum_out=psum_row[:, i, t:t + 1])
                                if t:
                                    do.tell(ins_, "smat_ready")
                                else:
                                    do.step(ins_)
                        else:
                            do.tell(v.tensor_scalar(nmax[:, i, :], rmax[:, i, :], -ATT_SCALE[block_no], None, ALU.mult),
                                    "rowmax_ready")
                        for other in (extra or {}).get(i, ()):
                            other()
                    g = heads[hi - 1][0]
                    n = hi - lo
                    scores_used(dve, g)
                    if lo != SOFT:
                        do.step(v.reciprocal(den_all[:, lo:hi, :], psum_row[:, lo:hi, :]))
                    else:
                        do.step(v.tensor_scalar(guard, nmax[:, lo:hi, :], -1.0, None, ALU.mult))
                        do.tell(v.tensor_tensor(guard, guard, cum[:, :, 6:10].rearrange("p t h -> p h t"), ALU.add),
                                "ml_m")
                        dve.wait_ge(sig["ml_guard"], 1)
                        do.step(v.scalar_tensor_tensor(out=den, in0=psum_row[:, lo:hi, :], scalar=-1.0,
                                                       in1=psum_row[:, lo:hi, :], op0=ALU.mult, op1=ALU.max))
                        do.step(v.tensor_tensor(den, den, guard, ALU.max))
                        do.step(v.reciprocal(den_all[:, lo:hi, :], den))
                    dve.wait_ge(sig["pv_done"], g + 1)
                    at = {0: 0, FOX: 640, SOFT: 384}[lo]
                    if block_no == 2 and lo == 0:
                        dve.wait_ge(sig["qk_sq"], 4)
                    for t in range(NT):
                        ins_ = v.tensor_tensor(rows[:, t, at:at + n * HD].rearrange("p (h d) -> p h d", h=n),
                                               bank(4 + t)[:, 0:n * HD].rearrange("p (h d) -> p h d", h=n),
                                               den_all[:, lo:hi, t:t + 1].to_broadcast([P, n, HD]), ALU.mult)
                        if t:
                            do.tell(ins_, "o_free")
                        else:
                            do.step(ins_)

            attention(1, {0: [lambda: keep_ada(0), square_pooled], 1: [keep_pooled], 3: [keep_pool_sums],
                          5: [lambda: keep_ada(1)]})
            st = stat(ms, S_MIX)
            for t in range(NT):
                do.step(v.tensor_tensor_reduce(out=rows[:, t, 512:1024], in0=att[:, t, :], in1=att[:, t, :], scale=1.0,
                                               scalar=0.0, op0=ALU.mult, op1=ALU.add,
                                               accum_out=st[:, NT + t:NT + t + 1]))
            r_mix = rstd(S_MIX, 512)
            ratio = small[:, 120:120 + NT]
            do.step(v.reciprocal(ratio, r_mix[:, 0:NT]))
            do.step(v.tensor_tensor(ratio, ratio, r_mix[:, NT:2 * NT], ALU.mult))
            for t in range(NT):
                do.tell(v.tensor_scalar(att[:, t, :], att[:, t, :], ratio[:, t:t + 1], None, ALU.mult), "att_rows")

            for t in range(NT):
                if t == 0:
                    dve.wait_ge(sig["out_half"], 1)
                else:
                    dve.wait_ge(chunk_used, N_OUT1 + 4)
                for h in range(2):
                    xs = x_sb[:, t, h * 512:(h + 1) * 512]
                    do.tell(v.scalar_tensor_tensor(out=xs, in0=bank(2 * t + h), scalar=r_mix[:, t:t + 1], in1=xs,
                                                   op0=ALU.mult, op1=ALU.add), "x_added")
                norm_rows(S_FFN, t)

            def keep_mod(g, b):
                dve.wait_ge(sig["mod_turned"], g + 1)
                do.tell(v.tensor_copy(modc[:, 16 * g:16 * g + 16].rearrange("p (j q) -> p j q", j=4),
                                      bank(b).rearrange("p (q j r) -> p j q r", q=4, j=4)[:, :, :, 0]), "mod_cols")

            def norm_gain(i, at, name):
                a = VEC_ROWS[name][0]
                do.step(v.scalar_tensor_tensor(out=modg[:, 8 * i:8 * i + 8], in0=modc[:, at:at + 8], scalar=1.0,
                                               in1=vcol[:, a:a + 8], op0=ALU.add, op1=ALU.mult))

            keep_mod(0, 6)
            keep_mod(1, 5)
            keep_cols(lambda k: col("g_ffn_norm", k))

            keep_ada(2)
            do.step(v.memset(lg[:, :, EXPERTS:EXPERTS + 4], BIG))
            do.step(v.memset(rank[:, :, :], -1.0))
            do.step(v.memset(gates[:, :, :], 0.0))
            dve.wait_ge(sig["logits_done"], 1)
            dve.wait_ge(sig["brouter_in"], 16)
            do.step(v.tensor_tensor(lg[:, :, 0:EXPERTS],
                                    bank(4)[:, 0:NT * EXPERTS].rearrange("p (t e) -> p t e", t=NT),
                                    brouter[:, :].unsqueeze(1).to_broadcast([P, NT, EXPERTS]), ALU.add))
            for t in range(NT):
                do.step(v.max(top[:, t, :], lg[:, t, :]))
                do.step(v.match_replace(out=lr[:, t, :], in_to_replace=top[:, t, :], in_values=lg[:, t, :],
                                        imm_value=-BIG))
            do.step(v.tensor_scalar(small[:, 0:NT], top[:, :, 4], -1.0, None, ALU.mult))
            do.tell(v.tensor_tensor(chosen, lr[:, :, 0:EXPERTS], lg[:, :, 0:EXPERTS], ALU.not_equal), "routed")
            do.tell(v.tensor_copy(small[:, 4:6], small[:, 0:2]), "shifted")
            dve.wait_ge(sig["exp_ready"], 2)
            do.step(v.reciprocal(small[:, 4:6], small[:, 2:4]))
            for t in range(NT):
                do.step(v.scalar_tensor_tensor(out=gates[:, t, 0:EXPERTS], in0=gexp[:, t, :],
                                               scalar=small[:, 4 + t:5 + t], in1=chosen[:, t, :],
                                               op0=ALU.mult, op1=ALU.mult))
            dve.wait_ge(sig["ranks_done"], 1)
            counts = bank(5)[0:1, 64:96].unsqueeze(1).to_broadcast([1, 3, EXPERTS])
            flag, upto = small[0:1, 16:112], lr_row
            do.step(v.tensor_tensor(flag.rearrange("p (b e) -> p b e", b=3), counts,
                                    const("pass_floor", 1).rearrange("p (b e) -> p b e", b=3), ALU.is_gt))
            do.step(v.scalar_tensor_tensor(out=gexp, in0=bank(5)[:, 0:64].rearrange("p (t e) -> p t e", t=NT),
                                           scalar=1.0, in1=chosen, op0=ALU.add, op1=ALU.mult))
            do.tell(v.tensor_scalar(rank[:, :, 0:EXPERTS], gexp, 1.0, None, ALU.subtract), "ranks_kept")
            iota = const("iota")

            def pick_gather(e, at, done):
                for t in range(NT):
                    ins_ = v.tensor_scalar(sel_g[:, t, :], iota[:, at], rank[:, t, bass.ds(e, 1)], None, ALU.is_equal)
                    if t:
                        ins_.then_inc(done, 1)

            def pick_scatter(e, at, done):
                for t in range(NT):
                    ins_ = v.tensor_scalar(sel_s[:, t, :], iota[:, at], rank[:, t, bass.ds(e, 1)],
                                           gates[:, t, bass.ds(e, 1)], ALU.is_equal, ALU.mult)
                    if t and done is not None:
                        ins_.then_inc(done, 1)

            def pick_bias(dst, e, done):
                v.tensor_scalar(dst, ones[0:96, 0:CAP], const("pick", 96)[:, bass.ds(e, 1)], None,
                                ALU.mult).then_inc(done, 1)

            def keep_x(done):
                a = VEC_ROWS["g_ffn_norm"][0]
                v.tensor_tensor(xg, bank(2).rearrange("p (k s) -> p k s", k=KD),
                                vcol[:, a:a + KD].unsqueeze(2).to_broadcast([P, KD, CAP]), ALU.mult).then_inc(done, 1)

            def gate_up(clipped, n, up_done, up_n):
                v.tensor_scalar(g_min, bank(0), LIMIT, None, ALU.min).then_inc(clipped, 1)
                v.tensor_scalar(u_clip, bank(1), -LIMIT, LIMIT, ALU.max, ALU.min).then_inc(up_done, 1)
                dve.wait_ge(clipped, n)
                dve.wait_ge(up_done, up_n)
                v.scalar_tensor_tensor(out=u_clip, in0=u_clip, scalar=1.0, in1=g_min, op0=ALU.add,
                                       op1=ALU.mult).then_inc(up_done, 1)

            pick_gather(0, slice(0, CAP), sig["picked"])
            pick_bias(sel_b, 0, sig["selb_ready"])
            keep_mod(2, 6)
            norm_gain(0, 8, "norm1_g_2")
            norm_gain(1, 32, "norm2_g_2")
            dve.wait_ge(sig["gathered"], 1)
            keep_x(sig["xg_ready"])
            do.step(v.tensor_tensor_scan(out=upto, data0=ones[0:1, 0:96], data1=flag, initial=0.0,
                                         op0=ALU.mult, op1=ALU.add))
            do.step(v.tensor_tensor(list_eq, upto.unsqueeze(1).to_broadcast([1, 16, 96]),
                                    const("pass_rank", 1).unsqueeze(2).to_broadcast([1, 16, 96]), ALU.is_equal))
            do.step(v.tensor_tensor(list_eq, list_eq, flag.unsqueeze(1).to_broadcast([1, 16, 96]), ALU.mult))
            for i, name in enumerate(("pass_expert", "pass_block")):
                do.step(v.tensor_tensor(list_w, list_eq, const(name, 1).unsqueeze(1).to_broadcast([1, 16, 96]),
                                        ALU.mult))
                do.step(v.tensor_reduce(list_f[:, 16 * i:16 * i + 16], list_w, AX.X, ALU.add))
            do.step(v.tensor_copy(list_f[:, 32:33], upto[:, 95:96]))
            do.tell(v.tensor_copy(lists[:, 0:33], list_f[:, 0:33]), "lists_ready")
            with dve.Fori(0, EXPERTS) as e:
                pick_scatter(e, slice(0, P), sig["sel_ready"])
                pick_gather(e + 1, slice(0, CAP), sig["picked"])
                dve.wait_ge(chunk_used, e * SLOTS + (N_MOE + KD))
                gate_up(sig["clipped"], e + 1, sig["up_steps"], e * 2 + 1)
                pick_bias(sel_b, e + 1, sig["selb_ready"])
                pick_bias(sel_d, e, sig["seld_ready"])
                dve.wait_ge(sig["up_steps"], e * 2 + 2)
                dve.wait_ge(sig["sig_ready"], e + 1)
                v.tensor_tensor(act_buf, u_clip, sg, ALU.mult).then_inc(sig["act_ready"], 1)
                dve.wait_ge(sig["gathered"], e + 2)
                keep_x(sig["xg_ready"])
                dve.wait_ge(sig["xg_ready"], e + 2)
            n_over = dve.value_load(lists[0:1, 32:33], min_val=0, max_val=16)
            with dve.If(n_over > 0):
                with dve.Fori(0, OVER) as j:
                    with dve.If(j < n_over):
                        e = dve.value_load(lists[0:1, bass.ds(j, 1)], min_val=0, max_val=EXPERTS - 1)
                        b = dve.value_load(lists[0:1, bass.ds(j + 16, 1)], min_val=0, max_val=PASSES - 1)
                        dve.wait_ge(sig["o_scattered"], j + 1)
                        pick_scatter(e, bass.ds(b * P, P), sig["o_steps"])
                        pick_gather(e, bass.ds(b * P, CAP), sig["o_steps"])
                        pick_bias(sel_d, e, sig["o_steps"])
                        pick_bias(sel_b, e, sig["o_picked"])
                        dve.wait_ge(sig["o_gathered"], j + 1)
                        keep_x(sig["o_xg"])
                        dve.wait_ge(sig["o_gu"], j + 1)
                        gate_up(sig["o_clipped"], j + 1, sig["o_up_steps"], j * 2 + 1)
                        dve.wait_ge(sig["o_up_steps"], j * 2 + 2)
                        dve.wait_ge(sig["o_sig"], j + 1)
                        v.tensor_tensor(act_buf, u_clip, sg, ALU.mult).then_inc(sig["o_act"], 1)

            dve.wait_ge(sig["moe_done"], 1)
            for i in range(4):
                t, h = divmod(i, 2)
                xs = x_sb[:, t, h * 512:(h + 1) * 512]
                do.step(v.tensor_tensor(xs, bank(4 + i), xs, ALU.add))
            st = stat(ms, S_FINAL)
            for t in range(NT):
                do.step(v.tensor_tensor_reduce(out=rows[:, t, :], in0=x_sb[:, t, :], in1=x_sb[:, t, :], scale=1.0,
                                               scalar=0.0, op0=ALU.mult, op1=ALU.add, accum_out=st[:, t:t + 1]))
            r_ = rstd(S_FINAL, D)
            dve.wait_ge(sig["gfin_in"], 16)
            for t in range(NT):
                do.step(v.scalar_tensor_tensor(out=x_sb[:, t, :], in0=x_sb[:, t, :], scalar=r_[:, t:t + 1],
                                               in1=gfin[:, :], op0=ALU.mult, op1=ALU.mult))

            for t in range(NT):
                norm_rows(S_NORM1, t)
            keep_cols(lambda k: modg[:, k:k + 1], lambda k: modc[:, k:k + 1])
            do.step(v.memset(conv_x[:, :, 0:3], 0.0))
            dve.wait_ge(sig["proj_kept"], len(IN1_CHUNKS) + IN2_GATES)
            dve.wait_ge(sig["bias14_in"], 48)

            def bias_of(a, n):
                return bias14[:, a:a + n].unsqueeze(1).to_broadcast([P, NT, n])

            do.step(v.tensor_tensor(fg[:, :, 0:6], proj[:, :, C_FF:C_FF + FOX], bias_of(0, 6), ALU.add))
            do.step(v.tensor_tensor(fg[:, :, 6:10], proj[:, :, C_MF:C_MF + ML], bias_of(6, 4), ALU.add))
            do.step(v.tensor_tensor(bias_c[:, :, 12:16], proj[:, :, C_MI:C_MI + ML], bias_of(10, 4), ALU.add))
            do.tell(v.scalar_tensor_tensor(out=logf, in0=fg, scalar=-1.0, in1=fg, op0=ALU.mult, op1=ALU.min), "ff_ready")
            dve.wait_ge(sig["ff_ln"], 1)
            do.step(v.tensor_scalar(fg, fg, 0.0, None, ALU.min))
            do.tell(v.tensor_tensor(logf, fg, logf, ALU.subtract), "decay_ready")
            st = stat(ms, S_HEADS)
            for n in range(4):
                dve.wait_ge(sig["qk_sq"], n + 1)
                do.tell(v.tensor_reduce(st[:, 12 * n:12 * n + 12], sq_buf[n % 2].rearrange("p (h d) -> p h d", h=12),
                                        AX.X, ALU.add), "sq_used")
            r_ = rstd(S_HEADS, HD)
            for n in range(4):
                i, t = divmod(n, 2)
                c = (C_FQ, C_BQ)[i]
                view = proj[:, t, c:c + 768].rearrange("p (h d) -> p h d", h=12)
                do.tell(v.tensor_tensor(view, view, r_[:, 12 * n:12 * n + 12].unsqueeze(2).to_broadcast([P, 12, HD]),
                                        ALU.mult), "heads_ready")
            dve.wait_ge(sig["cum_done"], 1)
            for t in range(NT):
                do.step(v.tensor_copy(cum[:, t, :], bank(6)[:, 16 * t:16 * t + 10]))
            do.step(v.tensor_scalar(bias_c[:, :, 0:FOX], cum[:, :, 0:FOX], -float(HD) ** 0.5, None, ALU.mult))
            do.step(v.tensor_copy(bias_c[:, :, FOX:SOFT], const("slope").rearrange("p (t h) -> p t h", t=NT)))
            do.tell(v.tensor_tensor(bias_c[:, :, 12:16], bias_c[:, :, 12:16], cum[:, :, 6:10], ALU.subtract),
                    "cum_kept")
            dve.wait_ge(sig["conv_in"], 2)
            for c in range(4):
                dst = qk[:, 12 + c, :]
                for j in range(CONV):
                    w_ = col("ml_conv_w_2", 4 * j + c)
                    src = conv_x[:, c, j:j + T]
                    if j == 0:
                        do.step(v.tensor_scalar(dst, src, w_, None, ALU.mult))
                        continue
                    ins_ = v.scalar_tensor_tensor(out=dst, in0=src, scalar=w_, in1=dst, op0=ALU.mult, op1=ALU.add)
                    if j == CONV - 1:
                        do.tell(ins_, "conv_sum")
                    else:
                        do.step(ins_)
            dve.wait_ge(sig["cumt_turned"], 1)
            do.tell(v.tensor_copy(bias_r, bank(7)[0:16, 0:T]), "bias_rows")
            attention(2)
            y_ml = rows[:, :, 384:640].rearrange("p t (h d) -> p t h d", h=ML)
            ml_sq = probs_flat[:, 0:512].rearrange("p (t h d) -> p t h d", t=NT, h=ML)
            st, r_ = (stat(x_, S_ML).rearrange("p (t h) -> p t h", t=NT) for x_ in (ms, rs))
            dve.wait_ge(sig["probs_turned"], HEADS + SOFT + ML)
            for t in range(NT):
                do.step(v.tensor_tensor(ml_sq[:, t], y_ml[:, t], y_ml[:, t], ALU.mult))
                do.step(v.tensor_reduce(st[:, t, :], ml_sq[:, t], AX.X, ALU.add))
            rstd(S_ML, HD)
            dve.wait_ge(sig["ml_sig"], 1)
            for t in range(NT):
                do.step(v.tensor_tensor(y_ml[:, t], y_ml[:, t], r_[:, t, :].unsqueeze(2).to_broadcast([P, ML, HD]),
                                        ALU.mult))
            do.tell(v.tensor_tensor(rows[:, :, 384:640], rows[:, :, 384:640], proj[:, :, C_MO:C_MO + 256], ALU.mult),
                    "rows_ready")
            keep_cols(lambda k: col("ml_h_g_2", 0) if k == 3 else 1.0)

            def add_gated(base, t, tell):
                for h in range(2):
                    g_, xs = gate_b[:, h * 512:(h + 1) * 512], x_sb[:, t, h * 512:(h + 1) * 512]
                    tmp = rows[:, t, h * 512:(h + 1) * 512]
                    do.step(v.tensor_tensor(tmp, bank(base + 2 * t + h), g_, ALU.mult))
                    do.tell(v.tensor_tensor(xs, xs, tmp, ALU.add), tell)

            dve.wait_ge(sig["bcast_kept"], 1)
            for t in range(NT):
                if t == 0:
                    dve.wait_ge(sig["out_half"], 2)
                else:
                    dve.wait_ge(chunk_used, N_OUT2 + 4)
                add_gated(0, t, "gate_used")
                norm_rows(S_NORM2, t)
            keep_cols(lambda k: modg[:, 8 + k:9 + k], lambda k: modc[:, 24 + k:25 + k])
            dve.wait_ge(sig["rows_turned"], 20)
            for j in range(PAIRS):
                dve.wait_ge(sig["silu_ready"], j + 1)
                dve.wait_ge(chunk_used, N_GU2 + 2 * j + 2)
                if j >= 2:
                    dve.wait_ge(sig["h_turned"], j - 1)
                do.tell(v.tensor_tensor(h_rows[:, j % 2, :], h_sil[:, j % 2, :], bank(5 + 2 * (j % 2)), ALU.mult),
                        "h_ready")
            dve.wait_ge(sig["bcast_kept"], 2)
            dve.wait_ge(sig["h_turned"], PAIRS)
            dve.wait_ge(chunk_used, N_END)
            for t in range(NT):
                add_gated(4, t, "out_ready")

        @block.gpsimd
        def _(pool):
            steps = 0
            for parts, full, loaded in ((bias_b, bgu_f, "bgu_in"), (bdown_b, bdown_f, "bdown_in")):
                pool.wait_ge(sig[loaded], 48)
                for hi in (96, 64, 32):
                    done = sig["pool_steps"] if hi > 32 else sig["bias_split"]
                    nc.gpsimd.tensor_copy(parts[0:hi, :], full[0:hi, :]).then_inc(done, 1)
                    if hi > 32:
                        steps += 1
                        pool.wait_ge(sig["pool_steps"], steps)
                        nc.gpsimd.tensor_tensor(full[0:hi - 32, :], full[0:hi - 32, :], parts[0:hi - 32, :],
                                                ALU.subtract).then_inc(sig["pool_steps"], 1)
                        steps += 1
                        pool.wait_ge(sig["pool_steps"], steps)


_INS = ["x", "positions", "g_attn_norm", "w_in", "w_pool", "b_pool", "pool_scale", "g_q_a", "w_q_b", "g_kv_a", "w_kv_b",
        "g_out_pool", "g_out_attn", "w_out", "g_ffn_norm", "w_router", "b_router", "w_gate_up", "b_gate_up", "w_down",
        "b_down", "g_final", "c_2", "w_ada_2", "b_ada_2", "norm1_g_2", "norm2_g_2", "w_in_2", "fox_f_bias_2",
        "fox_q_g_2", "fox_k_g_2", "ml_conv_w_2", "ml_conv_b_2", "ml_i_bias_2", "ml_f_bias_2", "ml_h_g_2",
        "moba_q_g_2", "moba_k_g_2", "w_out_2", "w_gate_up_2", "w_down_2"]


def shape_constants():
    import numpy as np

    c = np.zeros((P, NCONST), np.float32)

    def put(name, a):
        at, n = CONST[name]
        c[:np.shape(a)[0], at:at + n] = a

    i = np.arange(P)
    put("ident", np.eye(P))
    put("ones", np.ones((P, P)))
    put("tri_inc", i[:, None] <= i[None, :])
    put("tri_exc", i[:, None] < i[None, :])
    put("mask", np.where(i[None, :] <= i[:, None], 0.0, NEG))
    put("iota", np.tile((np.arange(PASSES)[:, None] * CAP + i[None, :] % CAP).reshape(1, -1), (P, 1)))
    slopes = np.float32(2.0) ** (np.float32(-8.0) * np.arange(1, MOBA + 1, dtype=np.float32) / np.float32(MOBA))
    tok = np.arange(NT)[None, :, None] * P + i[:, None, None]
    put("slope", (tok * slopes[None, None, :] * np.float32(HD ** 0.5)).reshape(P, -1))
    put("inv", np.tile((np.float32(10000.0) ** (-np.arange(HALF, dtype=np.float32) / np.float32(HALF)))[None], (P, 1)))
    j = np.arange(96)
    put("pass_expert", (j % EXPERTS)[None])
    put("pass_block", (j // EXPERTS + 1)[None])
    put("pass_floor", ((j // EXPERTS + 1) * CAP)[None])
    put("pass_rank", np.arange(1, 17)[None])
    put("pick", (i[:, None] % EXPERTS == np.arange(EXPERTS + 1)[None, :]) & (np.arange(EXPERTS + 1)[None, :] < EXPERTS))
    t = np.arange(T)
    band = np.zeros((T, GROUPS, T), np.float32)
    for g, w in enumerate(WINDOWS):
        inside = (t[:, None] <= t[None, :]) & (t[:, None] > t[None, :] - w)
        band[:, g, :] = inside / np.minimum(t + 1, w)[None, :].astype(np.float32) - np.eye(T)
    band = band.reshape(NT, P, GROUPS, T).transpose(1, 2, 0, 3)
    return c, np.ascontiguousarray(band)


def kernel(**inputs):
    import numpy as _np
    import concourse.bacc as _bacc
    from concourse import mybir as _mybir
    from concourse.bass_utils import run_bass_kernel_spmd as _run

    nc = _bacc.Bacc("TRN2", target_bir_lowering=False, num_devices=1)
    arrays, aps = {}, {}
    consts, band = shape_constants()
    for name in _INS + ["consts", "band"]:
        a = consts if name == "consts" else band if name == "band" else _np.ascontiguousarray(inputs[name])
        arrays[f"in_{name}_dram"] = a
        aps[name] = nc.dram_tensor(f"in_{name}_dram", a.shape, _mybir.dt.from_np(a.dtype), kind="ExternalInput").ap()
    out = nc.dram_tensor("out_0_dram", (1, T, D), _mybir.dt.float32, kind="ExternalOutput").ap()
    two_blocks(nc, aps, aps.pop("consts"), aps.pop("band"), out)
    r = _run(nc, [arrays], core_ids=[0])
    return r.results[0]["out_0_dram"]
```

```python
from contextlib import ExitStack

import concourse.bass as bass
from concourse import mybir

F32 = mybir.dt.float32
BF16 = mybir.dt.bfloat16
I32 = mybir.dt.int32
ALU = mybir.AluOpType
ACT = mybir.ActivationFunctionType
AX = mybir.AxisListType

P = 128
D = 1024
T = 256
NT = T // P
KD = D // P
EPS = 1e-6
INV_2PI = 0.15915494309189535
TWO_PI = (6.28125, 1.93500518798828125e-3, 3.0199159795074593e-07)
PI_IN, HALF_PI = 3.1415925, 1.5707963267948966
RSQRT_GUESS = float(0x5F3759DF)
ROUND = 12582912.0
NEG = -1.0e30
BIG = 3.0e38

D_POOL, GROUPS = 512, 4
WINDOWS = (2, 4, 8, 16)
Q_LORA, KV_LORA, ROPE, NOPE, VDIM, HEADS = 256, 128, 32, 64, 64, 8
HALF = ROPE // 2
QK = NOPE + ROPE
IN1 = D_POOL + Q_LORA + KV_LORA + ROPE
EXPERTS, TOPK, FE = 32, 4, 1024
LIMIT, ALPHA = 7.0, 1.702
CAP = 64
PASSES = T // CAP
OVER = NT * P * TOPK // (CAP + 1)

HD = 64
FOX, ML, MOBA = 6, 4, 6
SOFT = FOX + MOBA
C_FQ, C_FK, C_FV, C_FF = 0, 384, 768, 1152
C_MQ, C_MK, C_MV, C_MI, C_MF, C_MO = 1158, 1414, 1670, 1926, 1930, 1934
C_BQ, C_BK, C_BV, IN2 = 2190, 2574, 2958, 3342
CONV = 4
D_FF = 2816
FT = D_FF // P

SLOTS, SLOT = 12, 2048
CW = SLOT // KD


def split(n, w):
    return [(a, min(w, n - a)) for a in range(0, n, w)]


IN1_CHUNKS = sorted(split(IN1, CW), key=lambda c: (c[0] < D_POOL, c[0]))



IN2_W = -(-IN2 // (-(-IN2 // CW) * 16)) * 16


def spans(lo, hi):
    return list(range(lo // IN2_W, (hi - 1) // IN2_W + 1))


IN2_ORDER = list(dict.fromkeys(spans(C_FQ, C_FV) + spans(C_BQ, C_BV) + spans(C_FF, C_MQ) + spans(C_MI, C_MO)
                               + spans(C_MQ, C_MV) + list(range(-(-IN2 // IN2_W)))))
IN2_CHUNKS = [split(IN2, IN2_W)[i] for i in IN2_ORDER]


def in2_ready(lo, hi):
    return max(IN2_ORDER.index(i) for i in spans(lo, hi)) + 1


R_FOX, R_MOBA, R_CONV = in2_ready(C_FQ, C_FV), in2_ready(C_BQ, C_BV), in2_ready(C_MQ, C_MV)
R_GATES = max(in2_ready(C_FF, C_MQ), in2_ready(C_MI, C_MO))
assert R_FOX < R_MOBA < R_GATES < R_CONV < len(IN2_CHUNKS) - 1
ADA_CHUNKS = [(g, k) for g in range(3) for k in range(KD)]
PAIRS = D_FF // CW

ADA_FIRST, ADA_NEXT, ADA_MID = 2, 4, 18
N_IN1 = ADA_FIRST
N_QB = N_IN1 + len(IN1_CHUNKS) + ADA_NEXT - ADA_FIRST
N_KVB = N_QB + 1
N_OUT1 = N_KVB + 1 + ADA_MID - ADA_NEXT
N_MOE = N_OUT1 + 4 + len(ADA_CHUNKS) - ADA_MID
N_IN2 = N_MOE + EXPERTS * SLOTS
N_OUT2 = N_IN2 + len(IN2_CHUNKS)
N_GU2 = N_OUT2 + 4
N_DN2 = N_GU2 + 2 * PAIRS
N_END = N_DN2 + FT // 2



def ada_at(i):
    if i < ADA_FIRST:
        return i
    if i < ADA_NEXT:
        return N_QB - ADA_NEXT + i
    return N_KVB + 1 + i - ADA_NEXT if i < ADA_MID else N_OUT1 + 4 + i - ADA_MID


ADA_OF = {ada_at(i): gk for i, gk in enumerate(ADA_CHUNKS)}

VEC_ROWS = {}
_at = 0
for _name, _n in (("c_2", 8), ("g_attn_norm", 8), ("g_q_a", 2), ("g_kv_a", 1), ("pool_scale", 4), ("b_pool", 4),
                  ("g_out_pool", 4), ("norm1_g_2", 8), ("norm2_g_2", 8), ("g_ffn_norm", 8), ("g_out_attn", 4), ("ml_conv_w_2", 16), ("ml_conv_b_2", 4), ("ml_h_g_2", 2),
                  ("fox_q_g_2", 1), ("fox_k_g_2", 1), ("moba_q_g_2", 1), ("moba_k_g_2", 1)):
    VEC_ROWS[_name] = (_at, _n)
    _at += _n
NVEC = _at
VEC_FIRST = list(VEC_ROWS)[:7]
NVEC_FIRST = VEC_ROWS["norm1_g_2"][0]

CONST = {}
VEC_DMAS = len(VEC_ROWS) - len(VEC_FIRST) + 4
_at = 0
for _name, _n in (("ident", P), ("ones", P), ("tri_inc", P), ("tri_exc", P), ("mask", P), ("iota", PASSES * P),
                  ("slope", NT * MOBA), ("bias_row", 16), ("inv", HALF), ("pass_expert", 96), ("pass_block", 96), ("pass_floor", 96),
                  ("pass_rank", 16), ("pick", EXPERTS + 1)):
    CONST[_name] = (_at, _n)
    _at += _n
NCONST = _at
CONST_FIRST = 2 * P

STAT_W = (2, 4, 4, 2, 2, 2, 48, 8, 2)
STAT_AT = [sum(STAT_W[:i]) for i in range(len(STAT_W))]
NSTAT = sum(STAT_W)
S_ATTN, S_LAT, S_MIX, S_FFN, S_FINAL, S_NORM1, S_HEADS, S_ML, S_NORM2 = range(9)

SIGNALS = """x0_in x1_in const_in const2_in band_in vec_in vec_a_in vec2_in pos_in wpool_in bias14_in gfin_in bada_in bgu_in bdown_in router_in
brouter_in vec_turned vec_cols vec2_turned vec2_cols c_ready rows_ready rows_turned cols_dve cols_act proj_kept
lat_rows lat_turned lat_cols qkv_kept trig_arg trig_ready q_roped k_roped qk_turned q_cols k_cols
diff_done diff_kept mixed_done pooled_kept pool_sq pool_sum pool_cols ada_kept mod_turned mod_cols
out_half x_added scores_done rowmax_ready probs_ready smat_ready probs_turned pt_kept pv_done o_free att_rows att_turned att_cols
pool_steps up_steps o_up_steps o_steps parts_done parts_kept logits_done shifted exp_ready routed ranks_done
lists_ready bias_split
picked sel_ready selb_ready seld_ready gathered xg_ready clipped sig_ready act_ready act_turned actt_ready yb_ready
sel_turned selt_ready scattered
o_loaded o_picked o_gathered o_xg o_gu o_clipped o_sig o_act o_act_turned o_actt o_down o_yb o_sel_turned
o_selt o_scattered o_ring_back
moe_done x_summed x_squared z_ready r_ready x_scaled ff_ready ff_ln decay_ready cum_done cum_kept cumt_turned bias_rows conv_in conv_turned
conv_sum conv_tanh conv_silu qk_sq sq_used heads_ready heads_turned heads_cols ml_exp ml_m ml_guard ml_tanh
bcast_done bcast_kept gate_used silu_ready h_ready h_turned h_cols out_ready out_stored""".split()


class Steps:

    def __init__(self, eng, own, signals):
        self.eng, self.own, self.signals, self.n, self.told = eng, own, signals, 0, {}

    def step(self, ins):
        self.n += 1
        ins.then_inc(self.own, 1)
        self.eng.wait_ge(self.own, self.n)

    def tell(self, ins, name):
        self.told[name] = self.told.get(name, 0) + 1
        ins.then_inc(self.signals[name], 1)
        self.eng.wait_ge(self.signals[name], self.told[name])


def two_blocks(nc, ins, consts, band, out):
    with ExitStack() as ctx:
        def sb(name, shape, dt=F32):
            return ctx.enter_context(nc.sbuf_tensor(name, shape, dt))

        def sem(name):
            return ctx.enter_context(nc.semaphore(name))

        ring = sb("ring", [P, SLOTS, SLOT])
        x_sb = sb("x_sb", [P, NT, D])
        rows = sb("rows", [P, NT, D])
        cols = sb("cols", [P, KD, T])
        work = sb("work", [P, 7488])
        qk = sb("qk", [P, 16, T])
        probs = sb("probs", [P, 2, 384])
        probs_flat = probs[:, :, :].rearrange("p a b -> p (a b)")
        pt = sb("pt", [P, 2, 384])
        mod = sb("mod", [P, 3, 512])
        gfin = sb("gfin", [P, D])
        gate_b = sb("gate_b", [P, D])
        bdown_b = sb("bdown_b", [96, D], BF16)
        cst = sb("cst", [P, NCONST])
        vec = sb("vec", [NVEC, P])
        vcol = sb("vcol", [P, NVEC])
        modc = sb("modc", [P, 48])
        modg = sb("modg", [P, 16])
        c_rep = sb("c_rep", [P, KD, 32])
        wide = sb("wide", [P, 1036])
        router = sb("router", [P, KD, EXPERTS])
        wpool = sb("wpool", [P, GROUPS, P])
        maskb = sb("maskb", [P, P], BF16)
        rowb = sb("rowb", [P, 16], BF16)
        identb = sb("identb", [P, P], BF16)
        ms = sb("ms", [P, NSTAT])
        rs = sb("rs", [P, NSTAT])
        rsqrt_tmp = sb("rsqrt_tmp", [P, 48])
        rmax = sb("rmax", [P, 16, NT])
        nmax = sb("nmax", [P, 16, NT])
        psum_row = sb("psum_row", [P, 16, NT])
        rank = sb("rank", [P, NT, EXPERTS + 1])
        gates = sb("gates", [P, NT, EXPERTS + 1])
        pos_i = sb("pos_i", [P, NT], I32)
        lists = sb("lists", [1, 36], I32)
        den_all = sb("den_all", [P, 16, NT])
        brouter = sb("brouter", [P, EXPERTS])
        bias14 = sb("bias14", [P, 14])
        trig = sb("trig", [P, 2, NT, HALF])
        PS = ctx.enter_context(nc.psum_tensor("PS", [P, 8, 512], F32))

        sig = {name: sem(name) for name in SIGNALS}
        landed = [sem(f"slot{i}_landed") for i in range(SLOTS)]
        chunk_used = sem("chunk_used")
        dve_own, act_own = sem("dve_order"), sem("act_order")

        def const(name, parts=P):
            a, n = CONST[name]
            return cst[0:parts, a:a + n]

        def col(name, i=0):
            return vcol[:, VEC_ROWS[name][0] + i:VEC_ROWS[name][0] + i + 1]

        def stat(tile, request):
            return tile[:, STAT_AT[request]:STAT_AT[request] + STAT_W[request]]

        ident, ones = const("ident"), const("ones")

        proj1 = work[:, 0:NT * IN1].rearrange("p (t n) -> p t n", t=NT)
        b_at = NT * IN1
        band_sb = work[:, b_at:b_at + 2048].rearrange("p (g s t) -> p g s t", g=GROUPS, s=NT)
        q_rows = work[:, b_at + 2048:b_at + 3584].rearrange("p (t h n) -> p t h n", t=NT, h=HEADS)
        kv_rows = work[:, b_at + 3584:b_at + 5632].rearrange("p (t h n) -> p t h n", t=NT, h=HEADS)
        k_rows = rows[:, :, 0:HEADS * QK].rearrange("p t (h n) -> p t h n", h=HEADS)
        lat_rows = pt[:, :, 0:384]
        lat = cols[:, 0:3, :]
        diff = work[:, b_at:b_at + 1024].rearrange("p (g t) -> p g t", g=GROUPS)
        pooled = work[:, b_at + 1024:b_at + 2048].rearrange("p (g t) -> p g t", g=GROUPS)
        pool_sq = work[:, 0:1024].rearrange("p (g t) -> p g t", g=GROUPS)
        bgu_f = qk[0:96, 0:8, :].rearrange("p a b -> p (a b)")
        rope_area = qk[:, 8:12, :].rearrange("p a b -> p (a b)")
        rope_tmp = [rope_area[:, i * 256:(i + 1) * 256].rearrange("p (t h n) -> p t h n", t=NT, h=HEADS)
                    for i in range(4)]
        ang, turns = (rope_area[:, a:a + NT * HALF].rearrange("p (t n) -> p t n", t=NT) for a in (0, NT * HALF))
        att = rows[:, :, 0:512]
        sel_g = work[:, 0:128].rearrange("p (t s) -> p t s", t=NT)
        sel_s = work[:, 128:384].rearrange("p (t s) -> p t s", t=NT)
        sel_t = work[:, 384:640]
        xg = work[:, 640:1152].rearrange("p (k s) -> p k s", k=KD)
        g_min, act_buf, sg, act_t, yb = (work[:, a:a + 512] for a in range(1152, 1152 + 5 * 512, 512))
        u_clip = work[:, 3712:4224]
        sel_b = work[0:96, 4224:4256].bitcast(BF16)
        sel_d = work[0:96, 4256:4288].bitcast(BF16)
        lg = work[:, 6304:6376].rearrange("p (t e) -> p t e", t=NT)
        lr = work[:, 6376:6448].rearrange("p (t e) -> p t e", t=NT)
        top = work[:, 6448:6464].rearrange("p (t e) -> p t e", t=NT)
        logit_parts = work[:, 7000:7000 + T]
        chosen = work[:, 6464:6528].rearrange("p (t e) -> p t e", t=NT)
        gexp = work[:, 6528:6592].rearrange("p (t e) -> p t e", t=NT)
        small = work[:, 6592:6720]
        lr_row, list_f = work[0:1, 7296:7392], work[0:1, 7392:7440]
        list_eq, list_w = (qk[0:1, a:a + 6, :].rearrange("p a b -> p (a b)").rearrange("p (j i) -> p j i", j=16)
                           for a in (0, 6))
        bias_b = wide[0:96, 0:1024].bitcast(BF16)
        bdown_f = gate_b[0:96, :]
        z_rows = [cols[:, 4 * t:4 * t + 4, :].rearrange("p a b -> p (a b)") for t in range(NT)]
        proj = work[:, 0:NT * IN2].rearrange("p (t n) -> p t n", t=NT)
        tail = work[:, NT * IN2:7488]
        bias_r = tail[:, 0:T // 2].bitcast(BF16)
        bias_p = tail[:, 128:224].rearrange("p (t h) -> p t h", t=NT)
        bias_bf = tail[:, 224:240].bitcast(BF16).rearrange("p (t h) -> p t h", t=NT)
        bias_c = tail[:, 256:288].rearrange("p (t h) -> p t h", t=NT)
        logf, fg, cum = (tail[:, a:a + 20].rearrange("p (t h) -> p t h", t=NT) for a in (288, 308, 328))
        ml_e = tail[:, 348:732]
        guard, den = (tail[:, a:a + 8].rearrange("p (h t) -> p h t", t=NT) for a in (732, 740))
        rinv = tail[:, 748:764].rearrange("p (h t) -> p h t", t=NT)
        sq_buf = [rows[:, b, 0:768] for b in range(2)]
        conv_x = wide[:, :].rearrange("p (c t) -> p c t", c=CONV)
        h_t = work[:, 0:FT * T].rearrange("p (f t) -> p f t", f=FT)
        h_sil = work[:, FT * T:FT * T + 1024].rearrange("p (b n) -> p b n", b=2)
        h_rows = rows[:, :, 0:512]

        def slot(n):
            return ring[:, n % SLOTS, :]

        def bank(b):
            return PS[:, b, :]

        def by_rows(w, r0, n_cols, tiles):
            return w[r0:r0 + tiles * P, :].rearrange("(k p) n -> p k n", p=P)

        def chunk_source(n):
            if n in ADA_OF:
                g, k = ADA_OF[n]
                return ins["w_ada_2"][0][k * P:(k + 1) * P, g * SLOT:(g + 1) * SLOT].rearrange(
                    "(k p) n -> p k n", p=P), 1, SLOT
            if n < N_QB:
                a, w = IN1_CHUNKS[n - N_IN1]
                return ins["w_in"][0][:, a:a + w].rearrange("(k p) n -> p k n", p=P), KD, w
            if n == N_QB:
                return ins["w_q_b"][0].rearrange("(k p) n -> p k n", p=P), 2, HEADS * QK
            if n == N_KVB:
                return ins["w_kv_b"][0].rearrange("(k p) n -> p k n", p=P), 1, 1024
            if n < N_MOE:
                return by_rows(ins["w_out"][0], (n - N_OUT1) * 2 * P, D, 2), 2, D
            n_ = n
            if n_ < N_OUT2:
                a, w = IN2_CHUNKS[n_ - N_IN2]
                return ins["w_in_2"][0][:, a:a + w].rearrange("(k p) n -> p k n", p=P), KD, w
            if n_ < N_GU2:
                return by_rows(ins["w_out_2"][0], (n_ - N_OUT2) * 2 * P, D, 2), 2, D
            if n_ < N_DN2:
                j, up = divmod(n_ - N_GU2, 2)
                a = up * D_FF + j * CW
                return ins["w_gate_up_2"][0][:, a:a + CW].rearrange("(k p) n -> p k n", p=P), KD, CW
            return by_rows(ins["w_down_2"][0], (n_ - N_DN2) * 2 * P, D, 2), 2, D

        def chunk(n):
            _, k, w = chunk_source(n)
            return slot(n)[:, 0:k * w].rearrange("p (k n) -> p k n", k=k)

        gu_dram = ins["w_gate_up"][0].rearrange("e (k p) n -> (e k) p n", p=P)
        dn_dram = ins["w_down"][0].rearrange("e (s k p) n -> (e s) p k n", p=P, k=2)

        heads2 = [(h // 2, 3 + h // 2, HD * (h % 2), C_FV + HD * h, h) for h in range(FOX)]
        heads2 += [(12 + h // 2, 14 + h // 2, HD * (h % 2), C_MV + HD * h, SOFT + h) for h in range(ML)]
        heads2 += [(6 + h // 2, 9 + h // 2, HD * (h % 2), C_BV + HD * h, FOX + h) for h in range(MOBA)]
        ML_LO, ML_HI = FOX, FOX + ML
        GROUPS_OF = {1: [(0, HEADS)], 2: [(0, FOX), (ML_LO, ML_HI), (ML_HI, ML_HI + MOBA)]}
        OUT_AT = {0: 0, ML_LO: 384, ML_HI: 640}

        def attention_heads(block_no):
            if block_no == 1:
                for h in range(HEADS):
                    yield (h, qk[0:QK, h, :], qk[0:QK, 8 + h, :],
                           lambda kt, h=h: kv_rows[:, kt, h, NOPE:NOPE + VDIM], None, False, h * VDIM)
            else:
                for i, (qt, kt_, base, v, row) in enumerate(heads2):
                    first = max(lo for lo, _ in GROUPS_OF[2] if lo <= i)
                    yield (HEADS + i, qk[base:base + HD, qt, :], qk[base:base + HD, kt_, :],
                           lambda kt, v=v: proj[:, kt, v:v + HD], row, ML_LO <= i < ML_HI, (i - first) * HD)

        def is_ml(g):
            return HEADS + ML_LO <= g < HEADS + ML_HI

        def scores_used(eng, g):
            so_far = sum(is_ml(j) for j in range(g + 1))
            if is_ml(g):
                eng.wait_ge(sig["smat_ready"], so_far)
            else:
                eng.wait_ge(sig["probs_ready"], g + 1 - so_far)

        PARTS = ((0, (0, 1)), (1, (0,)), (1, (1,)))
        ATT_SCALE = {1: float(QK) ** -0.5, 2: float(HD) ** -0.5}

        block = ctx.enter_context(nc.Block())

        @block.sync
        def _(sp):
            def load(n):
                src, k, w = chunk_source(n)
                if n >= SLOTS:
                    sp.wait_ge(chunk_used, n - SLOTS + 1)
                dst = slot(n)[:, 0:k * w].rearrange("p (k n) -> p k n", k=k)
                sp.dma_start(dst, src).then_inc(landed[n % SLOTS], 16)

            def load_small(dst, src, name, **kw):
                sp.dma_start(dst, src, **kw).then_inc(sig[name], 16)

            def load_vec(name):
                at, n = VEC_ROWS[name]
                load_small(vec[at:at + n, :], ins[name].rearrange("o (k p) -> (o k) p", p=P), "vec_in")

            x_rows = ins["x"][0].rearrange("(t p) n -> p t n", p=P)
            load_small(x_sb[:, 0, :], x_rows[:, 0, :], "x0_in")
            load_small(x_sb[:, 1, :], x_rows[:, 1, :], "x1_in")
            load_small(cst[:, 0:CONST_FIRST], consts[:, 0:CONST_FIRST], "const_in")
            for name in VEC_FIRST[:2]:
                load_vec(name)
            for n in range(SLOTS):
                load(n)
                if n == 2:
                    load_small(cst[:, CONST_FIRST:NCONST], consts[:, CONST_FIRST:NCONST], "const2_in")
                    load_small(pos_i[:, :], ins["positions"][0].rearrange("(t p) -> p t", p=P), "pos_in",
                          allow_slow_non_contiguous=True)
                if n == 3:
                    for i in range(3):
                        load_small(bgu_f[32 * i:32 * i + 32, :], ins["b_gate_up"][0], "bgu_in")
                if n == 5:
                    load_small(band_sb, band, "band_in")
                if n == 7:
                    load_small(wpool[:, :, :], ins["w_pool"][0].rearrange("g c d -> c g d"), "wpool_in")
                if n == 8:
                    for j in range(4):
                        load_small(mod[32 * j:32 * j + 32, :, :],
                              ins["b_ada_2"][0].rearrange("(g j n) -> j g n", g=3, j=4)[j].partition_broadcast(32),
                              "bada_in")
            for name, (at, n) in VEC_ROWS.items():
                src = ins[name]
                if name in VEC_FIRST:
                    continue
                if name in ("fox_q_g_2", "fox_k_g_2", "moba_q_g_2", "moba_k_g_2"):
                    load_small(vec[at:at + 1, 0:HD], src, "vec2_in")
                    load_small(vec[at:at + 1, HD:P], src, "vec2_in")
                elif name == "ml_conv_w_2":
                    load_small(vec[at:at + n, :], src[0].rearrange("j (c p) -> (j c) p", p=P), "vec2_in")
                else:
                    load_small(vec[at:at + n, :], src.rearrange("o (k p) -> (o k) p", p=P), "vec2_in")
            for n in range(SLOTS, N_MOE):
                load(n)
                if n == SLOTS:
                    for i in range(3):
                        load_small(bdown_f[32 * i:32 * i + 32, :], ins["b_down"][0], "bdown_in")
                if n == SLOTS + 2:
                    load_small(router[:, :, :], ins["w_router"][0].rearrange("(k p) e -> p k e", p=P), "router_in")
                    load_small(brouter[:, :], ins["b_router"][0].partition_broadcast(P), "brouter_in")
                if n == N_OUT1:
                    load_small(gfin[:, :], ins["g_final"].partition_broadcast(P), "gfin_in")
                    load_small(bias14[:, 0:6], ins["fox_f_bias_2"][0].partition_broadcast(P), "bias14_in")
                    load_small(bias14[:, 6:10], ins["ml_f_bias_2"][0].partition_broadcast(P), "bias14_in")
                    load_small(bias14[:, 10:14], ins["ml_i_bias_2"][0].partition_broadcast(P), "bias14_in")
            with sp.Fori(0, EXPERTS) as e:
                for c in range(SLOTS):
                    s = (N_MOE + c) % SLOTS
                    sp.wait_ge(chunk_used, e * SLOTS + (N_MOE + c - SLOTS + 1))
                    if c < KD:
                        sp.dma_start(ring[:, s, :], gu_dram[bass.ds(e * KD + c, 1), :, :]
                                     .rearrange("o p n -> (o p) n")).then_inc(landed[s], 16)
                    else:
                        sp.dma_start(ring[:, s, :].rearrange("p (o k n) -> p o k n", o=1, k=2),
                                     dn_dram[bass.ds(e * 4 + (c - KD), 1), :, :, :]
                                     .rearrange("o p k n -> p o k n")).then_inc(landed[s], 16)
            sp.wait_ge(sig["lists_ready"], 1)
            n_over = sp.value_load(lists[0:1, 32:33], min_val=0, max_val=16)
            with sp.If(n_over > 0):
                sp.wait_ge(chunk_used, N_IN2)
                with sp.Fori(0, OVER) as j:
                    with sp.If(j < n_over):
                        e = sp.value_load(lists[0:1, bass.ds(j, 1)], min_val=0, max_val=EXPERTS - 1)
                        for c in range(SLOTS):
                            if c < KD:
                                sp.dma_start(ring[:, c, :], gu_dram[bass.ds(e * KD + c, 1), :, :]
                                             .rearrange("o p n -> (o p) n")).then_inc(sig["o_loaded"], 16)
                            else:
                                sp.dma_start(ring[:, c, :].rearrange("p (o k n) -> p o k n", o=1, k=2),
                                             dn_dram[bass.ds(e * 4 + (c - KD), 1), :, :, :]
                                             .rearrange("o p k n -> p o k n")).then_inc(sig["o_loaded"], 16)
                        sp.wait_ge(sig["o_down"], j + 1)
                        sp.sem_inc(sig["o_ring_back"], 1)
            for n in range(N_IN2, N_END):
                load(n)
            sp.wait_ge(sig["out_stored"], 16 * 4)

        @block.tensor
        def _(pe):
            def need(n):
                pe.wait_ge(landed[n % SLOTS], 16 * (n // SLOTS + 1))

            turned = [0]

            def turn_rows(wait_rows, by_tile=True):
                for t in range(NT):
                    pe.wait_ge(sig["rows_ready"], wait_rows - (NT - 1 - t if by_tile else 0))
                    for k in range(KD):
                        mm = pe.transpose(bank(k // 2)[:, (k % 2) * T + t * P:][:, 0:P],
                                          rows[:, t, k * P:(k + 1) * P], ident)
                        if t == NT - 1 and k % 2:
                            mm.then_inc(sig["rows_turned"], 1)
                turned[0] += 1

            def need_cols():
                pe.wait_ge(sig["cols_dve"], 4 * turned[0])
                pe.wait_ge(sig["cols_act"], 4 * turned[0])

            pe.wait_ge(sig["const_in"], 16)
            pe.wait_ge(sig["vec_in"], 2 * 16)
            pe.wait_ge(sig["vec_a_in"], (len(VEC_FIRST) - 2) * 16)
            pe.transpose(bank(6)[:, 0:NVEC_FIRST], vec[0:NVEC_FIRST, :],
                         ident[0:NVEC_FIRST, 0:NVEC_FIRST]).then_inc(sig["vec_turned"], 1)

            def ada(i):
                g, k = ADA_CHUNKS[i]
                if i == 0:
                    pe.wait_ge(sig["c_ready"], 1)
                elif k == 0:
                    pe.wait_ge(sig["ada_kept"], g)
                n = ada_at(i)
                need(n)
                for j in range(4):
                    mm = pe.matmul(bank(7)[32 * j:32 * j + 32, :], c_rep[:, k, :], slot(n)[:, j * 512:(j + 1) * 512],
                                   start=(k == 0), stop=(k == KD - 1))
                mm.then_inc(chunk_used, 1)

            for i in range(ADA_FIRST):
                ada(i)

            def project(chunks, base_n, banks, first, between=None):
                for c, (a, w) in enumerate(chunks):
                    n = base_n + c
                    b = banks[c % 2]
                    if c >= 2:
                        pe.wait_ge(sig["proj_kept"], first + c - 1)
                    need(n)
                    for t in range(NT):
                        for k in range(KD):
                            mm = pe.matmul(bank(b)[:, t * w:(t + 1) * w], cols[:, k, t * P:(t + 1) * P],
                                           chunk(n)[:, k, :], start=(k == 0), stop=(k == KD - 1))
                    mm.then_inc(chunk_used, 1)
                    for other in (between or {}).get(c + 1, ()):
                        other()

            turn_rows(2)
            need_cols()
            project(IN1_CHUNKS, N_IN1, (4, 5), 0)

            pe.wait_ge(sig["lat_rows"], 4)
            for i in range(3):
                for t in range(NT):
                    mm = pe.transpose(bank(i // 2)[:, (i % 2) * T + t * P:][:, 0:P],
                                      lat_rows[:, t, i * P:(i + 1) * P], ident)
            mm.then_inc(sig["lat_turned"], 1)
            for i in range(ADA_FIRST, ADA_NEXT):
                ada(i)
            pe.wait_ge(sig["proj_kept"], len(IN1_CHUNKS))
            pe.wait_ge(sig["lat_cols"], 1)
            need(N_QB)
            for b, t, at, a, w in ((4, 0, 0, 0, 512), (5, 1, 0, 0, 512), (6, 0, 0, 512, 256), (6, 1, 256, 512, 256)):
                for k in range(2):
                    mm = pe.matmul(bank(b)[:, at:at + w], lat[:, k, t * P:(t + 1) * P],
                                   chunk(N_QB)[:, k, a:a + w], start=(k == 0), stop=(k == 1))
            mm.then_inc(chunk_used, 1)
            need(N_KVB)
            for t in range(NT):
                if t:
                    pe.wait_ge(sig["qkv_kept"], 2)
                for a in (0, 512):
                    mm = pe.matmul(bank(4 * t + a // 512), lat[:, 2, t * P:(t + 1) * P],
                                   chunk(N_KVB)[:, 0, a:a + 512], start=True, stop=True)
            mm.then_inc(chunk_used, 1)
            pe.wait_ge(sig["band_in"], 16)
            for g in range(GROUPS):
                for s in range(NT):
                    mm = pe.matmul(bank(2 + g // 2)[:, (g % 2) * T:(g % 2 + 1) * T],
                                   proj1[:, s, g * P:(g + 1) * P], band_sb[:, g, s, :],
                                   start=(s == 0), stop=(s == NT - 1))
            mm.then_inc(sig["diff_done"], 1)

            def turn_heads(which, src, b):
                for h in (2 * b, 2 * b + 1):
                    for t in range(NT):
                        mm = pe.transpose(bank((0, 1, 4, 5)[b])[0:QK, (h % 2) * T + t * P:][:, 0:P],
                                          src[:, t, h, :], ident)
                mm.then_inc(sig["qk_turned"], 1)

            pe.wait_ge(sig["q_roped"], 1)
            pe.wait_ge(sig["qkv_kept"], 7)
            for b in range(4):
                turn_heads("q", q_rows, b)
            pe.wait_ge(sig["diff_kept"], 2)
            pe.wait_ge(sig["wpool_in"], 16)
            for g in range(GROUPS):
                mm = pe.matmul(bank(2 + g // 2)[:, (g % 2) * T:(g % 2 + 1) * T], wpool[:, g, :],
                               diff[:, g, :], start=True, stop=True)
            mm.then_inc(sig["mixed_done"], 1)
            pe.wait_ge(sig["k_roped"], 1)
            for b in range(4):
                pe.wait_ge(sig["q_cols"], b + 1)
                turn_heads("k", k_rows, b)
            pe.wait_ge(sig["vec2_in"], VEC_DMAS * 16)
            pe.transpose(bank(6)[:, 0:NVEC], vec[:, :], ident[0:NVEC, 0:NVEC]).then_inc(sig["vec2_turned"], 1)
            ada(ADA_NEXT)
            ada(ADA_NEXT + 1)

            def pool_sums():
                pe.wait_ge(sig["pool_sq"], 1)
                pe.wait_ge(sig["vec2_cols"], 1)
                for t in range(NT):
                    for g in range(GROUPS):
                        mm = pe.matmul(bank(6)[:, t:t + 1], pool_sq[:, g, t * P:(t + 1) * P], ones[:, 0:1],
                                       start=(g == 0), stop=(g == GROUPS - 1))
                mm.then_inc(sig["pool_sum"], 1)

            def scores(head):
                g, q, k, v, row, ml, _ = head
                s = bank(g % 2)
                if g == HEADS:
                    pe.wait_ge(sig["bias_rows"], 1)
                if g == HEADS + ML_LO:
                    pe.wait_ge(sig["conv_silu"], 4)
                if g >= 2:
                    scores_used(pe, g - 2)
                for t in range(NT):
                    a, w = (0, P) if t == 0 else (P, T)
                    pe.matmul(s[:, a:a + w], q[:, t * P:(t + 1) * P], k[:, 0:w], start=True, stop=ml)
                    d = bank(6 + g % 2) if ml else s
                    if row is not None:
                        pe.matmul(d[:, a:a + w], rowb[:, row:row + 1].to_broadcast([P, P]), bias_r[:, 0:w],
                                  start=ml, stop=False)
                    mm = pe.matmul(d[:, t * T:t * T + P], identb[:, :], maskb[:, :], start=False, stop=True)
                mm.then_inc(sig["scores_done"], 1)

            def attention(block_no, extra=None, started=0):
                heads = list(attention_heads(block_no))
                n_heads = len(heads)
                for i in range(n_heads + 2):
                    if started <= i < n_heads:
                        scores(heads[i])
                        for other in (extra or {}).get(i, ()):
                            other()
                    if 0 < i <= n_heads:
                        g = heads[i - 1][0]
                        scores_used(pe, g)
                        if g >= 2:
                            pe.wait_ge(sig["pt_kept"], g - 1)
                        elif g == 0:
                            pe.wait_ge(sig["pooled_kept"], 1)
                        for b in range(3):
                            mm = pe.transpose(bank(2 + g % 2)[:, b * P:(b + 1) * P],
                                              probs[:, g % 2, b * P:(b + 1) * P], ident)
                        mm.then_inc(sig["probs_turned"], 1)
                    if i >= 2:
                        g, _, _, v, _, _, oc = heads[i - 2]
                        pe.wait_ge(sig["pt_kept"], g + 1)
                        if g and oc == 0:
                            pe.wait_ge(sig["o_free"], 1 + [lo for lo, _ in GROUPS_OF[2]].index(i - 2))
                        pe.matmul(bank(4)[:, oc:oc + HD], pt[:, g % 2, 0:P], v(0), start=True, stop=True)
                        pe.matmul(bank(5)[:, oc:oc + HD], pt[:, g % 2, P:2 * P], v(0), start=True, stop=False)
                        mm = pe.matmul(bank(5)[:, oc:oc + HD], pt[:, g % 2, 2 * P:3 * P], v(1),
                                       start=False, stop=True)
                        mm.then_inc(sig["pv_done"], 1)

            pe.wait_ge(sig["k_cols"], 4)

            def adas(lo, hi):
                return [lambda i=i: ada(i) for i in range(lo, hi)]

            attention(1, {0: adas(6, 8), 1: adas(8, 9), 2: [pool_sums] + adas(9, 10), 3: adas(10, 12), 4: adas(12, 14),
                          5: adas(14, 16), 6: adas(16, 17), 7: adas(17, ADA_MID)})

            def out_columns(base_n, c, k, t, halves=(0, 1)):
                for h in halves:
                    mm = pe.matmul(bank(2 * t + h), cols[:, k, t * P:(t + 1) * P],
                                   chunk(base_n + c)[:, k % 2, h * 512:(h + 1) * 512],
                                   start=(k == 0), stop=(k == KD - 1))
                return mm

            def project_out_start(base_n, chunks=(0, 1)):
                for c in chunks:
                    need(base_n + c)
                    for k in (2 * c, 2 * c + 1):
                        for t in range(NT):
                            mm = out_columns(base_n, c, k, t)
                    mm.then_inc(chunk_used, 1)

            def project_out_end(base_n):
                need(base_n + 2)
                need(base_n + 3)
                for t, halves in PARTS:
                    for k in range(4, KD):
                        mm = out_columns(base_n, k // 2, k, t, halves)
                        if (t, halves) == PARTS[-1] and k % 2:
                            mm.then_inc(chunk_used, 1)
                        elif k == KD - 1:
                            mm.then_inc(sig["out_half"], 1)

            pe.wait_ge(sig["pool_cols"], 4)
            project_out_start(N_OUT1, (0,))
            pe.wait_ge(sig["att_rows"], 2)
            for f in range(4):
                for t in range(NT):
                    mm = pe.transpose(bank(4 + f // 2)[:, (f % 2) * T + t * P:][:, 0:P], att[:, t, f * P:(f + 1) * P],
                                      ident)
            mm.then_inc(sig["att_turned"], 1)
            project_out_start(N_OUT1, (1,))
            pe.wait_ge(sig["att_cols"], 4)
            project_out_end(N_OUT1)

            def turn_mod(g, b):
                pe.wait_ge(sig["ada_kept"], g + 1)
                for q in range(4):
                    mm = pe.transpose(bank(b)[:, q * P:(q + 1) * P], mod[:, g, q * P:(q + 1) * P], ident)
                mm.then_inc(sig["mod_turned"], 1)

            for i in range(ADA_MID, ADA_MID + 3):
                ada(i)
            turn_mod(0, 6)
            turn_mod(1, 5)
            ada(ADA_MID + 3)

            pe.wait_ge(sig["x_added"], 4)
            turn_rows(4)
            ada(ADA_MID + 4)
            need_cols()
            pe.wait_ge(sig["router_in"], 16)
            for k in (0, 4):
                for j in range(4):
                    mm = pe.matmul(bank(4)[32 * j:32 * j + 32, 0:T], router[:, k + j, :], cols[:, k + j, :],
                                   start=(k == 0), stop=(k == 4))
            mm.then_inc(sig["parts_done"], 1)
            ada(ADA_MID + 5)
            pe.wait_ge(sig["parts_kept"], 1)
            pe.wait_ge(sig["mod_cols"], 2)
            for t in range(NT):
                mm = pe.matmul(bank(5)[:, t * EXPERTS:(t + 1) * EXPERTS], logit_parts[:, t * P:(t + 1) * P],
                               const("pick")[:, 0:EXPERTS], start=True, stop=True)
            mm.then_inc(sig["logits_done"], 1)
            pe.wait_ge(sig["routed"], 1)
            pe.matmul(bank(5)[:, 0:32], const("tri_exc"), chosen[:, 0, :], start=True, stop=True)
            pe.matmul(bank(5)[:, 32:64], ones, chosen[:, 0, :], start=True, stop=False)
            pe.matmul(bank(5)[:, 32:64], const("tri_exc"), chosen[:, 1, :], start=False, stop=True)
            pe.matmul(bank(5)[:, 64:96], ones, chosen[:, 0, :], start=True, stop=False)
            pe.matmul(bank(5)[:, 64:96], ones, chosen[:, 1, :], start=False, stop=True).then_inc(sig["ranks_done"], 1)

            def zeros(n):
                return identb[0:1, 1:2].to_broadcast([1, n])

            def add_zero(*banks, **when):
                for b in banks:
                    mm = pe.matmul(bank(b), zeros(P), zeros(512), **when)
                return mm

            def moe_gather(done):
                for k in range(KD):
                    for t in range(NT):
                        mm = pe.matmul(bank(2)[:, k * CAP:(k + 1) * CAP], rows[:, t, k * P:(k + 1) * P],
                                       sel_g[:, t, :], start=(t == 0), stop=(t == NT - 1))
                mm.then_inc(done, 1)

            def moe_gate_up(weights, used):
                for b in range(2):
                    for h in range(2):
                        pe.matmul(bank(b)[CAP * h:CAP * (h + 1), :], sel_b[:, :],
                                  bias_b[:, b * FE + h * 512:b * FE + (h + 1) * 512], start=True, stop=False)
                for k in range(KD):
                    w = weights(k)
                    for b in range(2):
                        for h in range(2):
                            mm = pe.matmul(bank(b)[CAP * h:CAP * (h + 1), :], xg[:, k, :],
                                           w[:, b * FE + h * 512:b * FE + (h + 1) * 512],
                                           start=False, stop=(k == KD - 1))
                    used(mm, k)

            def moe_turn_sel(done):
                for t in range(NT):
                    mm = pe.transpose(bank(3)[:, t * P:(t + 1) * P], sel_s[:, t, :], ident)
                mm.then_inc(done, 1)

            def moe_turn_act(done):
                for j in range(4):
                    mm = pe.transpose(bank(0)[:, j * P:(j + 1) * P], act_buf[:, j * P:(j + 1) * P], ident)
                mm.then_inc(done, 1)

            def moe_down(weights, used):
                for h in range(2):
                    pe.matmul(bank(3)[CAP * h:CAP * (h + 1), :], sel_d[:, :], bdown_b[:, h * 512:(h + 1) * 512],
                              start=True, stop=False)
                for s in range(4):
                    w = weights(s)
                    for f in (2 * s, 2 * s + 1):
                        lhs = act_t[:, (f % 4) * P + CAP * (f // 4):][:, 0:CAP]
                        for h in range(2):
                            mm = pe.matmul(bank(3)[CAP * h:CAP * (h + 1), :], lhs,
                                           w[:, (f % 2) * D + h * 512:(f % 2) * D + (h + 1) * 512],
                                           start=False, stop=(f == 7))
                    used(mm, s)

            def moe_scatter(done, tiles=range(NT)):
                for t in tiles:
                    for h in range(2):
                        mm = pe.matmul(bank(4 + 2 * t + h), sel_t[CAP * h:CAP * (h + 1), t * P:(t + 1) * P],
                                       yb[CAP * h:CAP * (h + 1), :], start=False, stop=False)
                mm.then_inc(done, 1)

            turn_mod(2, 3)
            add_zero(4, 6, 7, start=True, stop=False)
            pe.wait_ge(sig["picked"], 1)
            moe_gather(sig["gathered"])
            add_zero(5, start=True, stop=False)
            pe.wait_ge(sig["bias_split"], 2)
            with pe.Fori(0, EXPERTS) as e:
                def ring_w(first):
                    def get(i):
                        s = (N_MOE + first + i) % SLOTS
                        pe.wait_ge(landed[s], e * 16 + 16 * ((N_MOE + first + i) // SLOTS + 1))
                        return ring[:, s, :]
                    return get

                pe.wait_ge(sig["selb_ready"], e + 1)
                pe.wait_ge(sig["xg_ready"], e + 1)
                moe_gate_up(ring_w(0), lambda mm, k: mm.then_inc(chunk_used, 1))
                pe.wait_ge(sig["yb_ready"], e + 1)
                moe_scatter(sig["scattered"])
                pe.wait_ge(sig["sel_ready"], e + 1)
                moe_turn_sel(sig["sel_turned"])
                pe.wait_ge(sig["picked"], e + 2)
                moe_gather(sig["gathered"])
                pe.wait_ge(sig["act_ready"], e + 1)
                moe_turn_act(sig["act_turned"])
                pe.wait_ge(sig["actt_ready"], e + 1)
                pe.wait_ge(sig["selt_ready"], e + 1)
                pe.wait_ge(sig["seld_ready"], e + 1)
                moe_down(ring_w(KD), lambda mm, s: mm.then_inc(chunk_used, 1))
            pe.wait_ge(sig["yb_ready"], EXPERTS + 1)
            moe_scatter(sig["o_scattered"])

            pe.wait_ge(sig["lists_ready"], 1)
            n_over = pe.value_load(lists[0:1, 32:33], min_val=0, max_val=16)
            with pe.If(n_over > 0):
                with pe.Fori(0, OVER) as j:
                    with pe.If(j < n_over):
                        pe.wait_ge(sig["o_picked"], j + 1)
                        moe_gather(sig["o_gathered"])
                        moe_turn_sel(sig["o_sel_turned"])
                        pe.wait_ge(sig["o_xg"], j + 1)
                        pe.wait_ge(sig["o_loaded"], j * (16 * SLOTS) + 16 * SLOTS)
                        moe_gate_up(lambda k: ring[:, k, :],
                                    lambda mm, k: mm.then_inc(sig["o_gu"], 1) if k == KD - 1 else None)
                        pe.wait_ge(sig["o_act"], j + 1)
                        moe_turn_act(sig["o_act_turned"])
                        pe.wait_ge(sig["o_actt"], j + 1)
                        pe.wait_ge(sig["o_selt"], j + 1)
                        moe_down(lambda s: ring[:, KD + s, :],
                                 lambda mm, s: mm.then_inc(sig["o_down"], 1) if s == 3 else None)
                        pe.wait_ge(sig["o_yb"], j + 1)
                        moe_scatter(sig["o_scattered"])
            for t in range(NT):
                add_zero(4 + 2 * t, 5 + 2 * t, start=False, stop=True).then_inc(sig["moe_done"], 1)

            turn_rows(6)
            need_cols()

            def turn_soft(i):
                pe.wait_ge(sig["heads_ready"], 2 if i < 3 else 4)
                if i >= 2:
                    pe.wait_ge(sig["heads_cols"], i - 1)
                for f in (2 * i, 2 * i + 1):
                    c = (C_FQ + f * P) if f < 6 else (C_BQ + (f - 6) * P)
                    for t in range(NT):
                        mm = pe.transpose(bank(i % 2)[:, (f % 2) * T + t * P:][:, 0:P], proj[:, t, c:c + P], ident)
                mm.then_inc(sig["heads_turned"], 1)

            def sum_decay():
                pe.wait_ge(sig["decay_ready"], 1)
                pe.matmul(bank(6)[:, 0:10], const("tri_inc"), logf[:, 0, :], start=True, stop=True)
                pe.matmul(bank(6)[:, 16:26], ones, logf[:, 0, :], start=True, stop=False)
                pe.matmul(bank(6)[:, 16:26], const("tri_inc"), logf[:, 1, :], start=False, stop=True).then_inc(
                    sig["cum_done"], 1)

            def turn_bias():
                pe.wait_ge(sig["cum_kept"], 1)
                for t in range(NT):
                    mm = pe.transpose(bank(7)[0:48, t * P:(t + 1) * P], bias_p[:, t, :], ident)
                mm.then_inc(sig["cumt_turned"], 1)

            def turn_conv():
                pe.wait_ge(sig["proj_kept"], len(IN1_CHUNKS) + R_CONV)
                for f in range(4):
                    for t in range(NT):
                        mm = pe.transpose(bank(2 + f // 2)[:, (f % 2) * T + t * P:][:, 0:P],
                                          proj[:, t, C_MQ + f * P:C_MQ + (f + 1) * P], ident)
                mm.then_inc(sig["conv_turned"], 1)

            between = {}
            for i in range(3):
                between.setdefault(R_FOX + 2 + i, []).append(lambda i=i: turn_soft(i))
                between.setdefault(R_MOBA + 2 + i, []).append(lambda i=i: turn_soft(3 + i))
            between.setdefault(R_GATES + 1, []).append(sum_decay)
            between.setdefault(R_GATES + 2, []).append(turn_bias)
            between.setdefault(R_CONV + 1, []).append(turn_conv)

            def first_scores():
                pe.wait_ge(sig["heads_cols"], 6)
                for head in list(attention_heads(2))[:2]:
                    scores(head)

            between[R_CONV + 1].append(first_scores)
            project(IN2_CHUNKS, N_IN2, (4, 5), len(IN1_CHUNKS), between)
            pe.wait_ge(sig["proj_kept"], len(IN1_CHUNKS) + len(IN2_CHUNKS))
            attention(2, started=2)

            def spread(g, j0, first, halves=(0, 1)):
                if first:
                    pe.wait_ge(sig["bcast_kept"], first)
                for i in halves:
                    j = j0 + i
                    mm = pe.matmul(bank(6 + i), ident[:, 32 * j:32 * j + 1].to_broadcast([P, P]), mod[:, g, :],
                                   start=True, stop=True)
                if halves[-1] == 1:
                    mm.then_inc(sig["bcast_done"], 1)

            spread(1, 0, 0, (0,))
            pe.wait_ge(sig["o_free"], 4)
            turn_rows(7, by_tile=False)
            spread(1, 0, 0, (1,))
            need_cols()
            project_out_start(N_OUT2)
            project_out_end(N_OUT2)
            spread(2, 2, 1)
            pe.wait_ge(sig["gate_used"], 4)
            turn_rows(9)
            need_cols()

            for j in range(PAIRS + 1):
                if j < PAIRS:
                    if j >= 2:
                        pe.wait_ge(sig["h_ready"], j - 1)
                    if j == 1:
                        pe.wait_ge(sig["bcast_kept"], 2)
                    for up in range(2):
                        n = N_GU2 + 2 * j + up
                        need(n)
                        for t in range(NT):
                            for k in range(KD):
                                mm = pe.matmul(bank(4 + 2 * (j % 2) + up)[:, t * CW:(t + 1) * CW],
                                               cols[:, k, t * P:(t + 1) * P], chunk(n)[:, k, :],
                                               start=(k == 0), stop=(k == KD - 1))
                        mm.then_inc(chunk_used, 1)
                if j >= 1:
                    i = j - 1
                    pe.wait_ge(sig["h_ready"], i + 1)
                    if i >= 2:
                        pe.wait_ge(sig["h_cols"], i - 1)
                    for f in range(2):
                        for t in range(NT):
                            mm = pe.transpose(bank(i % 2)[:, f * T + t * P:][:, 0:P],
                                              h_rows[:, i % 2, t * CW + f * P:t * CW + (f + 1) * P], ident)
                    mm.then_inc(sig["h_turned"], 1)
            def down_columns(f, t, halves=(0, 1)):
                for h in halves:
                    mm = pe.matmul(bank(4 + 2 * t + h), h_t[:, f, t * P:(t + 1) * P],
                                   chunk(N_DN2 + f // 2)[:, f % 2, h * 512:(h + 1) * 512],
                                   start=(f == 0), stop=(f == FT - 1))
                return mm

            pe.wait_ge(sig["h_cols"], PAIRS)
            for c in range(FT // 2 - 2):
                need(N_DN2 + c)
                for f in (2 * c, 2 * c + 1):
                    for t in range(NT):
                        mm = down_columns(f, t)
                mm.then_inc(chunk_used, 1)
            need(N_END - 2)
            need(N_END - 1)
            for t, halves in PARTS:
                for f in range(FT - 4, FT):
                    mm = down_columns(f, t, halves)
                    if (t, halves) == PARTS[-1] and f % 2:
                        mm.then_inc(chunk_used, 1)
                    elif f == FT - 1:
                        mm.then_inc(sig["out_half"], 1)

        @block.scalar
        def _(act):
            do = Steps(act, act_own, sig)

            for name in VEC_FIRST[2:]:
                at, n = VEC_ROWS[name]
                src = ins[name][0] if name == "b_pool" else ins[name].rearrange("o (k p) -> (o k) p", p=P)
                act.dma_start(vec[at:at + n, :], src).then_inc(sig["vec_a_in"], 16)

            turned = [0]

            def keep_cols(scale, shift=None):
                turned[0] += 1
                for k in range(4, KD):
                    act.wait_ge(sig["rows_turned"], 4 * (turned[0] - 1) + k // 2 + 1)
                    ins_ = nc.scalar.activation(cols[:, k, :], bank(k // 2)[:, (k % 2) * T:(k % 2 + 1) * T],
                                                ACT.Identity, scale=scale(k) if scale else 1.0,
                                                bias=shift(k) if shift else 0.0)
                    do.tell(ins_, "cols_act")

            act.wait_ge(sig["vec_cols"], 1)
            a = VEC_ROWS["c_2"][0]
            do.tell(nc.scalar.activation(c_rep[:, :, :], vcol[:, a:a + KD].unsqueeze(2).to_broadcast([P, KD, 32]),
                                         ACT.Silu), "c_ready")
            keep_cols(lambda k: col("g_attn_norm", k))

            def keep_proj(dst, chunks, banks, base_n, between=None):
                for c, (a, w) in enumerate(chunks):
                    act.wait_ge(chunk_used, base_n + c + 1)
                    do.tell(nc.scalar.copy(dst[:, :, a:a + w],
                                           bank(banks[c % 2])[:, 0:NT * w].rearrange("p (t n) -> p t n", t=NT)),
                            "proj_kept")
                    for other in (between or {}).get(c + 1, ()):
                        other()

            act.wait_ge(sig["trig_arg"], 1)
            do.tell(nc.scalar.activation(trig[:, :, :, :], trig[:, :, :, :], ACT.Sin), "trig_ready")
            keep_proj(proj1, IN1_CHUNKS, (4, 5), N_IN1)
            flat_q = q_rows.rearrange("p t h n -> p t (h n)")
            flat_kv = kv_rows.rearrange("p t h n -> p t (h n)")
            act.wait_ge(chunk_used, N_QB + 1)
            for t in range(NT):
                do.tell(nc.scalar.copy(flat_q[:, t, 0:512], bank(4 + t)), "qkv_kept")
            do.tell(nc.scalar.copy(flat_q[:, :, 512:768], bank(6).rearrange("p (t n) -> p t n", t=NT)), "qkv_kept")
            act.wait_ge(chunk_used, N_KVB + 1)
            for t in range(NT):
                for a in (0, 512):
                    do.tell(nc.scalar.copy(flat_kv[:, t, a:a + 512], bank(4 * t + a // 512)), "qkv_kept")
            act.wait_ge(sig["diff_done"], 1)
            for b in range(2):
                do.tell(nc.scalar.copy(diff[:, 2 * b:2 * b + 2, :],
                                       bank(2 + b).rearrange("p (g t) -> p g t", g=2)), "diff_kept")
            act.wait_ge(sig["bias_split"], 1)
            for b in range(4):
                act.wait_ge(sig["qk_turned"], b + 1)
                do.tell(nc.scalar.copy(qk[0:QK, 2 * b:2 * b + 2, :],
                                       bank((0, 1, 4, 5)[b])[0:QK, :].rearrange("p (h t) -> p h t", h=2)), "q_cols")

            def exps(i, head):
                g, _, _, _, _, ml, _ = head
                b = g % 2
                src = bank(6 + b) if ml else bank(b)
                dst = ml_e if ml else probs[:, b, :]
                act.wait_ge(sig["rowmax_ready"], g + 1)
                if ml:
                    if is_ml(g - 1):
                        scores_used(act, g - 1)
                elif g >= 2:
                    act.wait_ge(sig["probs_turned"], g - 1)
                for t in range(NT):
                    a, w = (0, P) if t == 0 else (P, T)
                    kw = {} if ml else {"accum_out": psum_row[:, i, t:t + 1]}
                    ins_ = nc.scalar.activation(dst[:, a:a + w], src[:, a:a + w], ACT.Exp, bias=nmax[:, i, t:t + 1],
                                                scale=1.0 if ml else ATT_SCALE[1 if g < HEADS else 2], **kw)
                    if t == 0:
                        do.step(ins_)
                    elif ml:
                        do.tell(ins_, "ml_exp")
                    else:
                        do.tell(ins_, "probs_ready")

            def attention(block_no, extra=None, started=0):
                heads = list(attention_heads(block_no))
                n_heads = len(heads)
                for i in range(n_heads + 1):
                    if started <= i < n_heads:
                        exps(i, heads[i])
                    if i:
                        g = heads[i - 1][0]
                        act.wait_ge(sig["probs_turned"], g + 1)
                        if g >= 2:
                            act.wait_ge(sig["pv_done"], g - 1)
                        do.tell(nc.scalar.copy(pt[:, g % 2, :], bank(2 + g % 2)[:, 0:384]), "pt_kept")
                    for other in (extra or {}).get(i, ()):
                        other()

            attention(1)
            act.wait_ge(sig["att_turned"], 1)
            for f in range(4):
                do.tell(nc.scalar.activation(cols[:, 4 + f, :], bank(4 + f // 2)[:, (f % 2) * T:(f % 2 + 1) * T],
                                             ACT.Copy, scale=col("g_out_attn", f)), "att_cols")
            keep_cols(lambda k: col("g_ffn_norm", k))
            act.wait_ge(sig["shifted"], 1)
            for t in range(NT):
                do.step(nc.scalar.activation(gexp[:, t, :], lg[:, t, 0:EXPERTS], ACT.Exp, bias=small[:, t:t + 1]))
            for t in range(NT):
                ins_ = nc.scalar.activation(small[:, 8 + 4 * t:12 + 4 * t], top[:, t, 4:8], ACT.Exp,
                                            bias=small[:, t:t + 1], accum_out=small[:, 2 + t:3 + t])
                do.tell(ins_, "exp_ready")

            def keep_sel(done):
                return nc.scalar.copy(sel_t, bank(3)[:, 0:T]).then_inc(done, 1)

            def sigmoid(done):
                return nc.scalar.activation(sg, g_min, ACT.Sigmoid, scale=ALPHA).then_inc(done, 1)

            def keep_act(done):
                return nc.scalar.copy(act_t, bank(0)).then_inc(done, 1)

            def keep_y(done):
                return nc.scalar.copy(yb, bank(3)).then_inc(done, 1)

            nc.scalar.activation(sel_t, const("iota")[:, 0:T], ACT.Copy, scale=0.0)
            nc.scalar.activation(yb, const("iota"), ACT.Copy, scale=0.0).then_inc(sig["yb_ready"], 1)
            with act.Fori(0, EXPERTS) as e:
                act.wait_ge(sig["clipped"], e + 1)
                sigmoid(sig["sig_ready"])
                act.wait_ge(sig["sel_turned"], e + 1)
                act.wait_ge(sig["scattered"], e + 1)
                keep_sel(sig["selt_ready"])
                act.wait_ge(sig["act_turned"], e + 1)
                keep_act(sig["actt_ready"])
                act.wait_ge(chunk_used, e * SLOTS + (N_MOE + SLOTS))
                keep_y(sig["yb_ready"])
            act.wait_ge(sig["lists_ready"], 1)
            n_over = act.value_load(lists[0:1, 32:33], min_val=0, max_val=16)
            with act.If(n_over > 0):
                with act.Fori(0, OVER) as j:
                    with act.If(j < n_over):
                        act.wait_ge(sig["o_sel_turned"], j + 1)
                        act.wait_ge(sig["o_scattered"], j + 1)
                        keep_sel(sig["o_selt"])
                        act.wait_ge(sig["o_clipped"], j + 1)
                        sigmoid(sig["o_sig"])
                        act.wait_ge(sig["o_act_turned"], j + 1)
                        keep_act(sig["o_actt"])
                        act.wait_ge(sig["o_down"], j + 1)
                        keep_y(sig["o_yb"])

            for i in range(2 * NT):
                t = i % NT
                act.wait_ge(sig["x_summed" if i < NT else "z_ready"], t + 1)
                do.tell(nc.scalar.activation(rows[:, t, :], x_sb[:, t, :] if i < NT else z_rows[t], ACT.Square,
                                             accum_out=stat(ms, S_FINAL if i < NT else S_NORM1)[:, t:t + 1]),
                        "x_squared")
            act.wait_ge(sig["r_ready"], 1)
            for t in range(NT):
                do.tell(nc.scalar.activation(x_sb[:, t, :], z_rows[t], ACT.Copy, scale=stat(rs, S_FINAL)[:, t:t + 1]),
                        "x_scaled")

            keep_cols(lambda k: modg[:, k:k + 1], lambda k: modc[:, k:k + 1])

            def log_sigmoid():
                act.wait_ge(sig["ff_ready"], 1)
                do.step(nc.scalar.activation(logf, logf, ACT.Exp))
                do.tell(nc.scalar.activation(logf, logf, ACT.Ln, bias=1.0), "ff_ln")

            def squares(i):
                c = (C_FQ, C_BQ)[i]
                for t in range(NT):
                    n = 2 * i + t
                    if n >= 2:
                        act.wait_ge(sig["sq_used"], n - 1)
                    do.tell(nc.scalar.activation(sq_buf[n % 2], proj[:, t, c:c + 768], ACT.Square), "qk_sq")

            def keep_soft(i):
                act.wait_ge(sig["heads_turned"], i + 1)
                gname = ("fox_q_g_2", "fox_k_g_2", "moba_q_g_2", "moba_k_g_2")
                for f in (2 * i, 2 * i + 1):
                    ins_ = nc.scalar.activation(qk[:, f, :], bank(i % 2)[:, (f % 2) * T:(f % 2 + 1) * T], ACT.Copy,
                                                scale=col(gname[f // 3]))
                    if f % 2:
                        do.tell(ins_, "heads_cols")
                    else:
                        do.step(ins_)

            def keep_conv():
                act.wait_ge(sig["conv_turned"], 1)
                for b in range(2):
                    do.tell(nc.scalar.copy(conv_x[:, 2 * b:2 * b + 2, 3:3 + T],
                                           bank(2 + b).rearrange("p (c t) -> p c t", c=2)), "conv_in")

            between = {R_FOX: [lambda: squares(0)], R_MOBA: [lambda: squares(1)]}
            for i in range(3):
                between.setdefault(R_FOX + 2 + i, []).append(lambda i=i: keep_soft(i))
                between.setdefault(R_MOBA + 2 + i, []).append(lambda i=i: keep_soft(3 + i))
            between.setdefault(R_GATES, []).append(log_sigmoid)
            between.setdefault(R_CONV + 1, []).append(keep_conv)
            for i, head in enumerate(list(attention_heads(2))[:2]):
                between[R_CONV + 1].append(lambda i=i, head=head: exps(i, head))
            keep_proj(proj, IN2_CHUNKS, (4, 5), N_IN2, between)

            def conv_tanhs(*channels):
                for c in channels:
                    act.wait_ge(sig["conv_sum"], c + 1)
                    do.tell(nc.scalar.activation(conv_x[:, c, 0:T], qk[:, 12 + c, :], ACT.Tanh, scale=0.5),
                            "conv_tanh")

            def ml_finish():
                act.wait_ge(sig["ml_m"], 1)
                do.tell(nc.scalar.activation(guard, guard, ACT.Exp, scale=-1.0), "ml_guard")
                do.tell(nc.scalar.activation(proj[:, :, C_MO:C_MO + 256], proj[:, :, C_MO:C_MO + 256], ACT.Tanh,
                                             scale=0.5), "ml_tanh")

            attention(2, {2: [lambda: conv_tanhs(0, 1)], 3: [lambda: conv_tanhs(2, 3)], ML_HI + 1: [ml_finish]}, started=2)

            def keep_bcast(n):
                act.wait_ge(sig["bcast_done"], n)
                do.step(nc.scalar.copy(gate_b[:, 0:512], bank(6)))
                do.tell(nc.scalar.copy(gate_b[:, 512:1024], bank(7)), "bcast_kept")

            keep_cols(lambda k: col("ml_h_g_2", 1) if k == 4 else 1.0)
            keep_bcast(1)
            keep_cols(lambda k: modg[:, 8 + k:9 + k], lambda k: modc[:, 24 + k:25 + k])
            act.wait_ge(sig["gate_used"], 4)
            keep_bcast(2)
            for j in range(PAIRS + 1):
                if j < PAIRS:
                    act.wait_ge(chunk_used, N_GU2 + 2 * j + 1)
                    if j >= 2:
                        act.wait_ge(sig["h_ready"], j - 1)
                    do.tell(nc.scalar.activation(h_sil[:, j % 2, :], bank(4 + 2 * (j % 2)), ACT.Silu), "silu_ready")
                if j >= 1:
                    i = j - 1
                    act.wait_ge(sig["h_turned"], i + 1)
                    do.tell(nc.scalar.copy(h_t[:, 2 * i:2 * i + 2, :],
                                           bank(i % 2).rearrange("p (f t) -> p f t", f=2)), "h_cols")
            for i in range(4):
                t, h = divmod(i, 2)
                act.wait_ge(sig["out_ready"], i + 1)
                act.dma_start(out[0, t * P:(t + 1) * P, h * 512:(h + 1) * 512],
                              x_sb[:, t, h * 512:(h + 1) * 512]).then_inc(sig["out_stored"], 16)
            act.wait_ge(sig["out_stored"], 16 * 4)

        @block.vector
        def _(dve):
            v = nc.vector
            do = Steps(dve, dve_own, sig)

            def rsqrt(dst, src, tmp):
                do.step(v.tensor_scalar(dst.bitcast(I32), src.bitcast(I32), 1, None, ALU.logical_shift_right))
                do.step(v.tensor_scalar(dst.bitcast(I32), dst.bitcast(I32), -1.0, RSQRT_GUESS, ALU.mult, ALU.add))
                for _ in range(3):
                    do.step(v.tensor_tensor(tmp, dst, src, ALU.mult))
                    do.step(v.scalar_tensor_tensor(out=tmp, in0=tmp, scalar=-0.5, in1=dst, op0=ALU.mult, op1=ALU.mult))
                    do.step(v.scalar_tensor_tensor(out=dst, in0=tmp, scalar=1.5, in1=dst, op0=ALU.add, op1=ALU.mult))

            def rstd(request, n, first=0, width=None):
                at = slice(first, first + (width or STAT_W[request]))
                src, dst = stat(ms, request)[:, at], stat(rs, request)[:, at]
                do.step(v.tensor_scalar(src, src, 1.0 / n, EPS, ALU.mult, ALU.add))
                rsqrt(dst, src, rsqrt_tmp[:, 0:at.stop - at.start])
                return dst

            def norm_rows(request, t):
                do.step(v.tensor_tensor_reduce(out=rows[:, t, :], in0=x_sb[:, t, :], in1=x_sb[:, t, :], scale=1.0,
                                               scalar=0.0, op0=ALU.mult, op1=ALU.add,
                                               accum_out=stat(ms, request)[:, t:t + 1]))
                r_ = rstd(request, D, t, 1)
                do.tell(v.tensor_scalar(rows[:, t, :], x_sb[:, t, :], r_, None, ALU.mult), "rows_ready")

            turned = [0]

            def keep_cols(scale, shift=None):
                turned[0] += 1
                for k in range(4):
                    dve.wait_ge(sig["rows_turned"], 4 * (turned[0] - 1) + k // 2 + 1)
                    src = bank(k // 2)[:, (k % 2) * T:(k % 2 + 1) * T]
                    if shift:
                        ins_ = v.tensor_scalar(cols[:, k, :], src, scale(k), shift(k), ALU.mult, ALU.add)
                    else:
                        ins_ = v.tensor_scalar(cols[:, k, :], src, scale(k), None, ALU.mult)
                    do.tell(ins_, "cols_dve")

            dve.wait_ge(sig["x0_in"], 16)
            norm_rows(S_ATTN, 0)
            dve.wait_ge(sig["vec_turned"], 1)
            do.tell(v.tensor_copy(vcol[:, 0:NVEC_FIRST], bank(6)[:, 0:NVEC_FIRST]), "vec_cols")
            dve.wait_ge(sig["x1_in"], 16)
            norm_rows(S_ATTN, 1)
            keep_cols(lambda k: col("g_attn_norm", k))
            dve.wait_ge(sig["const_in"], 16)
            dve.wait_ge(sig["const2_in"], 16)
            do.step(v.tensor_copy(identb[:, :], ident))
            do.step(v.tensor_copy(rowb[:, :], const("bias_row")))
            do.step(v.tensor_copy(maskb[:, :], const("mask")))

            dve.wait_ge(sig["pos_in"], 16)
            do.step(v.tensor_copy(ms[:, 0:NT], pos_i[:, :]))
            for t in range(NT):
                do.step(v.tensor_scalar(ang[:, t, :], const("inv"), ms[:, t:t + 1], None, ALU.mult))
            do.step(v.tensor_scalar(turns, ang, INV_2PI, None, ALU.mult))
            do.step(v.tensor_scalar(turns, turns, ROUND, None, ALU.add))
            do.step(v.tensor_scalar(turns, turns, -ROUND, None, ALU.add))
            for part in TWO_PI:
                do.step(v.scalar_tensor_tensor(out=ang, in0=turns, scalar=-part, in1=ang, op0=ALU.mult, op1=ALU.add))
            do.step(v.tensor_scalar(trig[:, 0, :, :], ang, PI_IN, -PI_IN, ALU.min, ALU.max))
            do.step(v.scalar_tensor_tensor(out=ang, in0=trig[:, 0, :, :], scalar=-1.0, in1=trig[:, 0, :, :],
                                           op0=ALU.mult, op1=ALU.min))
            do.tell(v.tensor_scalar(trig[:, 1, :, :], ang, HALF_PI, None, ALU.add), "trig_arg")

            dve.wait_ge(sig["proj_kept"], 2)
            st = stat(ms, S_LAT)
            for i, (a, w) in enumerate(((D_POOL, Q_LORA), (D_POOL + Q_LORA, KV_LORA))):
                for t in range(NT):
                    do.step(v.tensor_tensor_reduce(out=lat_rows[:, t, a - D_POOL:a - D_POOL + w],
                                                   in0=proj1[:, t, a:a + w], in1=proj1[:, t, a:a + w], scale=1.0 / w,
                                                   scalar=0.0, op0=ALU.mult, op1=ALU.add,
                                                   accum_out=st[:, 2 * i + t:2 * i + t + 1]))
            r_ = rstd(S_LAT, 1)
            for i, (a, w) in enumerate(((D_POOL, Q_LORA), (D_POOL + Q_LORA, KV_LORA))):
                for t in range(NT):
                    do.tell(v.tensor_scalar(lat_rows[:, t, a - D_POOL:a - D_POOL + w], proj1[:, t, a:a + w],
                                            r_[:, 2 * i + t:2 * i + t + 1], None, ALU.mult), "lat_rows")
            dve.wait_ge(sig["lat_turned"], 1)
            for i in range(3):
                g_ = col("g_q_a", i) if i < 2 else col("g_kv_a")
                ins_ = v.tensor_scalar(lat[:, i, :], bank(i // 2)[:, (i % 2) * T:(i % 2 + 1) * T], g_, None, ALU.mult)
                if i < 2:
                    do.step(ins_)
                else:
                    do.tell(ins_, "lat_cols")

            def rope(x1, x2, y1, y2, heads_n):
                cos, sin = (trig[:, i, :, :].unsqueeze(2).to_broadcast([P, NT, heads_n, HALF]) for i in (1, 0))
                tmp = [r[:, :, 0:heads_n, :] for r in rope_tmp]
                for dst, a_, b_ in zip(tmp, (x1, x2, x2, x1), (cos, sin, cos, sin)):
                    do.step(v.tensor_tensor(dst, a_, b_, ALU.mult))
                return (v.tensor_tensor(y1, tmp[0], tmp[1], ALU.subtract), v.tensor_tensor(y2, tmp[2], tmp[3], ALU.add))

            dve.wait_ge(sig["trig_ready"], 1)
            k1 = proj1[:, :, IN1 - ROPE:IN1 - HALF].unsqueeze(2)
            k2 = proj1[:, :, IN1 - HALF:IN1].unsqueeze(2)
            for ins_ in rope(k1, k2, k1, k2, 1):
                do.step(ins_)
            dve.wait_ge(sig["rows_turned"], 4)
            for t in range(NT):
                do.step(v.tensor_copy(k_rows[:, t, :, NOPE:QK],
                                      proj1[:, t, IN1 - ROPE:IN1].unsqueeze(1).to_broadcast([P, HEADS, ROPE])))
            dve.wait_ge(sig["qkv_kept"], 3)
            q1, q2 = q_rows[:, :, :, NOPE:NOPE + HALF], q_rows[:, :, :, NOPE + HALF:QK]
            a_, b_ = rope(q1, q2, q1, q2, HEADS)
            do.step(a_)
            do.tell(b_, "q_roped")
            dve.wait_ge(sig["qkv_kept"], 7)
            do.tell(v.tensor_copy(k_rows[:, :, :, 0:NOPE], kv_rows[:, :, :, 0:NOPE]), "k_roped")

            dve.wait_ge(sig["mixed_done"], 1)
            for g in range(GROUPS):
                (do.step if g < GROUPS - 1 else lambda i_: do.tell(i_, "pooled_kept"))(v.tensor_scalar(pooled[:, g, :], bank(2 + g // 2)[:, (g % 2) * T:(g % 2 + 1) * T],
                                        col("b_pool", g), col("pool_scale", g), ALU.add, ALU.mult))
            for b in range(4):
                dve.wait_ge(sig["qk_turned"], 4 + b + 1)
                do.tell(v.tensor_copy(qk[0:QK, 8 + 2 * b:8 + 2 * b + 2, :],
                                      bank((0, 1, 4, 5)[b])[0:QK, :].rearrange("p (h t) -> p h t", h=2)), "k_cols")
            dve.wait_ge(sig["vec2_turned"], 1)
            do.tell(v.tensor_copy(vcol[:, NVEC_FIRST:NVEC], bank(6)[:, NVEC_FIRST:NVEC]), "vec2_cols")

            def square_pooled():
                do.tell(v.tensor_tensor(pool_sq, pooled, pooled, ALU.mult), "pool_sq")

            def keep_pooled():
                for g in range(GROUPS):
                    do.tell(v.tensor_scalar(cols[:, g, :], pooled[:, g, :], col("g_out_pool", g), None, ALU.mult),
                            "pool_cols")

            def keep_pool_sums():
                dve.wait_ge(sig["pool_sum"], 1)
                do.step(v.tensor_copy(stat(ms, S_MIX)[:, 0:NT], bank(6)[:, 0:NT]))

            def keep_ada(g):
                dve.wait_ge(sig["bada_in"], 64)
                dve.wait_ge(chunk_used, ada_at(KD * g + KD - 1) + 1)
                do.tell(v.tensor_tensor(mod[:, g, :], bank(7), mod[:, g, :], ALU.add), "ada_kept")

            def row_max(i, head):
                g, _, _, _, _, ml, _ = head
                src = bank((6 if ml else 0) + g % 2)
                dve.wait_ge(sig["scores_done"], g + 1)
                do.step(v.tensor_reduce(rmax[:, i, 0:1], src[:, 0:P], AX.X, ALU.max))
                do.step(v.tensor_reduce(rmax[:, i, 1:2], src[:, P:3 * P], AX.X, ALU.max))
                if not ml:
                    do.tell(v.tensor_scalar(nmax[:, i, :], rmax[:, i, :], -ATT_SCALE[1 if g < HEADS else 2], None,
                                            ALU.mult), "rowmax_ready")
                    return
                do.tell(v.tensor_scalar(nmax[:, i, :], rmax[:, i, :], 0.0, -1.0, ALU.max, ALU.mult), "rowmax_ready")
                dve.wait_ge(sig["ml_exp"], i - ML_LO + 1)
                dve.wait_ge(sig["probs_turned"], g - 1)
                for t in range(NT):
                    a, w = (0, P) if t == 0 else (P, T)
                    ins_ = v.tensor_tensor_reduce(
                        out=probs[:, g % 2, a:a + w], in0=bank(g % 2)[:, a:a + w], in1=ml_e[:, a:a + w],
                        scale=0.25 * float(HD) ** -0.5, scalar=0.0, op0=ALU.mult, op1=ALU.add,
                        accum_out=psum_row[:, i, t:t + 1])
                    if t:
                        do.tell(ins_, "smat_ready")
                    else:
                        do.step(ins_)

            def group_end(lo, hi, last):
                g = last[0]
                n = hi - lo
                scores_used(dve, g)
                if not is_ml(g):
                    do.step(v.reciprocal(den_all[:, lo:hi, :], psum_row[:, lo:hi, :]))
                else:
                    do.step(v.tensor_scalar(guard, nmax[:, lo:hi, :], -1.0, None, ALU.mult))
                    do.tell(v.tensor_tensor(guard, guard, cum[:, :, 6:10].rearrange("p t h -> p h t"), ALU.add),
                            "ml_m")
                    dve.wait_ge(sig["ml_guard"], 1)
                    do.step(v.scalar_tensor_tensor(out=den, in0=psum_row[:, lo:hi, :], scalar=-1.0,
                                                   in1=psum_row[:, lo:hi, :], op0=ALU.mult, op1=ALU.max))
                    do.step(v.tensor_tensor(den, den, guard, ALU.max))
                    do.step(v.reciprocal(den_all[:, lo:hi, :], den))
                dve.wait_ge(sig["pv_done"], g + 1)
                at = OUT_AT[lo]
                for t in range(NT):
                    ins_ = v.tensor_tensor(rows[:, t, at:at + n * HD].rearrange("p (h d) -> p h d", h=n),
                                           bank(4 + t)[:, 0:n * HD].rearrange("p (h d) -> p h d", h=n),
                                           den_all[:, lo:hi, t:t + 1].to_broadcast([P, n, HD]), ALU.mult)
                    if t:
                        do.tell(ins_, "o_free")
                    else:
                        do.step(ins_)

            def attention(block_no, extra=None, started=0):
                heads = list(attention_heads(block_no))
                for i, head in enumerate(heads):
                    if i >= started:
                        row_max(i, head)
                    for other in (extra or {}).get(i, ()):
                        other()
                    for lo, hi in GROUPS_OF[block_no]:
                        if i == hi + 1:
                            group_end(lo, hi, heads[hi - 1])
                lo, hi = GROUPS_OF[block_no][-1]
                group_end(lo, hi, heads[-1])

            attention(1, {0: [lambda: keep_ada(0), square_pooled], 1: [keep_pooled], 3: [keep_pool_sums],
                          5: [lambda: keep_ada(1)]})
            st = stat(ms, S_MIX)
            for t in range(NT):
                do.step(v.tensor_tensor_reduce(out=rows[:, t, 512:1024], in0=att[:, t, :], in1=att[:, t, :], scale=1.0,
                                               scalar=0.0, op0=ALU.mult, op1=ALU.add,
                                               accum_out=st[:, NT + t:NT + t + 1]))
            r_mix = rstd(S_MIX, 512)
            ratio = small[:, 120:120 + NT]
            do.step(v.reciprocal(ratio, r_mix[:, 0:NT]))
            do.step(v.tensor_tensor(ratio, ratio, r_mix[:, NT:2 * NT], ALU.mult))
            for t in range(NT):
                do.tell(v.tensor_scalar(att[:, t, :], att[:, t, :], ratio[:, t:t + 1], None, ALU.mult), "att_rows")

            def part_done(product, t, h, last_chunk):
                if (t, h) == (NT - 1, 1):
                    dve.wait_ge(chunk_used, last_chunk)
                elif (t, h) != (0, 1):
                    dve.wait_ge(sig["out_half"], 2 * product + 1 + t)

            for t in range(NT):
                for h in range(2):
                    part_done(0, t, h, N_OUT1 + 4)
                    xs = x_sb[:, t, h * 512:(h + 1) * 512]
                    do.tell(v.scalar_tensor_tensor(out=xs, in0=bank(2 * t + h), scalar=r_mix[:, t:t + 1], in1=xs,
                                                   op0=ALU.mult, op1=ALU.add), "x_added")
                norm_rows(S_FFN, t)

            def keep_mod(g, b):
                dve.wait_ge(sig["mod_turned"], g + 1)
                do.tell(v.tensor_copy(modc[:, 16 * g:16 * g + 16].rearrange("p (j q) -> p j q", j=4),
                                      bank(b).rearrange("p (q j r) -> p j q r", q=4, j=4)[:, :, :, 0]), "mod_cols")

            def norm_gain(i, at, name):
                a = VEC_ROWS[name][0]
                do.step(v.scalar_tensor_tensor(out=modg[:, 8 * i:8 * i + 8], in0=modc[:, at:at + 8], scalar=1.0,
                                               in1=vcol[:, a:a + 8], op0=ALU.add, op1=ALU.mult))

            keep_mod(0, 6)
            keep_mod(1, 5)
            keep_cols(lambda k: col("g_ffn_norm", k))

            do.step(v.memset(lg[:, :, EXPERTS:EXPERTS + 4], BIG))
            do.step(v.memset(rank[:, :, :], -1.0))
            do.step(v.memset(gates[:, :, :], 0.0))
            dve.wait_ge(sig["parts_done"], 1)
            do.tell(v.tensor_copy(logit_parts, bank(4)[:, 0:T]), "parts_kept")
            dve.wait_ge(sig["logits_done"], 1)
            dve.wait_ge(sig["brouter_in"], 16)
            do.step(v.tensor_tensor(lg[:, :, 0:EXPERTS],
                                    bank(5)[:, 0:NT * EXPERTS].rearrange("p (t e) -> p t e", t=NT),
                                    brouter[:, :].unsqueeze(1).to_broadcast([P, NT, EXPERTS]), ALU.add))
            for t in range(NT):
                do.step(v.max(top[:, t, :], lg[:, t, :]))
                do.step(v.match_replace(out=lr[:, t, :], in_to_replace=top[:, t, :], in_values=lg[:, t, :],
                                        imm_value=-BIG))
            do.step(v.tensor_scalar(small[:, 0:NT], top[:, :, 4], -1.0, None, ALU.mult))
            do.tell(v.tensor_tensor(chosen, lr[:, :, 0:EXPERTS], lg[:, :, 0:EXPERTS], ALU.not_equal), "routed")
            do.tell(v.tensor_copy(small[:, 4:6], small[:, 0:2]), "shifted")
            keep_ada(2)
            dve.wait_ge(sig["exp_ready"], 2)
            do.step(v.reciprocal(small[:, 4:6], small[:, 2:4]))
            for t in range(NT):
                do.step(v.scalar_tensor_tensor(out=gates[:, t, 0:EXPERTS], in0=gexp[:, t, :],
                                               scalar=small[:, 4 + t:5 + t], in1=chosen[:, t, :],
                                               op0=ALU.mult, op1=ALU.mult))
            dve.wait_ge(sig["ranks_done"], 1)
            counts = bank(5)[0:1, 64:96].unsqueeze(1).to_broadcast([1, 3, EXPERTS])
            flag, upto = small[0:1, 16:112], lr_row
            do.step(v.tensor_tensor(flag.rearrange("p (b e) -> p b e", b=3), counts,
                                    const("pass_floor", 1).rearrange("p (b e) -> p b e", b=3), ALU.is_gt))
            do.step(v.scalar_tensor_tensor(out=gexp, in0=bank(5)[:, 0:64].rearrange("p (t e) -> p t e", t=NT),
                                           scalar=1.0, in1=chosen, op0=ALU.add, op1=ALU.mult))
            do.step(v.tensor_scalar(rank[:, :, 0:EXPERTS], gexp, 1.0, None, ALU.subtract))
            iota = const("iota")

            def pick_gather(e, at, done):
                for t in range(NT):
                    ins_ = v.tensor_scalar(sel_g[:, t, :], iota[:, at], rank[:, t, bass.ds(e, 1)], None, ALU.is_equal)
                    if t:
                        ins_.then_inc(done, 1)

            def pick_scatter(e, at, done):
                for t in range(NT):
                    ins_ = v.tensor_scalar(sel_s[:, t, :], iota[:, at], rank[:, t, bass.ds(e, 1)],
                                           gates[:, t, bass.ds(e, 1)], ALU.is_equal, ALU.mult)
                    if t and done is not None:
                        ins_.then_inc(done, 1)

            def pick_bias(dst, e, done):
                v.tensor_scalar(dst, ones[0:96, 0:CAP], const("pick", 96)[:, bass.ds(e, 1)], None,
                                ALU.mult).then_inc(done, 1)

            def keep_x(done):
                a = VEC_ROWS["g_ffn_norm"][0]
                v.tensor_tensor(xg, bank(2).rearrange("p (k s) -> p k s", k=KD),
                                vcol[:, a:a + KD].unsqueeze(2).to_broadcast([P, KD, CAP]), ALU.mult).then_inc(done, 1)

            def gate_up(clipped, n, up_done, up_n):
                v.tensor_scalar(g_min, bank(0), LIMIT, None, ALU.min).then_inc(clipped, 1)
                v.tensor_scalar(u_clip, bank(1), -LIMIT, LIMIT, ALU.max, ALU.min).then_inc(up_done, 1)
                dve.wait_ge(clipped, n)
                dve.wait_ge(up_done, up_n)
                v.scalar_tensor_tensor(out=u_clip, in0=u_clip, scalar=1.0, in1=g_min, op0=ALU.add,
                                       op1=ALU.mult).then_inc(up_done, 1)

            pick_gather(0, slice(0, CAP), sig["picked"])
            pick_bias(sel_b, 0, sig["selb_ready"])
            dve.wait_ge(sig["gathered"], 1)
            keep_x(sig["xg_ready"])
            keep_mod(2, 3)
            norm_gain(0, 8, "norm1_g_2")
            norm_gain(1, 32, "norm2_g_2")
            do.step(v.tensor_tensor_scan(out=upto, data0=ones[0:1, 0:96], data1=flag, initial=0.0,
                                         op0=ALU.mult, op1=ALU.add))
            do.step(v.tensor_tensor(list_eq, upto.unsqueeze(1).to_broadcast([1, 16, 96]),
                                    const("pass_rank", 1).unsqueeze(2).to_broadcast([1, 16, 96]), ALU.is_equal))
            do.step(v.tensor_tensor(list_eq, list_eq, flag.unsqueeze(1).to_broadcast([1, 16, 96]), ALU.mult))
            for i, name in enumerate(("pass_expert", "pass_block")):
                do.step(v.tensor_tensor(list_w, list_eq, const(name, 1).unsqueeze(1).to_broadcast([1, 16, 96]),
                                        ALU.mult))
                do.step(v.tensor_reduce(list_f[:, 16 * i:16 * i + 16], list_w, AX.X, ALU.add))
            do.step(v.tensor_copy(list_f[:, 32:33], upto[:, 95:96]))
            do.tell(v.tensor_copy(lists[:, 0:33], list_f[:, 0:33]), "lists_ready")
            with dve.Fori(0, EXPERTS) as e:
                pick_scatter(e, slice(0, P), sig["sel_ready"])
                pick_gather(e + 1, slice(0, CAP), sig["picked"])
                dve.wait_ge(chunk_used, e * SLOTS + (N_MOE + KD))
                gate_up(sig["clipped"], e + 1, sig["up_steps"], e * 2 + 1)
                pick_bias(sel_b, e + 1, sig["selb_ready"])
                pick_bias(sel_d, e, sig["seld_ready"])
                dve.wait_ge(sig["up_steps"], e * 2 + 2)
                dve.wait_ge(sig["sig_ready"], e + 1)
                v.tensor_tensor(act_buf, u_clip, sg, ALU.mult).then_inc(sig["act_ready"], 1)
                dve.wait_ge(sig["gathered"], e + 2)
                keep_x(sig["xg_ready"])
                dve.wait_ge(sig["xg_ready"], e + 2)
            n_over = dve.value_load(lists[0:1, 32:33], min_val=0, max_val=16)
            with dve.If(n_over > 0):
                with dve.Fori(0, OVER) as j:
                    with dve.If(j < n_over):
                        e = dve.value_load(lists[0:1, bass.ds(j, 1)], min_val=0, max_val=EXPERTS - 1)
                        b = dve.value_load(lists[0:1, bass.ds(j + 16, 1)], min_val=0, max_val=PASSES - 1)
                        dve.wait_ge(sig["o_scattered"], j + 1)
                        pick_scatter(e, bass.ds(b * P, P), sig["o_steps"])
                        pick_gather(e, bass.ds(b * P, CAP), sig["o_steps"])
                        pick_bias(sel_d, e, sig["o_steps"])
                        pick_bias(sel_b, e, sig["o_picked"])
                        dve.wait_ge(sig["o_gathered"], j + 1)
                        keep_x(sig["o_xg"])
                        dve.wait_ge(sig["o_gu"], j + 1)
                        gate_up(sig["o_clipped"], j + 1, sig["o_up_steps"], j * 2 + 1)
                        dve.wait_ge(sig["o_up_steps"], j * 2 + 2)
                        dve.wait_ge(sig["o_sig"], j + 1)
                        v.tensor_tensor(act_buf, u_clip, sg, ALU.mult).then_inc(sig["o_act"], 1)

            for t in range(NT):
                dve.wait_ge(sig["moe_done"], t + 1)
                for h in range(2):
                    xs = x_sb[:, t, h * 512:(h + 1) * 512]
                    ins_ = v.tensor_tensor(xs, bank(4 + 2 * t + h), xs, ALU.add)
                    if h:
                        do.tell(ins_, "x_summed")
                    else:
                        do.step(ins_)
            dve.wait_ge(sig["gfin_in"], 16)
            for t in range(NT):
                do.tell(v.tensor_tensor(z_rows[t], x_sb[:, t, :], gfin[:, :], ALU.mult), "z_ready")
            dve.wait_ge(sig["x_squared"], 2)
            r_ = rstd(S_FINAL, D)
            dve.wait_ge(sig["x_squared"], 4)
            st = stat(ms, S_NORM1)
            do.tell(v.tensor_tensor(st, st, r_, ALU.mult), "r_ready")
            do.step(v.tensor_tensor(st, st, r_, ALU.mult))
            r2 = rstd(S_NORM1, D)
            do.step(v.tensor_tensor(r2, r2, r_, ALU.mult))

            for t in range(NT):
                do.tell(v.tensor_scalar(rows[:, t, :], z_rows[t], r2[:, t:t + 1], None, ALU.mult), "rows_ready")
            dve.wait_ge(sig["x_scaled"], 2)
            keep_cols(lambda k: modg[:, k:k + 1], lambda k: modc[:, k:k + 1])
            do.step(v.memset(conv_x[:, :, 0:3], 0.0))
            st = stat(ms, S_HEADS)
            for i, c in enumerate((C_FQ, C_BQ)):
                for t in range(NT):
                    n = NT * i + t
                    dve.wait_ge(sig["qk_sq"], n + 1)
                    do.tell(v.tensor_reduce(st[:, 12 * n:12 * n + 12],
                                            sq_buf[n % 2].rearrange("p (h d) -> p h d", h=12), AX.X, ALU.add), "sq_used")
                r_ = rstd(S_HEADS, HD, 24 * i, 24)
                for t in range(NT):
                    view = proj[:, t, c:c + 768].rearrange("p (h d) -> p h d", h=12)
                    do.tell(v.tensor_tensor(view, view, r_[:, 12 * t:12 * t + 12].unsqueeze(2).to_broadcast([P, 12, HD]),
                                            ALU.mult), "heads_ready")
            dve.wait_ge(sig["proj_kept"], len(IN1_CHUNKS) + R_GATES)
            dve.wait_ge(sig["bias14_in"], 48)

            def bias_of(a, n):
                return bias14[:, a:a + n].unsqueeze(1).to_broadcast([P, NT, n])

            do.step(v.tensor_tensor(fg[:, :, 0:6], proj[:, :, C_FF:C_FF + FOX], bias_of(0, 6), ALU.add))
            do.step(v.tensor_tensor(fg[:, :, 6:10], proj[:, :, C_MF:C_MF + ML], bias_of(6, 4), ALU.add))
            do.step(v.tensor_tensor(bias_c[:, :, 12:16], proj[:, :, C_MI:C_MI + ML], bias_of(10, 4), ALU.add))
            do.tell(v.scalar_tensor_tensor(out=logf, in0=fg, scalar=-1.0, in1=fg, op0=ALU.mult, op1=ALU.min), "ff_ready")
            dve.wait_ge(sig["ff_ln"], 1)
            do.step(v.tensor_scalar(fg, fg, 0.0, None, ALU.min))
            do.tell(v.tensor_tensor(logf, fg, logf, ALU.subtract), "decay_ready")
            dve.wait_ge(sig["cum_done"], 1)
            for t in range(NT):
                do.step(v.tensor_copy(cum[:, t, :], bank(6)[:, 16 * t:16 * t + 10]))
            do.step(v.tensor_scalar(bias_c[:, :, 0:FOX], cum[:, :, 0:FOX], -float(HD) ** 0.5, None, ALU.mult))
            do.step(v.tensor_copy(bias_c[:, :, FOX:SOFT], const("slope").rearrange("p (t h) -> p t h", t=NT)))
            do.step(v.tensor_tensor(bias_c[:, :, 12:16], bias_c[:, :, 12:16], cum[:, :, 6:10], ALU.subtract))
            for i in range(3):
                part = bias_p[:, :, 16 * i:16 * i + 16]
                do.step(v.tensor_copy(bias_bf, bias_c))
                if i < 2:
                    do.step(v.tensor_copy(part, bias_bf))
                    do.step(v.tensor_tensor(bias_c, bias_c, part, ALU.subtract))
                else:
                    do.tell(v.tensor_copy(part, bias_bf), "cum_kept")
            dve.wait_ge(sig["cumt_turned"], 1)
            do.step(v.memset(bias_r, 0.0))
            do.tell(v.tensor_copy(bias_r[0:48, :], bank(7)[0:48, 0:T]), "bias_rows")
            for i, head in enumerate(list(attention_heads(2))[:2]):
                row_max(i, head)
            dve.wait_ge(sig["conv_in"], 2)
            for c in range(4):
                dst = qk[:, 12 + c, :]
                for j in range(CONV):
                    w_ = col("ml_conv_w_2", 4 * j + c)
                    src = conv_x[:, c, j:j + T]
                    if j == 0:
                        do.step(v.tensor_scalar(dst, src, w_, col("ml_conv_b_2", c), ALU.mult, ALU.add))
                        continue
                    ins_ = v.scalar_tensor_tensor(out=dst, in0=src, scalar=w_, in1=dst, op0=ALU.mult, op1=ALU.add)
                    if j == CONV - 1:
                        do.tell(ins_, "conv_sum")
                    else:
                        do.step(ins_)

            y_ml = rows[:, :, 384:640].rearrange("p t (h d) -> p t h d", h=ML)
            ml_sq = ml_e[:, 0:256].rearrange("p (h d) -> p h d", h=ML)
            ml_st, ml_r = (stat(x_, S_ML).rearrange("p (t h) -> p t h", t=NT) for x_ in (ms, rs))

            def conv_silus(*channels):
                for c in channels:
                    dve.wait_ge(sig["conv_tanh"], c + 1)
                    y_ = qk[:, 12 + c, :]
                    do.tell(v.scalar_tensor_tensor(out=y_, in0=conv_x[:, c, 0:T], scalar=1.0, in1=y_, op0=ALU.add,
                                                   op1=ALU.mult), "conv_silu")

            def ml_squares():
                for t in range(NT):
                    do.step(v.tensor_tensor(ml_sq, y_ml[:, t], y_ml[:, t], ALU.mult))
                    do.step(v.tensor_reduce(ml_st[:, t, :], ml_sq, AX.X, ALU.add))

            def ml_gate():
                dve.wait_ge(sig["ml_tanh"], 1)
                do.step(v.tensor_scalar(ml_r, ml_r, 0.5, None, ALU.mult))
                for t in range(NT):
                    do.step(v.tensor_tensor(y_ml[:, t], y_ml[:, t],
                                            ml_r[:, t, :].unsqueeze(2).to_broadcast([P, ML, HD]), ALU.mult))
                do.tell(v.scalar_tensor_tensor(out=rows[:, :, 384:640], in0=proj[:, :, C_MO:C_MO + 256], scalar=1.0,
                                               in1=rows[:, :, 384:640], op0=ALU.add, op1=ALU.mult), "rows_ready")

            attention(2, {3: [lambda: conv_silus(0, 1)], 4: [lambda: conv_silus(2, 3)], ML_HI + 2: [ml_squares], ML_HI + 3: [lambda: rstd(S_ML, HD)], ML_HI + 4: [ml_gate]},
                      started=2)
            keep_cols(lambda k: col("ml_h_g_2", 0) if k == 3 else 1.0)

            def add_gated(base, t, tell, product, last_chunk):
                for h in range(2):
                    part_done(product, t, h, last_chunk)
                    g_, xs = gate_b[:, h * 512:(h + 1) * 512], x_sb[:, t, h * 512:(h + 1) * 512]
                    tmp = rows[:, t, h * 512:(h + 1) * 512]
                    do.step(v.tensor_tensor(tmp, bank(base + 2 * t + h), g_, ALU.mult))
                    do.tell(v.tensor_tensor(xs, xs, tmp, ALU.add), tell)

            dve.wait_ge(sig["bcast_kept"], 1)
            for t in range(NT):
                add_gated(0, t, "gate_used", 1, N_OUT2 + 4)
                norm_rows(S_NORM2, t)
            keep_cols(lambda k: modg[:, 8 + k:9 + k], lambda k: modc[:, 24 + k:25 + k])
            dve.wait_ge(sig["rows_turned"], 20)
            for j in range(PAIRS):
                dve.wait_ge(sig["silu_ready"], j + 1)
                dve.wait_ge(chunk_used, N_GU2 + 2 * j + 2)
                if j >= 2:
                    dve.wait_ge(sig["h_turned"], j - 1)
                do.tell(v.tensor_tensor(h_rows[:, j % 2, :], h_sil[:, j % 2, :], bank(5 + 2 * (j % 2)), ALU.mult),
                        "h_ready")
            dve.wait_ge(sig["bcast_kept"], 2)
            dve.wait_ge(sig["h_turned"], PAIRS)
            for t in range(NT):
                add_gated(4, t, "out_ready", 2, N_END)

        @block.gpsimd
        def _(pool):
            steps = 0
            for parts, full, loaded in ((bias_b, bgu_f, "bgu_in"), (bdown_b, bdown_f, "bdown_in")):
                pool.wait_ge(sig[loaded], 48)
                for hi in (96, 64, 32):
                    done = sig["pool_steps"] if hi > 32 else sig["bias_split"]
                    nc.gpsimd.tensor_copy(parts[0:hi, :], full[0:hi, :]).then_inc(done, 1)
                    if hi > 32:
                        steps += 1
                        pool.wait_ge(sig["pool_steps"], steps)
                        nc.gpsimd.tensor_tensor(full[0:hi - 32, :], full[0:hi - 32, :], parts[0:hi - 32, :],
                                                ALU.subtract).then_inc(sig["pool_steps"], 1)
                        steps += 1
                        pool.wait_ge(sig["pool_steps"], steps)


_INS = ["x", "positions", "g_attn_norm", "w_in", "w_pool", "b_pool", "pool_scale", "g_q_a", "w_q_b", "g_kv_a", "w_kv_b",
        "g_out_pool", "g_out_attn", "w_out", "g_ffn_norm", "w_router", "b_router", "w_gate_up", "b_gate_up", "w_down",
        "b_down", "g_final", "c_2", "w_ada_2", "b_ada_2", "norm1_g_2", "norm2_g_2", "w_in_2", "fox_f_bias_2",
        "fox_q_g_2", "fox_k_g_2", "ml_conv_w_2", "ml_conv_b_2", "ml_i_bias_2", "ml_f_bias_2", "ml_h_g_2",
        "moba_q_g_2", "moba_k_g_2", "w_out_2", "w_gate_up_2", "w_down_2"]


def shape_constants():
    import numpy as np

    c = np.zeros((P, NCONST), np.float32)

    def put(name, a):
        at, n = CONST[name]
        c[:np.shape(a)[0], at:at + n] = a

    i = np.arange(P)
    put("ident", np.eye(P))
    put("ones", np.ones((P, P)))
    put("tri_inc", i[:, None] <= i[None, :])
    put("tri_exc", i[:, None] < i[None, :])
    put("mask", np.where(i[None, :] <= i[:, None], 0.0, NEG))
    put("iota", np.tile((np.arange(PASSES)[:, None] * CAP + i[None, :] % CAP).reshape(1, -1), (P, 1)))
    slopes = np.float32(2.0) ** (np.float32(-8.0) * np.arange(1, MOBA + 1, dtype=np.float32) / np.float32(MOBA))
    tok = np.arange(NT)[None, :, None] * P + i[:, None, None]
    put("bias_row", (i[0:48, None] % 16 == np.arange(16)[None, :]))
    put("slope", (tok * slopes[None, None, :] * np.float32(HD ** 0.5)).reshape(P, -1))
    put("inv", np.tile((np.float32(10000.0) ** (-np.arange(HALF, dtype=np.float32) / np.float32(HALF)))[None], (P, 1)))
    j = np.arange(96)
    put("pass_expert", (j % EXPERTS)[None])
    put("pass_block", (j // EXPERTS + 1)[None])
    put("pass_floor", ((j // EXPERTS + 1) * CAP)[None])
    put("pass_rank", np.arange(1, 17)[None])
    put("pick", (i[:, None] % EXPERTS == np.arange(EXPERTS + 1)[None, :]) & (np.arange(EXPERTS + 1)[None, :] < EXPERTS))
    t = np.arange(T)
    band = np.zeros((T, GROUPS, T), np.float32)
    for g, w in enumerate(WINDOWS):
        inside = (t[:, None] <= t[None, :]) & (t[:, None] > t[None, :] - w)
        band[:, g, :] = inside / np.minimum(t + 1, w)[None, :].astype(np.float32) - np.eye(T)
    band = band.reshape(NT, P, GROUPS, T).transpose(1, 2, 0, 3)
    return c, np.ascontiguousarray(band)


def kernel(**inputs):
    import numpy as _np
    import concourse.bacc as _bacc
    from concourse import mybir as _mybir
    from concourse.bass_utils import run_bass_kernel_spmd as _run

    nc = _bacc.Bacc("TRN2", target_bir_lowering=False, num_devices=1)
    arrays, aps = {}, {}
    consts, band = shape_constants()
    for name in _INS + ["consts", "band"]:
        a = consts if name == "consts" else band if name == "band" else _np.ascontiguousarray(inputs[name])
        arrays[f"in_{name}_dram"] = a
        aps[name] = nc.dram_tensor(f"in_{name}_dram", a.shape, _mybir.dt.from_np(a.dtype), kind="ExternalInput").ap()
    out = nc.dram_tensor("out_0_dram", (1, T, D), _mybir.dt.float32, kind="ExternalOutput").ap()
    two_blocks(nc, aps, aps.pop("consts"), aps.pop("band"), out)
    r = _run(nc, [arrays], core_ids=[0])
    return r.results[0]["out_0_dram"]
```
